# Optimizing a Trainium2 kernel written in Bass

```python
import jax, jax.numpy as jnp
from jax import lax
import numpy as np

D_MODEL = 1024
BATCH = 1
SEQ = 512
DEPTH = 2
DEC_BATCH = 8
DEC_SEQ = 8
PAST_LEN = 4096
PAGE_SIZE = 128

N_AB = (DEPTH + 1) // 2
N_C = DEPTH // 2
D_A = D_MODEL // 2
POOL_WINDOWS = (2, 4, 8, 16)
N_POOL_GROUPS = len(POOL_WINDOWS)
POOL_GROUP = D_A // N_POOL_GROUPS
POOL_BUF = max(POOL_WINDOWS) - 1
D_B = D_MODEL // 2
CONV_K = 31
CONV_BUF = CONV_K - 1
D_C = D_MODEL
H_C = 8
CHUNK = 128
D_FF = 2816
FFN_K = 3
FFN_BUF = FFN_K - 1
EPS = 1e-6

kernel_name = "pool_conv_sgu_hybrid_step"

def rmsnorm(x, g):
    xf = x.astype(jnp.float32)
    y = xf * lax.rsqrt(jnp.mean(xf * xf, axis=-1, keepdims=True) + EPS)
    return (y * g.astype(jnp.float32)).astype(x.dtype)

def layernorm(x, g, b):
    xf = x.astype(jnp.float32)
    mu = jnp.mean(xf, axis=-1, keepdims=True)
    var = jnp.mean(jnp.square(xf - mu), axis=-1, keepdims=True)
    y = (xf - mu) * lax.rsqrt(var + EPS) * g.astype(jnp.float32) + b.astype(jnp.float32)
    return y.astype(x.dtype)

def causal_dwconv(h, buf, w, b):
    k = w.shape[0]
    full = jnp.concatenate([buf.astype(h.dtype), h], axis=1)
    out = lax.conv_general_dilated(
        full, w.astype(h.dtype)[:, None, :], window_strides=(1,), padding="VALID",
        dimension_numbers=("NWC", "WIO", "NWC"), feature_group_count=h.shape[-1])
    return out + b.astype(h.dtype), full[:, full.shape[1] - (k - 1):]

def multi_scale_pool(xa, buf, start_pos, pool_w, pool_scale):
    bsz, t = xa.shape[0], xa.shape[1]
    full = jnp.concatenate([buf.astype(xa.dtype), xa], axis=1)
    cs = jnp.cumsum(full.astype(jnp.float32), axis=1)
    cs = jnp.pad(cs, ((0, 0), (1, 0), (0, 0)))
    pos = start_pos + jnp.arange(t, dtype=jnp.int32)
    means = []
    for g, w in enumerate(POOL_WINDOWS):
        sl = slice(g * POOL_GROUP, (g + 1) * POOL_GROUP)
        win = cs[:, POOL_BUF + 1:POOL_BUF + 1 + t, sl] - cs[:, POOL_BUF + 1 - w:POOL_BUF + 1 - w + t, sl]
        cnt = jnp.minimum(pos + 1, w).astype(jnp.float32)
        means.append(win / cnt[None, :, None])
    d = (jnp.concatenate(means, axis=-1) - xa.astype(jnp.float32)).astype(xa.dtype)
    d = d.reshape(bsz, t, N_POOL_GROUPS, POOL_GROUP)
    y = jnp.einsum("btgi,gio->btgo", d, pool_w).reshape(bsz, t, D_A) * pool_scale
    return y, full[:, full.shape[1] - POOL_BUF:]

def spatial_gating(v, w_s, b_s):
    bsz, t = v.shape[0], v.shape[1]
    ln = min(t, CHUNK)
    n = -(-t // ln)
    vp = jnp.pad(v, ((0, 0), (0, n * ln - t), (0, 0)))
    vc = vp.reshape(bsz, n, ln, H_C, D_C // H_C)
    w = jnp.tril(w_s[:, :ln, :ln])
    z = jnp.einsum("hij,bnjhd->bnihd", w, vc) + jnp.transpose(b_s[:, :ln])[None, None, :, :, None]
    return z.reshape(bsz, n * ln, D_C)[:, :t]

def trunk(x, start_pos, pool_bufs, conv_bufs, ffn_bufs, p):
    t = x.shape[1]
    new_pool, new_conv, new_v, new_ffn = [], [], [], []
    for layer in range(DEPTH):
        h = rmsnorm(x, p["mix_norm"][layer])
        if layer % 2 == 0:
            i = layer // 2
            proj = h @ p["w_in_ab"][i]
            xa = proj[..., :D_A]
            a = proj[..., D_A:D_A + D_B]
            gt = proj[..., D_A + D_B:]
            ya, pb = multi_scale_pool(xa, pool_bufs[i], start_pos, p["pool_w"][i], p["pool_scale"][i])
            glu = a * jax.nn.sigmoid(gt)
            c, cb = causal_dwconv(glu, conv_bufs[i], p["conv_w"][i], p["conv_b"][i])
            yb = jax.nn.silu(layernorm(c, p["conv_norm_g"][i], p["conv_norm_b"][i]))
            x = x + jnp.concatenate([ya, yb], axis=-1) @ p["w_out_ab"][i]
            new_pool.append(pb)
            new_conv.append(cb)
        else:
            j = layer // 2
            proj = h @ p["w_in_c"][j]
            u = proj[..., :D_C]
            v = layernorm(proj[..., D_C:], p["sgu_norm_g"][j], p["sgu_norm_b"][j])
            z = spatial_gating(v, p["sgu_w"][j], p["sgu_bias"][j])
            x = x + (u * z) @ p["w_out_c"][j]
            last_start = ((t - 1) // CHUNK) * CHUNK
            new_v.append(v[:, last_start:])
        h = rmsnorm(x, p["ffn_norm"][layer])
        up = h @ p["w_up"][layer]
        c, fb = causal_dwconv(up, ffn_bufs[layer], p["ffn_conv_w"][layer], p["ffn_conv_b"][layer])
        x = x + (jax.nn.silu(c[..., :D_FF]) * c[..., D_FF:]) @ p["w_down"][layer]
        new_ffn.append(fb)
    y = rmsnorm(x, p["final_norm"])
    return y, jnp.stack(new_pool), jnp.stack(new_conv), jnp.stack(new_v), jnp.stack(new_ffn)

def setup_inputs(seed: int = 0) -> dict:
    key = jax.random.key(seed)
    ks = jax.random.split(key, 32)
    f32 = jnp.float32

    def nrm(k, shape, scale):
        return jax.random.normal(k, shape, f32) * scale

    return {
        "x_prompt": nrm(ks[0], (BATCH, SEQ, D_MODEL), 1.0),
        "x_sample": nrm(ks[1], (DEC_BATCH, DEC_SEQ, D_MODEL), 1.0),
        "state_pool": nrm(ks[2], (N_AB, DEC_BATCH, POOL_BUF, D_A), 1.0),
        "state_conv": nrm(ks[3], (N_AB, DEC_BATCH, CONV_BUF, D_B), 0.5),
        "state_ffn": nrm(ks[4], (DEPTH, DEC_BATCH, FFN_BUF, 2 * D_FF), 1.0),
        "mix_norm": 1.0 + nrm(ks[5], (DEPTH, D_MODEL), 0.02),
        "w_in_ab": nrm(ks[6], (N_AB, D_MODEL, D_A + 2 * D_B), D_MODEL ** -0.5),
        "pool_w": nrm(ks[7], (N_AB, N_POOL_GROUPS, POOL_GROUP, POOL_GROUP), POOL_GROUP ** -0.5),
        "pool_scale": 0.5 + nrm(ks[8], (N_AB, D_A), 0.05),
        "conv_w": nrm(ks[9], (N_AB, CONV_K, D_B), CONV_K ** -0.5),
        "conv_b": nrm(ks[10], (N_AB, D_B), 0.02),
        "conv_norm_g": 1.0 + nrm(ks[11], (N_AB, D_B), 0.02),
        "conv_norm_b": nrm(ks[12], (N_AB, D_B), 0.02),
        "w_out_ab": nrm(ks[13], (N_AB, D_A + D_B, D_MODEL), (D_A + D_B) ** -0.5),
        "w_in_c": nrm(ks[14], (N_C, D_MODEL, 2 * D_C), D_MODEL ** -0.5),
        "sgu_norm_g": 1.0 + nrm(ks[15], (N_C, D_C), 0.02),
        "sgu_norm_b": nrm(ks[16], (N_C, D_C), 0.02),
        "sgu_w": nrm(ks[17], (N_C, H_C, CHUNK, CHUNK), 0.5 * CHUNK ** -0.5),
        "sgu_bias": 1.0 + nrm(ks[18], (N_C, H_C, CHUNK), 0.1),
        "w_out_c": nrm(ks[19], (N_C, D_C, D_MODEL), D_C ** -0.5),
        "ffn_norm": 1.0 + nrm(ks[20], (DEPTH, D_MODEL), 0.02),
        "w_up": nrm(ks[21], (DEPTH, D_MODEL, 2 * D_FF), D_MODEL ** -0.5),
        "ffn_conv_w": nrm(ks[22], (DEPTH, FFN_K, 2 * D_FF), FFN_K ** -0.5),
        "ffn_conv_b": nrm(ks[23], (DEPTH, 2 * D_FF), 0.02),
        "w_down": nrm(ks[24], (DEPTH, D_FF, D_MODEL), D_FF ** -0.5),
        "final_norm": 1.0 + nrm(ks[25], (D_MODEL,), 0.02),
    }

def reference(x_prompt, x_sample, state_pool, state_conv, state_ffn, mix_norm, w_in_ab, pool_w,
              pool_scale, conv_w, conv_b, conv_norm_g, conv_norm_b, w_out_ab, w_in_c, sgu_norm_g,
              sgu_norm_b, sgu_w, sgu_bias, w_out_c, ffn_norm, w_up, ffn_conv_w, ffn_conv_b, w_down,
              final_norm):
    p = dict(mix_norm=mix_norm, w_in_ab=w_in_ab, pool_w=pool_w, pool_scale=pool_scale,
             conv_w=conv_w, conv_b=conv_b, conv_norm_g=conv_norm_g, conv_norm_b=conv_norm_b,
             w_out_ab=w_out_ab, w_in_c=w_in_c, sgu_norm_g=sgu_norm_g, sgu_norm_b=sgu_norm_b,
             sgu_w=sgu_w, sgu_bias=sgu_bias, w_out_c=w_out_c, ffn_norm=ffn_norm, w_up=w_up,
             ffn_conv_w=ffn_conv_w, ffn_conv_b=ffn_conv_b, w_down=w_down, final_norm=final_norm)
    bp = x_prompt.shape[0]
    dt = x_prompt.dtype
    zero_pool = jnp.zeros((N_AB, bp, POOL_BUF, D_A), dt)
    zero_conv = jnp.zeros((N_AB, bp, CONV_BUF, D_B), dt)
    zero_ffn = jnp.zeros((DEPTH, bp, FFN_BUF, 2 * D_FF), dt)
    y_prompt, pool_prompt, conv_prompt, sgu_v_prompt, ffn_prompt = trunk(
        x_prompt, 0, zero_pool, zero_conv, zero_ffn, p)
    y_sample, pool_sample, conv_sample, sgu_v_sample, ffn_sample = trunk(
        x_sample, PAST_LEN, state_pool, state_conv, state_ffn, p)
    return (y_prompt, y_sample, pool_prompt, pool_sample, conv_prompt, conv_sample,
            sgu_v_prompt, sgu_v_sample, ffn_prompt, ffn_sample)


_drawn_inputs = setup_inputs


def setup_inputs(seed=0):
    import zlib

    import numpy as np

    out = dict(_drawn_inputs(seed))
    spreads = {}
    factors = {'conv_b': 3.019,
     'conv_norm_g': 5.11,
     'conv_norm_b': 6.106,
     'sgu_norm_g': 23.207,
     'sgu_norm_b': 23.243,
     'ffn_conv_b': 3.2,
     'final_norm': 22.058,
     'pool_scale': 4.872,
     'ffn_norm': 2.768,
     'sgu_bias': 3.212}
    for name, (base, spread) in spreads.items():
        noise = np.random.default_rng([zlib.crc32(name.encode()), seed]).standard_normal(out[name].shape)
        drawn = base * np.exp(spread * noise) if base else spread * noise
        out[name] = __import__('jax').numpy.asarray(drawn.astype(out[name].dtype))
    for name, factor in factors.items():
        out[name] = (out[name] * factor).astype(out[name].dtype)
    return out
```

```python
from contextlib import ExitStack

import concourse.bass as bass
from concourse import mybir

F32 = mybir.dt.float32
F32R = mybir.dt.float32r
ALU = mybir.AluOpType
ACT = mybir.ActivationFunctionType
P = 128

PSUM_BANK = 512
WINDOWS = (2, 4, 8, 16)


def hybrid_trunk(nc, x_prompt, x_sample, state_pool, state_conv, state_ffn, mix_norm, w_in_ab, pool_w,
                 pool_scale, conv_w, conv_b, conv_norm_g, conv_norm_b, w_out_ab, w_in_c, sgu_norm_g,
                 sgu_norm_b, sgu_w, sgu_bias, w_out_c, ffn_norm, w_up, ffn_conv_w, ffn_conv_b, w_down,
                 final_norm, y_prompt, y_sample, pool_prompt, pool_sample, conv_prompt, conv_sample,
                 sgu_v_prompt, sgu_v_sample, ffn_prompt, ffn_sample):
    _, PR, D = x_prompt.shape
    NS, DS, _ = x_sample.shape
    SM = NS * DS
    T = PR + SM
    HALF = T // 2
    KD = D // P
    DH = D // 2
    KH = DH // P
    DF = w_down.shape[1]
    KF = DF // P
    GT = KF // 2
    PB = state_pool.shape[2]
    CB = state_conv.shape[2]
    TAPS = CB + 1
    FB = state_ffn.shape[2]
    FK = FB + 1
    CH = PR // P
    EPS = 1e-6
    RT = CH + 1

    U_IN0 = 0
    N_IN0 = 3 * KH
    U_OUT0 = U_IN0 + N_IN0
    U_FFN0 = U_OUT0 + KD
    N_FFN = 2 * (2 * GT + KD)
    U_IN1 = U_FFN0 + N_FFN
    U_OUT1 = U_IN1 + 2 * KD
    U_FFN1 = U_OUT1 + KD
    U_FFN = (U_FFN0, U_FFN1)
    N_UNITS = U_FFN1 + N_FFN
    PAIR = [(KH + c, 2 * KH + c) for c in range(KH)]
    IN0 = [*PAIR[0], *PAIR[1], *range(KH), *PAIR[2], *PAIR[3]]
    assert KH == 4 and len(IN0) == N_IN0 and U_OUT0 % 2 == 0 and GT * 2 == KF

    H_MIX = (0, KH + KF)
    H_FFN = (KH, KH + KF + KD)
    X_FINAL = (None, U_OUT0, U_IN1 - KD, U_OUT1, N_UNITS - KD)

    rows0 = [("mix_norm", mix_norm, 2 * KD), ("ffn_norm", ffn_norm, 2 * KD), ("final_norm", final_norm, KD),
             ("pool_scale", pool_scale, KH), ("conv_b", conv_b, KH), ("conv_norm_g", conv_norm_g, KH),
             ("conv_norm_b", conv_norm_b, KH), ("sgu_norm_g", sgu_norm_g, KD), ("sgu_norm_b", sgu_norm_b, KD)]
    PC = {}
    at = 0
    for name, _, n in rows0:
        PC[name] = at
        at += n
    NP0 = at
    PC["conv_w"] = NP0
    PC["ffn_conv_w"] = PC["conv_w"] + TAPS * KH
    PC["ffn_conv_b"] = PC["ffn_conv_w"] + 2 * FK * 2 * KF
    NPAR = PC["ffn_conv_b"] + 2 * 2 * KF
    FBLK = 2 * 2 * KF

    GL = CB + PR + NS * (CB + DS)
    XL = PB + PR + NS * (PB + DS)
    UL = FB + PR + NS * (FB + DS)
    CL = UL - FB

    flat = lambda ap: ap.rearrange("l (t p) -> (l t) p", p=P) if len(ap.shape) == 2 else ap.rearrange("(t p) -> t p", p=P)
    wblocks = lambda w: w.rearrange("(k p) n -> p k n", p=P)
    xp_rows = x_prompt.rearrange("b (r p) d -> p (b r) d", p=P)
    xs_rows = x_sample.rearrange("s t d -> (s t) d")
    yp_rows = y_prompt.rearrange("b (r p) d -> p (b r) d", p=P)
    ys_rows = y_sample.rearrange("s t d -> (s t) d")

    with ExitStack() as ctx:
        def sb(name, shape, dt=F32):
            return ctx.enter_context(nc.sbuf_tensor(name, shape, dt))

        def sem(name):
            return ctx.enter_context(nc.semaphore(name))

        ctx.enter_context(nc.allow_non_contiguous_dma(reason="small state rows"))
        X = sb("residual", [P, KD, T])
        xh = sb("x_hi", [P, KD, T], F32R)
        xl = sb("x_lo", [P, KD, T], F32R)
        hh = sb("h_hi", [P, GT, T], F32R)
        hl = sb("h_lo", [P, GT, T], F32R)
        w_raw = [sb(f"w_raw{s}", [P, GT * P]) for s in range(2)]
        w_hi = [sb(f"w_hi{s}", [P, GT * P], F32R) for s in range(2)]
        w_lo = [sb(f"w_lo{s}", [P, GT * P], F32R) for s in range(2)]
        par = sb("params", [P, NPAR])
        state_T = sb("ffn_state_T", [P, 2, NS * FB, 2 * KF])
        ident = sb("ident", [P, P])
        ones = sb("ones", [P, P])
        rstd = sb("rstd", [P, T])
        sq = sb("squares", [P, 2, T])
        sqacc = sb("squares_sum", [P, T])
        poolw = sb("pool_w_sb", [P, KH, P])
        eps = sb("eps", [P, 1])
        std = sb("std", [P, RT])
        rinv = sb("rinv", [P, RT])
        corr = sb("count_corr", [P, sum(WINDOWS) - len(WINDOWS)])
        ARENA = 13152
        arena = sb("arena", [P, ARENA])
        diag = sq[:, :, :].rearrange("p a t -> p (a t)")[:, 0:RT * P].rearrange("p (r c) -> p r c", r=RT)

        def cut(start, *dims):
            n = 1
            for d in dims:
                n *= d
            assert start + n <= ARENA, (start, n)
            v = arena[:, start:start + n]
            if len(dims) == 2:
                v = v.rearrange("p (a b) -> p a b", a=dims[0])
            return v

        x_rows = cut(0, RT, D)
        conv_o = cut(0, KH, T)
        a_t = cut(KH * T, T)
        g_t = cut(KH * T + T, T)
        conv_rows = cut(7 * T, 2, DH)
        par_rows = cut(RT * D, 6, P)
        pool_rows = cut(RT * D + 6 * P, DH)
        pool_tmp = [cut(7 * T, XL), cut(RT * D, XL)]
        d_t = [cut(6 * T, T), cut(RT * D + XL, T), sq[:, 0, :], sq[:, 1, :]]
        XA0 = RT * D + XL + T + 1
        xa = cut(XA0, KH, XL)
        glu = cut(XA0 + KH * XL, KH, GL)
        new_x = cut(XA0 + KH * XL + KH * GL, KH, SM)
        new_glu = cut(XA0 + KH * XL + KH * GL + KH * SM, KH, SM)
        out_rows0 = [cut(KH * T, DH), cut(KH * T + DH, DH), cut(7 * T, DH), cut(RT * D, DH)]
        state_rows = cut(XA0 + KH * XL, 2 * NS * FB * 2 * KF // P, P)
        up = cut(0, 2, UL)
        cv = cut(2 * UL, 2, CL)
        F0 = 2 * UL + 2 * CL
        stash = cut(F0, (FB + NS * FB), 2 * KF)
        stash_rows = cut(F0 + (FB + NS * FB) * 2 * KF, 7, P)
        F1 = F0 + (FB + NS * FB) * 2 * KF + 7 * P
        xg = cut(F1, 2, T)
        y_rows = cut(F1 + 2 * T, RT, D)
        V = cut(0, KD, T)
        U = cut(KD * T, KD, T)
        gate_w_rows = cut(KD * T, KD, P)
        v_rows = [cut(2 * KD * T + i * RT * P, RT, P) for i in range(2)]
        G0 = 2 * KD * T + 2 * RT * P
        gate_w_T = cut(G0, KD, P)
        gate_b = cut(G0 + KD * P, KD, P)
        rstd_v = cut(G0 + 2 * KD * P, T)
        block_w = state_T[0:SM, 0, :, :].rearrange("p a b -> p (a b)")[:, 0:KD * SM].rearrange("p (h i) -> p h i", h=KD)

        PS = ctx.enter_context(nc.psum_tensor("psum", [P, 8, PSUM_BANK], F32))
        acc = lambda slot: PS[:, 2 * slot:2 * slot + 2, 0:HALF]
        S0, S1, M0, M1 = 4, 5, 6, 7
        POOL_BANK = (M0, S0, 0, 2)
        halves = lambda v: v.rearrange("p (a t) -> p a t", a=2)
        smp = lambda v, n=DS: v.rearrange("p (s t) -> p s t", t=n)

        ld_x, ld_p0, ld_par, ld_pw = sem("ld_x"), sem("ld_p0"), sem("ld_par"), sem("ld_pool_w")
        ld_cs, ld_fs, ld_gw, ld_gb = sem("ld_conv_state"), sem("ld_ffn_state"), sem("ld_gate_w"), sem("ld_gate_b")
        raw_ready = [sem("raw_ready0"), sem("raw_ready1")]
        hi_ready, lo_ready, unit_done, acc_free = sem("w_hi_ready"), sem("w_lo_ready"), sem("unit_done"), sem("acc_free")
        const_ready, ident_ready, corr_ready = sem("const_ready"), sem("ident_ready"), sem("corr_ready")
        p0_T, p0_ready, xs_T, xs_ready, xT = sem("p0_T"), sem("p0_ready"), sem("xs_T"), sem("xs_ready"), sem("x_T")
        setup_T, setup_ready = sem("setup_T"), sem("setup_ready")
        x_ready, xh_ready, xl_ready = sem("x_ready"), sem("xh_ready"), sem("xl_ready")
        sq_ready, sq_added = sem("sq_ready"), sem("sq_added")
        var_mm, std_ready, rinv_ready, diag_ready = sem("var_mm"), sem("std_ready"), sem("rinv_ready"), sem("diag_ready")
        bc_mm, rstd_ready = sem("bc_mm"), sem("rstd_ready")
        sig_ready, glu_ready = sem("sig_ready"), sem("glu_ready")
        conv_step, pads_zero = sem("conv_step"), sem("pads_zero")
        new_packed = sem("new_packed")
        win_step, d_ready = sem("win_step"), sem("d_ready")
        pool_mm, hh_ready, h_lo_ready = sem("pool_mm"), sem("hh_ready"), sem("h_lo_ready")
        ya_read, ya_hi, ya_ready = sem("ya_read"), sem("ya_hi"), sem("ya_ready")
        mean_mm, cent_ready = sem("mean_mm"), sem("cent_ready")
        csq_ready, csq_used = sem("csq_ready"), sem("csq_used")
        cn_ready, cs_ready = sem("cn_ready"), sem("cs_ready")
        so_T, so_rows, st_out = sem("state_out_T"), sem("state_out_rows"), sem("st_out")
        fs_T, fs_ready = sem("ffn_state_T_mm"), sem("ffn_state_ready")
        tap0_ready, tap1_ready, tap_ready = sem("tap0_ready"), sem("tap1_ready"), sem("tap_ready")
        silu_ready, h_ready, pad_ready, stash_ready = sem("silu_ready"), sem("h_ready"), sem("pad_ready"), sem("stash_ready")
        stash_T, stash_rows_ready, st_ffn = sem("stash_T"), sem("stash_rows_ready"), sem("st_ffn")
        gw_T, gw_copied, gw_ready = sem("gate_w_T_mm"), sem("gate_w_copied"), sem("gate_w_ready")
        bw_zero, bw_ready = sem("block_w_zero"), sem("block_w_ready")
        vsum = sem("vsum")
        vsq_ready, vsq_added = sem("vsq_ready"), sem("vsq_added")
        vn_ready, va_ready, v_T = sem("vn_ready"), sem("va_ready"), sem("v_T")
        vrow_ready, st_v, z_mm, zb_ready = sem("vrow_ready"), [sem("st_v0"), sem("st_v1")], sem("z_mm"), sem("zb_ready")
        uz_ready = sem("uz_ready")
        y_row_done = sem("y_row_done")
        xg_ready, y_T, yrow_ready, y_scaled, st_y = sem("xg_ready"), sem("y_T"), sem("yrow_ready"), sem("y_scaled"), sem("st_y")
        st_state = sem("st_state")

        block = ctx.enter_context(nc.Block())

        def sums(r):
            return r if r < 2 else r - 1

        def pcol(name, i):
            if isinstance(i, int):
                return par[:, PC[name] + i:PC[name] + i + 1]
            return par[:, bass.ds(i + PC[name], 1)]

        @block.sync
        def _(sp):
            sp.dma_start(x_rows[0:SM, CH, :], xs_rows).then_inc(ld_x, 16)
            for r in range(CH):
                sp.dma_start(x_rows[:, r, :], xp_rows[:, r, :]).then_inc(ld_x, 16)

            def load(slot, u, src, nk):
                if not isinstance(u, int) or u >= 2:
                    sp.wait_ge(lo_ready, u - 1)
                sp.dma_start(w_raw[slot][:, 0:nk * P].rearrange("p (k n) -> p k n", k=nk), src)\
                    .then_inc(raw_ready[slot], 16)

            def col(w, t):
                v = wblocks(w)
                return v[:, :, t * P:(t + 1) * P] if isinstance(t, int) else v[:, :, bass.ds(t * P, P)]

            for u in range(N_IN0):
                load(u % 2, U_IN0 + u, col(w_in_ab[0], IN0[u]), KD)
                if u == 1:
                    sp.wait_ge(xT, KD)
                    for b in range(2):
                        sp.dma_start(conv_rows[0:4 * CB, b, :],
                                     state_conv[0, 4 * b:4 * b + 4].rearrange("s r d -> (s r) d")).then_inc(ld_cs, 16)
            for j in range(2):
                load(j, U_OUT0 + j, col(w_out_ab[0], j), KD)
            sp.wait_ge(conv_step, 2 * TAPS * KH)
            sp.wait_ge(so_T, 2)
            sp.dma_start(state_rows, state_ffn.rearrange("l s r (t p) -> (l s r t) p", p=P)
                         .rearrange("(b q) p -> q b p", q=P)).then_inc(ld_fs, 16)
            with sp.Fori(1, KD // 2) as i:
                for j in range(2):
                    load(j, i * 2 + (U_OUT0 + j), col(w_out_ab[0], i * 2 + j), KD)
            for layer in range(2):
                if layer == 1:
                    with sp.Fori(0, KD // 2) as i:
                        for j in range(2):
                            load(j, i * 2 + (U_IN1 + j), col(w_in_c[0], i * 2 + (KD + j)), KD)
                    with sp.Fori(0, KD // 2) as i:
                        for j in range(2):
                            load(j, i * 2 + (U_IN1 + KD + j), col(w_in_c[0], i * 2 + j), KD)
                    with sp.Fori(0, KD // 2) as i:
                        for j in range(2):
                            load(j, i * 2 + (U_OUT1 + j), col(w_out_c[0], i * 2 + j), KD)
                for g in range(2):
                    u0 = U_FFN[layer] + g * (2 * GT + KD)
                    with sp.Fori(0, GT) as i:
                        for j in range(2):
                            load(j, i * 2 + (u0 + j), col(w_up[layer], i + (g * GT + j * KF)), KD)
                    down = w_down[layer, g * GT * P:(g + 1) * GT * P, :]
                    with sp.Fori(0, KD // 2) as i:
                        for j in range(2):
                            load(j, i * 2 + (u0 + 2 * GT + j), col(down, i * 2 + j), GT)
            for n, r in enumerate((0, 2, CH)):
                sp.wait_ge(y_row_done, n + 1)
                if r < CH:
                    sp.dma_start(yp_rows[:, r, :], y_rows[:, r, :]).then_inc(st_y, 16)
                else:
                    sp.dma_start(ys_rows, y_rows[P - SM:P, CH, :]).then_inc(st_y, 16)
            sp.wait_ge(st_state, 16 * 2)
            sp.wait_ge(st_out, 16 * 4)
            sp.wait_ge(st_ffn, 16 * 6)
            sp.wait_ge(st_v[0], 16 * KD)
            sp.wait_ge(st_v[1], 16 * KD)
            sp.wait_ge(st_y, 16 * RT)

        @block.tensor
        def _(pe):
            def unit(slot, u, nk, rh, rl, ready=None, base=0, middle=None):
                pe.wait_ge(lo_ready, u + 1)
                if not isinstance(u, int) or u >= 2:
                    pe.wait_ge(acc_free, u - 1)
                for k in range(nk):
                    if ready is not None and base + k + 1 > 0:
                        pe.wait_ge(ready, base + k + 1)
                    for n, (w, r) in enumerate(((w_hi, rh), (w_hi, rl), (w_lo, rh))):
                        for half in range(2):
                            last = nc.tensor.matmul(PS[:, 2 * slot + half, 0:HALF], w[slot][:, k * P:(k + 1) * P],
                                                    r[:, k, half * HALF:(half + 1) * HALF],
                                                    start=(k == 0 and n == 0), stop=(k == nk - 1 and n == 2))
                    if middle is not None and k == nk // 2:
                        middle()
                last.then_inc(unit_done, 1)

            def row_sums(src, first=True, final=True):
                for r in range(RT):
                    lo = r * P if r < CH else T - P
                    last = nc.tensor.matmul(PS[:, S0, r:r + 1], src[:, lo:lo + P], ones[:, 0:1],
                                            start=(first and r == 0), stop=(final and r == RT - 1),
                                            skip_group_check=True)
                return last

            def spread(r):
                pe.wait_ge(diag_ready, r + 1)
                nc.tensor.matmul(PS[:, M0, 0:PR], ones[:, :], diag[:, 0:CH, :], start=True, stop=True)
                nc.tensor.matmul(PS[:, M1, 0:SM], ones[:, :], diag[:, CH, P - SM:P], start=True, stop=True)\
                    .then_inc(bc_mm, 1)

            def norm_sums(n, r):
                pe.wait_ge(sq_added, (KD - 1) * (n + 1))
                row_sums(sqacc).then_inc(var_mm, 1)

            pe.wait_ge(ident_ready, 1)
            pe.wait_ge(ld_p0, 16 * len(rows0))
            nc.tensor.transpose(PS[:, M1, 0:NP0], par_rows[0:NP0, 0, :], ident[0:NP0, 0:NP0]).then_inc(p0_T, 1)
            pe.wait_ge(ld_x, 16 * RT)
            for k in range(KD):
                last = nc.tensor.transpose(PS[:, 0, k * SM:(k + 1) * SM], x_rows[0:SM, CH, k * P:(k + 1) * P],
                                           ident[0:SM, 0:SM])
            last.then_inc(xs_T, 1)
            for k in range(KD):
                if k + 1 == M1:
                    pe.wait_ge(p0_ready, 1)
                if k + 1 == 8:
                    pe.wait_ge(xs_ready, 1)
                for r in range(CH):
                    last = nc.tensor.transpose(PS[:, (k + 1) % 8, r * P:(r + 1) * P], x_rows[:, r, k * P:(k + 1) * P],
                                               ident[:, :])
                last.then_inc(xT, 1)

            pe.wait_ge(x_ready, KD)
            unit(0, U_IN0, KD, xh, xl, xl_ready, 0)
            pe.wait_ge(ld_par, 16 * 6)
            at = 0
            for b, n in ((1, TAPS * KH), (2, FBLK), (3, FBLK), (4, FBLK), (5, FBLK)):
                last = nc.tensor.transpose(PS[:, S0, at:at + n], par_rows[0:n, b, :], ident[0:n, 0:n])
                at += n
            last.then_inc(setup_T, 1)
            for c in range(KH):
                last = nc.tensor.transpose(PS[:, S1, c * NS * PB:(c + 1) * NS * PB],
                                           pool_rows[0:NS * PB, c * P:(c + 1) * P], ident[0:NS * PB, 0:NS * PB])
            last.then_inc(setup_T, 1)
            pe.wait_ge(ld_cs, 32)
            for b in range(2):
                for c in range(KH):
                    last = nc.tensor.transpose(PS[:, M0 + b, c * 4 * CB:(c + 1) * 4 * CB],
                                               conv_rows[0:4 * CB, b, c * P:(c + 1) * P],
                                               ident[0:4 * CB, 0:4 * CB])
                last.then_inc(setup_T, 1)
            pe.wait_ge(setup_ready, 1)
            norm_sums(0, 0)

            def middle0():
                pe.wait_ge(setup_ready, 4)
                spread(0)
            unit(1, U_IN0 + 1, KD, xh, xl, middle=middle0)
            for u in range(2, N_IN0, 2):
                for j in range(2):
                    unit(j, U_IN0 + u + j, KD, xh, xl)
            pe.wait_ge(ld_pw, 16)
            pe.wait_ge(rstd_ready, 1)
            for g in range(KH):
                pe.wait_ge(d_ready, g + 1)
                if g >= 2:
                    pe.wait_ge(acc_free, U_OUT0 - KH + g + 1)
                for half in range(2):
                    last = nc.tensor.matmul(PS[:, POOL_BANK[g] + half, 0:HALF], poolw[:, g, :],
                                            d_t[g][:, half * HALF:(half + 1) * HALF], start=True, stop=True)
                last.then_inc(pool_mm, 1)

            pe.wait_ge(new_packed, KH)
            pe.wait_ge(ya_read, 1)
            for g in range(KH):
                nc.tensor.transpose(PS[0:PB, M0, g * P:(g + 1) * P], xa[:, g, PR:PR + PB], ident[:, :])
            for g in range(KH):
                last = nc.tensor.transpose(PS[0:SM, M1, g * P:(g + 1) * P], new_x[:, g, :], ident[:, :])
            last.then_inc(so_T, 1)
            pe.wait_ge(ya_read, 2)
            for c in range(KH):
                pe.wait_ge(conv_step, 2 * TAPS * (c + 1))
                for half in range(2):
                    last = nc.tensor.matmul(PS[:, S0 + half, 0:HALF], ones[:, :],
                                            conv_o[:, c, half * HALF:(half + 1) * HALF],
                                            start=(c == 0), stop=(c == KH - 1))
            last.then_inc(mean_mm, 1)
            pe.wait_ge(so_rows, 2)
            pe.wait_ge(new_packed, KH + 1)
            for c in range(KH):
                nc.tensor.transpose(PS[0:CB, M0, c * P:(c + 1) * P], glu[:, c, PR:PR + CB], ident[:, :])
            for c in range(KH):
                last = nc.tensor.transpose(PS[0:SM, M1, c * P:(c + 1) * P], new_glu[:, c, :], ident[:, :])
            last.then_inc(so_T, 1)
            pe.wait_ge(cent_ready, KH)
            for c in range(KH):
                pe.wait_ge(csq_ready, c + 1)
                last = row_sums(sq[:, c % 2, :], first=(c == 0), final=(c == KH - 1))
                last.then_inc(csq_used, 1)
            pe.wait_ge(so_rows, 4)
            spread(1)

            def plain_units(u0, nk, rh, rl, n):
                with pe.Fori(0, n // 2) as i:
                    for j in range(2):
                        unit(j, i * 2 + (u0 + j), nk, rh, rl)

            pe.wait_ge(ya_read, KH)
            pe.wait_ge(ya_ready, KH)
            unit(0, U_OUT0, KD, hh, hl, h_lo_ready, -KH)
            unit(1, U_OUT0 + 1, KD, hh, hl)
            nb = 2 * NS * FB * 2 * KF // P
            pe.wait_ge(rstd_ready, 2)
            pe.wait_ge(ld_fs, 16)
            for b in range(nb):
                bank, c = (M0, M1, S1)[b // 4], b % 4
                last = nc.tensor.transpose(PS[:, bank, c * P:(c + 1) * P], state_rows[:, b, :], ident[:, :])
            last.then_inc(fs_T, 1)
            plain_units(U_OUT0 + 2, KD, hh, hl, KD - 2)

            def ffn(layer):
                n = 2 * layer + 1
                r = (2, 5)[layer]
                for g in range(2):
                    u0 = U_FFN[layer] + g * (2 * GT + KD)
                    if g == 0:
                        unit(0, u0, KD, xh, xl, xl_ready, KD * n)
                        norm_sums(n, r)

                        def middle():
                            if layer == 0:
                                pe.wait_ge(fs_ready, 3)
                            else:
                                pe.wait_ge(vrow_ready, 2 * KD)
                            spread(r)
                        unit(1, u0 + 1, KD, xh, xl, middle=middle)
                        plain_units(u0 + 2, KD, xh, xl, 2 * GT - 2)
                    else:
                        plain_units(u0, KD, xh, xl, 2 * GT)
                    ud = u0 + 2 * GT
                    unit(0, ud, GT, hh, hl, h_lo_ready, H_FFN[layer] + g * GT)
                    if g == 1:
                        pe.wait_ge(stash_ready, 2 * 2 * KF * (layer + 1))
                        flat_stash = stash.rearrange("p a b -> p (a b)")
                        np_, at = FB * 2 * KF, 0
                        for b in range(7):
                            n_ = np_ if b == 0 else min(P, (FB + NS * FB) * 2 * KF - at)
                            last = nc.tensor.transpose(PS[0:n_, (M0, M1)[b // 4], (b % 4) * P:(b % 4 + 1) * P],
                                                       flat_stash[:, at:at + n_], ident[:, :])
                            at += n_
                        last.then_inc(stash_T, 1)
                    if g == 0 or layer == 0:
                        unit(1, ud + 1, GT, hh, hl)
                        plain_units(ud + 2, GT, hh, hl, KD - 2)

            def out_rows(j, m):
                pe.wait_ge(xg_ready, m + 1)
                if isinstance(m, int) and m == 0:
                    pe.wait_ge(stash_rows_ready, 4)
                else:
                    pe.wait_ge(yrow_ready, m * 2)
                for r in range(CH):
                    nc.tensor.transpose(PS[:, M0, r * P:(r + 1) * P], xg[:, j, r * P:(r + 1) * P], ident[:, :])
                nc.tensor.transpose(PS[:, M1, 0:P], xg[:, j, T - P:T], ident[:, :]).then_inc(y_T, 1)

            ffn(0)

            unit(0, U_IN1, KD, xh, xl, xl_ready, KD * 2)
            norm_sums(2, 3)

            def middle1():
                pe.wait_ge(stash_rows_ready, 2)
                spread(3)
            unit(1, U_IN1 + 1, KD, xh, xl, middle=middle1)
            pe.wait_ge(ld_gw, 16)
            pe.wait_ge(rstd_ready, 4)
            for h in range(KD):
                last = nc.tensor.transpose(PS[:, M0 + h // 4, (h % 4) * P:(h % 4 + 1) * P], gate_w_rows[:, h, :],
                                           ident[:, :])
            last.then_inc(gw_T, 1)
            plain_units(U_IN1 + 2, KD, xh, xl, KD - 2)

            def v_turn(m):
                pe.wait_ge(va_ready, m + 1)
                if m == 0:
                    pe.wait_ge(rstd_ready, 5)
                else:
                    pe.wait_ge(vrow_ready, 2 * m)
                for r in range(CH):
                    nc.tensor.transpose(PS[:, M0, r * P:(r + 1) * P], V[:, m, r * P:(r + 1) * P], ident[:, :])
                nc.tensor.transpose(PS[0:SM, M1, 0:P], V[:, m, PR:T], ident[:, :]).then_inc(v_T, 1)

            def gate(m):
                pe.wait_ge(vrow_ready, 2 * m + 2)
                if m == 0:
                    pe.wait_ge(gw_ready, 1)
                    pe.wait_ge(bw_ready, 16 * NS)
                    pe.wait_ge(std_ready, 5)
                else:
                    pe.wait_ge(zb_ready, 2 * m)
                for c in range(CH):
                    nc.tensor.matmul(PS[:, S0, c * P:(c + 1) * P], v_rows[m % 2][:, c, :], gate_w_T[:, m, :],
                                     start=True, stop=True)
                nc.tensor.matmul(PS[:, S1, 0:SM], v_rows[m % 2][0:SM, CH, :], block_w[:, m, :],
                                 start=True, stop=True).then_inc(z_mm, 1)

            u0 = U_IN1 + KD
            unit(0, u0, KD, xh, xl)
            pe.wait_ge(vsum, KD - 1)
            for half in range(2):
                last = nc.tensor.matmul(PS[:, S0 + half, 0:HALF], ones[:, :], sq[:, 0, half * HALF:(half + 1) * HALF],
                                        start=True, stop=True)
            last.then_inc(mean_mm, 1)
            unit(1, u0 + 1, KD, xh, xl)
            unit(0, u0 + 2, KD, xh, xl)
            pe.wait_ge(vsq_added, KD - 1)
            pe.wait_ge(cent_ready, KH + KD)
            row_sums(sqacc).then_inc(var_mm, 1)
            unit(1, u0 + 3, KD, xh, xl, middle=lambda: spread(4))
            unit(0, u0 + 4, KD, xh, xl)
            v_turn(0)
            unit(1, u0 + 5, KD, xh, xl)
            v_turn(1)
            gate(0)
            unit(0, u0 + 6, KD, xh, xl)
            v_turn(2)
            gate(1)
            unit(1, u0 + 7, KD, xh, xl)
            for m in range(3, KD):
                v_turn(m)
                gate(m - 1)
            gate(KD - 1)

            unit(0, U_OUT1, KD, hh, hl, h_lo_ready, H_MIX[1])
            unit(1, U_OUT1 + 1, KD, hh, hl)
            plain_units(U_OUT1 + 2, KD, hh, hl, KD - 2)

            ffn(1)
            ud = U_FFN1 + N_FFN - KD
            unit(1, ud + 1, GT, hh, hl)
            out_rows(0, 0)
            with pe.Fori(0, KD // 2 - 1) as i:
                unit(0, i * 2 + (ud + 2), GT, hh, hl)
                out_rows(1, i * 2 + 1)
                unit(1, i * 2 + (ud + 3), GT, hh, hl)
                out_rows(0, i * 2 + 2)
            out_rows(1, KD - 1)
            norm_sums(4, 6)

        @block.scalar
        def _(act):
            at = 0
            for name, ap, n in rows0:
                act.dma_start(par_rows[at:at + n, 0, :], flat(ap)).then_inc(ld_p0, 16)
                at += n
            act.dma_start(par_rows[0:TAPS * KH, 1, :], conv_w.rearrange("l k (t p) -> (l k t) p", p=P)).then_inc(ld_par, 16)
            cw = ffn_conv_w.rearrange("l k (t p) -> (l k t) p", p=P)
            for b in range(3):
                n = FBLK
                act.dma_start(par_rows[0:n, 2 + b, :], cw[b * n:(b + 1) * n, :]).then_inc(ld_par, 16)
            act.dma_start(par_rows[0:FBLK, 5, :], flat(ffn_conv_b)).then_inc(ld_par, 16)
            act.dma_start(pool_rows[0:NS * PB, :], state_pool.rearrange("l s r d -> (l s r) d")).then_inc(ld_par, 16)
            act.dma_start(poolw[:, :, :], pool_w[0].rearrange("g i o -> i g o")).then_inc(ld_pw, 16)
            act.dma_start(pool_sample[0, :, 0:PB - DS, :], state_pool[0, :, DS:PB, :]).then_inc(st_state, 16)
            act.dma_start(conv_sample[0, :, 0:CB - DS, :], state_conv[0, :, DS:CB, :]).then_inc(st_state, 16)

            def split(slot, u, pair, nk):
                act.wait_ge(raw_ready[slot], (pair + 1) * 16)
                if not isinstance(u, int) or u >= 2:
                    act.wait_ge(unit_done, u - 1)
                nc.scalar.activation(w_hi[slot][:, 0:nk * P], w_raw[slot][:, 0:nk * P], ACT.Copy).then_inc(hi_ready, 1)

            def tiles_of(u):
                for f in U_FFN:
                    if f <= u < f + N_FFN and (u - f) % (2 * GT + KD) >= 2 * GT:
                        return GT
                return KD

            def split_n(u):
                if u < N_UNITS:
                    split(u % 2, u, u // 2, tiles_of(u))

            def norm_in(n, m, r, gname, gi):
                act.wait_ge(*((x_ready, m + 1) if n == 0 else (acc_free, X_FINAL[n] + m + 1)))
                nc.scalar.activation(xh[:, m, :], X[:, m, :], ACT.Identity, bias=0.0,
                                     scale=pcol(gname, gi)).then_inc(xh_ready, 1)
                square(n, m, r)

            def square(n, m, r):
                if m == 0:
                    if r:
                        act.wait_ge(var_mm, sums(r))
                        act.wait_ge(bc_mm, r)
                elif m >= 3:
                    act.wait_ge(sq_added, (KD - 1) * n + m - 2)
                dst = sqacc[:, :] if m == 0 else sq[:, m % 2, :]
                nc.scalar.activation(dst, X[:, m, :], ACT.Square).then_inc(sq_ready, 1)

            def root(r, width):
                act.wait_ge(var_mm, sums(r + 1))
                nc.scalar.activation(std[:, :], PS[:, S0, 0:RT], ACT.Sqrt, bias=eps[:, 0:1],
                                     scale=1.0 / width).then_inc(std_ready, 1)

            def take_rstd(r, dst):
                act.wait_ge(bc_mm, r + 1)
                nc.scalar.activation(dst[:, 0:PR], PS[:, M0, 0:PR], ACT.Copy)
                nc.scalar.activation(dst[:, PR:T], PS[:, M1, 0:SM], ACT.Copy).then_inc(rstd_ready, 1)

            act.wait_ge(p0_T, 1)
            nc.scalar.activation(par[:, 0:NP0], PS[:, M1, 0:NP0], ACT.Copy).then_inc(p0_ready, 1)
            split_n(0)
            act.wait_ge(p0_ready, 1)
            act.wait_ge(xs_ready, 1)
            for m in range(KD):
                norm_in(0, m, 0, "mix_norm", m)
                if m == 1:
                    split_n(1)
            act.wait_ge(setup_T, 1)
            nc.scalar.activation(par[:, NP0:NPAR], PS[:, S0, 0:NPAR - NP0], ACT.Copy).then_inc(setup_ready, 1)
            act.wait_ge(setup_T, 2)
            for c in range(KH):
                last = nc.scalar.activation(
                    smp(xa[:, c, PB + PR:XL], PB + DS)[:, :, 0:PB],
                    smp(PS[:, S1, c * NS * PB:(c + 1) * NS * PB], PB), ACT.Copy)
            last.then_inc(setup_ready, 1)
            for b in range(2):
                act.wait_ge(setup_T, 3 + b)
                for c in range(KH):
                    last = nc.scalar.activation(
                        smp(glu[:, c, CB + PR:GL], CB + DS)[:, 4 * b:4 * b + 4, 0:CB],
                        smp(PS[:, M0 + b, c * 4 * CB:(c + 1) * 4 * CB], CB), ACT.Copy)
                last.then_inc(setup_ready, 1)
            root(0, D)
            split_n(2)
            take_rstd(0, rstd)

            def pool_hi(g):
                act.wait_ge(pool_mm, g + 1)
                b = POOL_BANK[g]
                nc.scalar.activation(halves(d_t[g]), PS[:, b:b + 2, 0:HALF], ACT.Identity, bias=0.0,
                                     scale=pcol("pool_scale", g)).then_inc(ya_read, 1)
                act.wait_ge(ya_read, g + 1)
                nc.scalar.activation(hh[:, g, :], d_t[g], ACT.Copy).then_inc(ya_hi, 1)

            pair = 0
            for u in range(1, N_IN0):
                split_n(u + 2)
                if IN0[u] >= 2 * KH:
                    act.wait_ge(acc_free, u + 1)
                    nc.scalar.activation(g_t, g_t, ACT.Sigmoid).then_inc(sig_ready, 1)
                    pair += 1
            for g in range(KH):
                pool_hi(g)

            def state_rows_out(first, bank, n, dst_rows, dst):
                nc.scalar.activation(dst_rows[0:n, :], PS[0:n, bank, :], ACT.Copy).then_inc(so_rows, 1)
                act.wait_ge(so_rows, first)
                act.dma_start(dst, dst_rows[0:n, :]).then_inc(st_out, 16)

            act.wait_ge(so_T, 1)
            act.wait_ge(d_ready, KH)
            state_rows_out(1, M0, PB, out_rows0[2], pool_prompt[0, 0])
            state_rows_out(2, M1, SM, out_rows0[3], pool_sample[0, :, PB - DS:PB, :])
            for c in range(KH):
                act.wait_ge(cent_ready, c + 1)
                if c == 0:
                    act.wait_ge(ya_ready, KH)
                if c >= 2:
                    act.wait_ge(csq_used, c - 1)
                nc.scalar.activation(sq[:, c % 2, :], conv_o[:, c, :], ACT.Square).then_inc(csq_ready, 1)
                if c == 0:
                    act.wait_ge(so_T, 2)
                    state_rows_out(3, M0, CB, out_rows0[0], conv_prompt[0, 0])
                    state_rows_out(4, M1, SM, out_rows0[1], conv_sample[0, :, CB - DS:CB, :])
            act.wait_ge(csq_used, KH)
            nc.scalar.activation(std[:, :], PS[:, S0, 0:RT], ACT.Sqrt, bias=eps[:, 0:1],
                                 scale=1.0 / DH).then_inc(std_ready, 1)
            take_rstd(1, rstd)
            for c in range(KH):
                act.wait_ge(cn_ready, c + 1)
                nc.scalar.activation(conv_o[:, c, :], conv_o[:, c, :], ACT.Silu, bias=pcol("conv_norm_b", c),
                                     scale=pcol("conv_norm_g", c)).then_inc(cs_ready, 1)
                act.wait_ge(cs_ready, c + 1)
                nc.scalar.activation(hh[:, KH + c, :], conv_o[:, c, :], ACT.Copy).then_inc(hh_ready, 1)
            for m in range(KD):
                split_n(U_OUT0 + m + 2)
                if m == 1:
                    act.wait_ge(fs_T, 1)
                    st = state_T[:, :, :, :].rearrange("p l a b -> p (l a b)")
                    for b, (bank, n) in enumerate(((M0, 4 * P), (M1, 4 * P), (S1, 3 * P))):
                        nc.scalar.activation(st[:, b * 4 * P:b * 4 * P + n], PS[:, bank, 0:n], ACT.Copy)\
                            .then_inc(fs_ready, 1)
                norm_in(1, m, 1, "ffn_norm", m)

            def ffn(layer):
                n = 2 * layer + 1
                r = (2, 5)[layer]
                for g in range(2):
                    u0 = U_FFN[layer] + g * (2 * GT + KD)
                    c0 = layer * KF + g * GT

                    def step(i, ahead, start=False):
                        for j in range(2):
                            ahead(j)
                            if start and j == 0:
                                root(r, D)
                                take_rstd(r, rstd)
                            act.wait_ge(acc_free, i * 2 + (u0 + j + 1))
                            act.wait_ge(pad_ready, (i + c0) * 2 + (j + 1))
                            ti = i + (g * GT + j * KF)
                            nc.scalar.activation(cv[:, j, :], up[:, j, 0:CL], ACT.Identity,
                                                 bias=pcol("ffn_conv_b", ti + layer * 2 * KF),
                                                 scale=pcol("ffn_conv_w", ti + layer * FK * 2 * KF)).then_inc(tap0_ready, 1)
                            if j == 0:
                                act.wait_ge(tap_ready, (i + c0) * 2 + 1)
                                nc.scalar.activation(cv[:, 0, :], cv[:, 0, :], ACT.Silu).then_inc(silu_ready, 1)
                        act.wait_ge(h_ready, i + c0 + 1)
                        at_ = i if isinstance(i, int) else bass.ds(i, 1)
                        dst = hh[:, at_, :] if isinstance(i, int) else hh[:, at_, :].rearrange("p a t -> p (a t)")
                        nc.scalar.activation(dst[:, 0:PR], cv[:, 0, 0:PR], ACT.Copy)
                        nc.scalar.activation(smp(dst[:, PR:T]), smp(cv[:, 0, PR:PR + NS * (FB + DS)], FB + DS)[:, :, FB:],
                                             ACT.Copy).then_inc(hh_ready, 1)

                    first = 0
                    if g == 0:
                        step(0, lambda j: split_n(u0 + j + 2), start=True)
                        first = 1
                    with act.Fori(first, GT - 1) as i:
                        step(i, lambda j: split(j, i * 2 + (u0 + j + 2), i + (u0 // 2 + 1), KD))
                    step(GT - 1, lambda j: split_n(u0 + 2 * GT + j))
                    ud = u0 + 2 * GT
                    for m in range(KD):
                        split_n(ud + m + 2)
                        if g == 1:
                            if m == 1:
                                act.wait_ge(stash_T, layer + 1)
                                sr = stash_rows.rearrange("p a b -> p (a b)")
                                np_, ns_ = FB * 2 * KF, NS * FB * 2 * KF
                                last_n = ns_ % P
                                nc.scalar.activation(sr[0:np_, 0:P], PS[0:np_, M0, 0:P], ACT.Copy)
                                nc.scalar.activation(sr[:, P:4 * P], PS[:, M0, P:4 * P], ACT.Copy).then_inc(stash_rows_ready, 1)
                                nc.scalar.activation(sr[:, 4 * P:6 * P], PS[:, M1, 0:2 * P], ACT.Copy)
                                nc.scalar.activation(sr[0:last_n, 6 * P:7 * P], PS[0:last_n, M1, 2 * P:3 * P], ACT.Copy)\
                                    .then_inc(stash_rows_ready, 1)
                                act.wait_ge(stash_rows_ready, 2 * layer + 2)
                                fp = ffn_prompt[layer].rearrange("b r (t p) -> (b r t) p", p=P)
                                fs = ffn_sample[layer].rearrange("s r (t p) -> (s r t) p", p=P)
                                act.dma_start(fp, stash_rows[0:np_, 0, :]).then_inc(st_ffn, 16)
                                nf = ns_ // P
                                act.dma_start(fs[0:nf * P, :].rearrange("(b q) p -> q b p", q=P),
                                              stash_rows[:, 1:1 + nf, :]).then_inc(st_ffn, 16)
                                act.dma_start(fs[nf * P:ns_, :], stash_rows[0:last_n, 1 + nf, :]).then_inc(st_ffn, 16)
                            if layer == 0:
                                if m == 4:
                                    act.wait_ge(st_ffn, 48)
                                    act.wait_ge(h_lo_ready, H_FFN[0] + KF)
                                    act.dma_start(gate_w_rows, sgu_w[0].rearrange("h i j -> i h j")).then_inc(ld_gw, 16)
                                    act.dma_start(gate_b.rearrange("p h i -> p (h i)"),
                                                  sgu_bias.rearrange("l h i -> l (h i)").to_broadcast([P, KD * P]))\
                                        .then_inc(ld_gb, 16)
                                norm_in(2, m, r + 1, "mix_norm", KD + m)
                            else:
                                act.wait_ge(acc_free, X_FINAL[4] + m + 1)
                                if m >= 2:
                                    act.wait_ge(y_T, m - 1)
                                nc.scalar.activation(xg[:, m % 2, :], X[:, m, :], ACT.Identity, bias=0.0,
                                                     scale=pcol("final_norm", m)).then_inc(xg_ready, 1)
                                square(4, m, r + 1)
                                if m >= 1:
                                    take_y(m - 1)
                    if g == 1 and layer == 1:
                        take_y(KD - 1)

            def take_y(m):
                act.wait_ge(y_T, m + 1)
                nc.scalar.activation(y_rows[:, 0:CH, m * P:(m + 1) * P],
                                     PS[:, M0, :].rearrange("p (r c) -> p r c", r=CH), ACT.Copy).then_inc(yrow_ready, 1)
                nc.scalar.activation(y_rows[P - SM:P, CH, m * P:(m + 1) * P], PS[P - SM:P, M1, 0:P], ACT.Copy)\
                    .then_inc(yrow_ready, 1)

            ffn(0)

            def v_square(m):
                act.wait_ge(cent_ready, KH + m + 1)
                if m == 0:
                    act.wait_ge(bc_mm, 4)
                    act.wait_ge(var_mm, sums(4))
                elif m >= 3:
                    act.wait_ge(vsq_added, m - 2)
                dst = sqacc[:, :] if m == 0 else sq[:, m % 2, :]
                nc.scalar.activation(dst, V[:, m, :], ACT.Square).then_inc(vsq_ready, 1)

            split_n(U_IN1 + 2)
            root(3, D)
            take_rstd(3, rstd)
            split_n(U_IN1 + 3)
            act.wait_ge(gw_T, 1)
            act.wait_ge(ld_gb, 16)
            nc.scalar.activation(gate_w_T[:, 0:4, :], PS[:, M0, :].rearrange("p (h i) -> p h i", h=4), ACT.Copy)
            nc.scalar.activation(gate_w_T[:, 4:8, :], PS[:, M1, :].rearrange("p (h i) -> p h i", h=4), ACT.Copy)\
                .then_inc(gw_copied, 1)
            for m in range(2, KD):
                split_n(U_IN1 + m + 2)
                if m == 5:
                    act.wait_ge(gw_ready, 1)
                    act.wait_ge(bw_zero, 1)
                    for s in range(NS):
                        act.dma_start(block_w[s * DS:(s + 1) * DS, :, s * DS:(s + 1) * DS],
                                      gate_w_T[0:DS, :, 0:DS]).then_inc(bw_ready, 16)

            def v_affine(m):
                act.wait_ge(vn_ready, m + 1)
                nc.scalar.activation(V[:, m, :], V[:, m, :], ACT.Identity, bias=pcol("sgu_norm_b", m),
                                     scale=pcol("sgu_norm_g", m)).then_inc(va_ready, 1)

            def v_take(m):
                act.wait_ge(v_T, m + 1)
                if m >= 2:
                    act.wait_ge(st_v[m % 2], 32 * (m // 2))
                    act.wait_ge(z_mm, m - 1)
                nc.scalar.activation(v_rows[m % 2][:, 0:CH, :], PS[:, M0, :].rearrange("p (r c) -> p r c", r=CH), ACT.Copy)\
                    .then_inc(vrow_ready, 1)
                nc.scalar.activation(v_rows[m % 2][0:SM, CH, :], PS[0:SM, M1, 0:P], ACT.Copy).then_inc(vrow_ready, 1)
                act.wait_ge(vrow_ready, 2 * m + 2)
                act.dma_start(sgu_v_prompt[0, 0, :, m * P:(m + 1) * P], v_rows[m % 2][:, CH - 1, :]).then_inc(st_v[m % 2], 16)
                act.dma_start(sgu_v_sample[0, :, :, m * P:(m + 1) * P].rearrange("s t p -> (s t) p"),
                              v_rows[m % 2][0:SM, CH, :]).then_inc(st_v[m % 2], 16)

            def uz_hi(m):
                act.wait_ge(uz_ready, m + 1)
                nc.scalar.activation(hh[:, m, :], U[:, m, :], ACT.Copy).then_inc(hh_ready, 1)

            uu = U_IN1 + KD
            split_n(uu + 2)
            for m in range(4):
                v_square(m)
            split_n(uu + 3)
            for m in range(4, KD):
                v_square(m)
            split_n(uu + 4)
            root(4, D)
            split_n(uu + 5)
            take_rstd(4, rstd_v)
            for m in range(3):
                v_affine(m)
            split_n(uu + 6)
            v_take(0)
            for m in range(3, KD):
                v_affine(m)
            split_n(uu + 7)
            v_take(1)
            split_n(uu + 8)
            v_take(2)
            uz_hi(0)
            split_n(uu + 9)
            for m in range(3, KD):
                v_take(m)
                uz_hi(m - 2)
            uz_hi(KD - 2)
            uz_hi(KD - 1)
            for m in range(KD):
                split_n(U_OUT1 + m + 2)
                norm_in(3, m, 5, "ffn_norm", KD + m)

            ffn(1)
            root(6, D)
            act.wait_ge(rinv_ready, 7)
            for r in (1, 3):
                nc.scalar.activation(y_rows[:, r, :], y_rows[:, r, :], ACT.Copy, scale=rinv[:, r:r + 1])\
                    .then_inc(y_scaled, 1)
                act.wait_ge(y_scaled, (r + 1) // 2)
                act.dma_start(yp_rows[:, r, :], y_rows[:, r, :]).then_inc(st_y, 16)

        @block.gpsimd
        def _(pool):
            nc.gpsimd.memset(ones[:, :], 1.0).then_inc(const_ready, 1)
            pool.wait_ge(const_ready, 1)
            nc.gpsimd.affine_select(out=ident[:, :], in_=ones[:, :], compare_op=ALU.is_equal, fill=0.0, base=0,
                                    pattern=[[-1, P]], channel_multiplier=1).then_inc(ident_ready, 1)
            nc.gpsimd.memset(eps[:, :], EPS).then_inc(const_ready, 1)
            at = 0
            for w in WINDOWS:
                for j in range(w - 1):
                    nc.gpsimd.memset(corr[:, at:at + 1], w / (j + 1)).then_inc(corr_ready, 1)
                    at += 1

            def split(slot, u, nk):
                pool.wait_ge(hi_ready, u + 1)
                nc.gpsimd.tensor_tensor(w_lo[slot][:, 0:nk * P], w_raw[slot][:, 0:nk * P],
                                        w_hi[slot][:, 0:nk * P].bitcast(F32), ALU.subtract).then_inc(lo_ready, 1)

            def tiles_of(u):
                for f in U_FFN:
                    if f <= u < f + N_FFN and (u - f) % (2 * GT + KD) >= 2 * GT:
                        return GT
                return KD

            def split_n(u):
                if u < N_UNITS:
                    split(u % 2, u, tiles_of(u))

            def add_square(n, m):
                pool.wait_ge(sq_ready, KD * n + m + 1)
                if m > 1:
                    pool.wait_ge(sq_added, (KD - 1) * n + m - 1)
                nc.gpsimd.tensor_tensor(sqacc[:, :], sqacc[:, :], sq[:, m % 2, :], ALU.add).then_inc(sq_added, 1)

            split_n(0)
            for m in range(1, KD):
                add_square(0, m)
                if m == 1:
                    split_n(1)
            nc.gpsimd.memset(xa[:, :, 0:PB], 0.0).then_inc(pads_zero, 1)
            nc.gpsimd.memset(glu[:, :, 0:CB], 0.0).then_inc(pads_zero, 1)

            steps = [0]

            def windows(g):
                pool.wait_ge(acc_free, U_IN0 + 4 + g + 1)
                pool.wait_ge(setup_ready, 2)
                if g == 0:
                    pool.wait_ge(corr_ready, sum(WINDOWS) - len(WINDOWS))
                    pool.wait_ge(setup_ready, 4)
                    pool.wait_ge(bc_mm, 1)
                else:
                    pool.wait_ge(d_ready, g)
                nc.gpsimd.tensor_copy(smp(new_x[:, g, :]), smp(xa[:, g, PB + PR:XL], PB + DS)[:, :, PB:])\
                    .then_inc(new_packed, 1)
                src, lo, width = xa[:, g, :], 0, 1
                for level in range(g + 1):
                    dst = pool_tmp[(level + g) % 2]
                    lo += width
                    nc.gpsimd.tensor_tensor(dst[:, lo:XL], src[:, lo:XL], src[:, lo - width:XL - width], ALU.add)\
                        .then_inc(win_step, 1)
                    steps[0] += 1
                    pool.wait_ge(win_step, steps[0])
                    src, width = dst, 2 * width
                w = WINDOWS[g]
                c0 = sum(WINDOWS[:g]) - g
                nc.gpsimd.tensor_tensor(src[:, PB:PB + w - 1], src[:, PB:PB + w - 1], corr[:, c0:c0 + w - 1], ALU.mult)\
                    .then_inc(win_step, 1)
                pool.wait_ge(win_step, steps[0] + 1)
                nc.gpsimd.tensor_scalar(src[:, PB:XL], src[:, PB:XL], 1.0 / w, 1.0, ALU.mult, ALU.mult)\
                    .then_inc(win_step, 1)
                steps[0] += 2
                pool.wait_ge(win_step, steps[0])
                nc.gpsimd.tensor_tensor(d_t[g][:, 0:PR], src[:, PB:PB + PR], xa[:, g, PB:PB + PR], ALU.subtract)
                new = lambda v: smp(v[:, PB + PR:XL], PB + DS)[:, :, PB:]
                nc.gpsimd.tensor_tensor(smp(d_t[g][:, PR:T]), new(src), new(xa[:, g, :]), ALU.subtract)\
                    .then_inc(d_ready, 1)

            for u in range(0, N_IN0):
                split_n(u + 2)
                if u in (4, 5, 6, 7):
                    windows(u - 4)
            pool.wait_ge(glu_ready, 2 * KH)
            for c in range(KH):
                last = nc.gpsimd.tensor_copy(smp(new_glu[:, c, :]), smp(glu[:, c, CB + PR:GL], CB + DS)[:, :, CB:])
            last.then_inc(new_packed, 1)
            for g in range(KH):
                pool.wait_ge(ya_hi, g + 1)
                nc.gpsimd.tensor_tensor(hl[:, g, :], d_t[g], hh[:, g, :].bitcast(F32), ALU.subtract)\
                    .then_inc(ya_ready, 1)
            for m in range(KD):
                split_n(U_OUT0 + m + 2)
                if m:
                    add_square(1, m)
            pool.wait_ge(st_out, 16 * 4)
            pool.wait_ge(xl_ready, 2 * KD)
            nc.gpsimd.memset(up[:, :, 0:FB], 0.0).then_inc(pads_zero, 1)

            def ffn(layer):
                for g in range(2):
                    u0 = U_FFN[layer] + g * (2 * GT + KD)
                    c0 = layer * KF + g * GT
                    so = state_T[:, layer, :, :]

                    def pads(j, i):
                        ti = i + (g * GT + j * KF)
                        src = so[:, :, ti:ti + 1] if isinstance(ti, int) else so[:, :, bass.ds(ti, 1)]
                        nc.gpsimd.tensor_copy(smp(up[:, j, FB + PR:UL], FB + DS)[:, :, 0:FB],
                                              src.rearrange("p (s r) o -> p s (r o)", r=FB)).then_inc(pad_ready, 1)

                    def step(i, ahead, start=False):
                        for j in range(2):
                            ahead(j)
                            if start and layer == 0 and j == 0:
                                pool.wait_ge(fs_ready, 3)
                            if not (layer == 0 and start):
                                pool.wait_ge(tap_ready, (i + c0) * 2 + (j - 1))
                            pads(j, i)
                            pool.wait_ge(acc_free, i * 2 + (u0 + j + 1))
                            ti = i + (g * GT + j * KF)
                            dst = stash[:, :, ti:ti + 1] if isinstance(ti, int) else stash[:, :, bass.ds(ti, 1)]
                            nc.gpsimd.tensor_copy(dst[:, 0:FB, :].rearrange("p r o -> p (r o)"), up[:, j, PR:PR + FB])\
                                .then_inc(stash_ready, 1)
                            nc.gpsimd.tensor_copy(
                                dst[:, FB:, :].rearrange("p (s r) o -> p s (r o)", r=FB),
                                smp(up[:, j, FB + PR:UL], FB + DS)[:, :, DS:DS + FB]).then_inc(stash_ready, 1)

                    first = 0
                    if g == 0:
                        step(0, lambda j: split_n(u0 + j + 2), start=True)
                        first = 1
                    with pool.Fori(first, GT - 1) as i:
                        step(i, lambda j: split(j, i * 2 + (u0 + j + 2), KD))
                    step(GT - 1, lambda j: split_n(u0 + 2 * GT + j))
                    ud = u0 + 2 * GT
                    for m in range(KD):
                        split_n(ud + m + 2)
                        if g == 1 and m:
                            add_square(2 * layer + 2, m)

            ffn(0)
            nc.gpsimd.memset(block_w, 0.0).then_inc(bw_zero, 1)
            for m in range(KD):
                split_n(U_IN1 + m + 2)
                if m == 2:
                    pool.wait_ge(gw_copied, 1)
                    nc.gpsimd.affine_select(out=gate_w_T, in_=gate_w_T, compare_op=ALU.is_ge, fill=0.0, base=0,
                                            pattern=[[0, KD], [1, P]], channel_multiplier=-1).then_inc(gw_ready, 1)
                if m == 1:
                    pool.wait_ge(acc_free, U_IN1 + 2)
                    pool.wait_ge(bc_mm, 4)
                    nc.gpsimd.tensor_tensor(sq[:, 0, :], V[:, 0, :], V[:, 1, :], ALU.add).then_inc(vsum, 1)
                elif m > 1:
                    pool.wait_ge(acc_free, U_IN1 + m + 1)
                    pool.wait_ge(vsum, m - 1)
                    nc.gpsimd.tensor_tensor(sq[:, 0, :], sq[:, 0, :], V[:, m, :], ALU.add).then_inc(vsum, 1)

            def add_v_square(m):
                pool.wait_ge(vsq_ready, m + 1)
                if m > 1:
                    pool.wait_ge(vsq_added, m - 1)
                nc.gpsimd.tensor_tensor(sqacc[:, :], sqacc[:, :], sq[:, m % 2, :], ALU.add).then_inc(vsq_added, 1)

            uu = U_IN1 + KD
            split_n(uu + 2)
            for m in range(1, 4):
                add_v_square(m)
            split_n(uu + 3)
            for m in range(4, KD):
                add_v_square(m)
            for m in range(2, KD):
                split_n(uu + m + 2)
            for m in range(KD):
                split_n(U_OUT1 + m + 2)
                if m:
                    add_square(3, m)
            pool.wait_ge(xl_ready, 4 * KD)
            pool.wait_ge(st_v[0], 16 * KD)
            pool.wait_ge(st_v[1], 16 * KD)
            nc.gpsimd.memset(up[:, :, 0:FB], 0.0).then_inc(pads_zero, 1)
            ffn(1)

        @block.vector
        def _(dve):
            def x_lo(n, m, gname, gi):
                dve.wait_ge(xh_ready, KD * n + m + 1)
                nc.vector.scalar_tensor_tensor(out=xl[:, m, :], in0=X[:, m, :], scalar=pcol(gname, gi),
                                               in1=xh[:, m, :].bitcast(F32), op0=ALU.mult, op1=ALU.subtract)\
                    .then_inc(xl_ready, 1)

            def residual(u, m):
                dve.wait_ge(unit_done, u + 1)
                nc.vector.tensor_tensor(halves(X[:, m, :]), acc(u % 2), halves(X[:, m, :]), ALU.add)\
                    .then_inc(acc_free, 1)

            def factors(r):
                dve.wait_ge(std_ready, r + 1)
                nc.vector.reciprocal(rinv[:, :], std[:, :]).then_inc(rinv_ready, 1)
                dve.wait_ge(rinv_ready, r + 1)
                if r < 6:
                    for t in range(RT):
                        last = nc.vector.tensor_scalar(diag[:, t, :], ident[:, :], rinv[:, t:t + 1], None, ALU.mult)
                    last.then_inc(diag_ready, 1)

            def scaled(u, dst):
                dve.wait_ge(unit_done, u + 1)
                nc.vector.tensor_tensor(halves(dst), acc(u % 2), halves(rstd[:, :]), ALU.mult).then_inc(acc_free, 1)

            def scaled_padded(slot, u, dst, pad):
                dve.wait_ge(unit_done, u + 1)
                nc.vector.tensor_tensor(dst[:, pad:pad + HALF], PS[:, 2 * slot, 0:HALF], rstd[:, 0:HALF], ALU.mult)
                nc.vector.tensor_tensor(dst[:, pad + HALF:pad + PR], PS[:, 2 * slot + 1, 0:PR - HALF],
                                        rstd[:, HALF:PR], ALU.mult)
                n = NS * (pad + DS)
                nc.vector.tensor_tensor(smp(dst[:, pad + PR:pad + PR + n], pad + DS)[:, :, pad:],
                                        smp(PS[:, 2 * slot + 1, PR - HALF:HALF]), smp(rstd[:, PR:T]), ALU.mult)\
                    .then_inc(acc_free, 1)

            dve.wait_ge(xs_T, 1)
            nc.vector.tensor_copy(X[:, :, PR:T], smp(PS[:, 0, :], SM)).then_inc(xs_ready, 1)
            for k in range(KD):
                dve.wait_ge(xT, k + 1)
                nc.vector.tensor_copy(X[:, k, 0:PR], PS[:, (k + 1) % 8, :]).then_inc(x_ready, 1)
            for m in range(KD):
                x_lo(0, m, "mix_norm", m)
            factors(0)
            dve.wait_ge(rstd_ready, 1)

            conv_steps = [0]

            def conv_pair(u, c):
                if c == 0:
                    dve.wait_ge(pads_zero, 2)
                    dve.wait_ge(setup_ready, 4)
                scaled(u, a_t)
                scaled(u + 1, g_t)
                dve.wait_ge(sig_ready, c + 1)
                nc.vector.tensor_tensor(glu[:, c, CB:CB + PR], a_t[:, 0:PR], g_t[:, 0:PR], ALU.mult)\
                    .then_inc(glu_ready, 1)
                nc.vector.tensor_tensor(smp(glu[:, c, CB + PR:GL], CB + DS)[:, :, CB:], smp(a_t[:, PR:T]),
                                        smp(g_t[:, PR:T]), ALU.mult).then_inc(glu_ready, 1)
                dve.wait_ge(glu_ready, 2 * c + 2)
                for k in range(TAPS):
                    w = pcol("conv_w", k * KH + c)
                    sides = ((conv_o[:, c, 0:PR], glu[:, c, k:k + PR]),
                             (smp(conv_o[:, c, PR:T]), smp(glu[:, c, CB + PR:GL], CB + DS)[:, :, k:k + DS]))
                    for side, (o, win) in enumerate(sides):
                        if k == 0:
                            ins = nc.vector.tensor_scalar(o, win, w, pcol("conv_b", c), ALU.mult, ALU.add)
                        else:
                            dve.wait_ge(conv_step, conv_steps[0] - 1)
                            ins = nc.vector.scalar_tensor_tensor(out=o, in0=win, scalar=w, in1=o,
                                                                 op0=ALU.mult, op1=ALU.add)
                        ins.then_inc(conv_step, 1)
                        conv_steps[0] += 1

            conv_pair(0, 0)
            conv_pair(2, 1)
            for g in range(KH):
                scaled_padded(g % 2, U_IN0 + 4 + g, xa[:, g, :], PB)
            conv_pair(8, 2)
            conv_pair(10, 3)
            dve.wait_ge(mean_mm, 1)
            for c in range(KH):
                nc.vector.scalar_tensor_tensor(out=halves(conv_o[:, c, :]), in0=PS[:, S0:S1 + 1, 0:HALF],
                                               scalar=-1.0 / DH, in1=halves(conv_o[:, c, :]), op0=ALU.mult,
                                               op1=ALU.add).then_inc(cent_ready, 1)
            factors(1)
            dve.wait_ge(rstd_ready, 2)
            for c in range(KH):
                nc.vector.tensor_tensor(conv_o[:, c, :], conv_o[:, c, :], rstd[:, :], ALU.mult).then_inc(cn_ready, 1)
            for c in range(KH):
                dve.wait_ge(hh_ready, c + 1)
                nc.vector.tensor_tensor(hl[:, KH + c, :], conv_o[:, c, :], hh[:, KH + c, :].bitcast(F32), ALU.subtract)\
                    .then_inc(h_lo_ready, 1)
            for m in range(KD):
                residual(U_OUT0 + m, m)
                x_lo(1, m, "ffn_norm", m)

            def ffn(layer):
                n = 2 * layer + 1
                r = (2, 5)[layer]
                for g in range(2):
                    u0 = U_FFN[layer] + g * (2 * GT + KD)
                    c0 = layer * KF + g * GT

                    def step(i):
                        for j in range(2):
                            u = i * 2 + (u0 + j)
                            if layer or g or not isinstance(i, int) or i > 0:
                                dve.wait_ge(stash_ready, (i + c0) * 4 + (2 * j - 2))
                            scaled_padded(j, u, up[:, j, :], FB)
                            dve.wait_ge(tap0_ready, (i + c0) * 2 + (j + 1))
                            ti = i + (g * GT + j * KF)
                            for k in range(1, FK):
                                if k > 1:
                                    dve.wait_ge(tap1_ready, (i + c0) * 2 + (j + 1))
                                nc.vector.scalar_tensor_tensor(
                                    out=cv[:, j, :], in0=up[:, j, k:k + CL],
                                    scalar=pcol("ffn_conv_w", ti + (layer * FK + k) * 2 * KF), in1=cv[:, j, :],
                                    op0=ALU.mult, op1=ALU.add).then_inc(tap1_ready if k == 1 else tap_ready, 1)
                        dve.wait_ge(silu_ready, i + c0 + 1)
                        dve.wait_ge(tap_ready, (i + c0) * 2 + 2)
                        nc.vector.tensor_tensor(cv[:, 0, :], cv[:, 0, :], cv[:, 1, :], ALU.mult).then_inc(h_ready, 1)
                        dve.wait_ge(h_ready, i + c0 + 1)
                        dve.wait_ge(hh_ready, i + (H_FFN[layer] + g * GT + 1))
                        if isinstance(i, int):
                            hi_, lo_ = hh[:, i, :], hl[:, i, :]
                        else:
                            hi_ = hh[:, bass.ds(i, 1), :].rearrange("p a t -> p (a t)")
                            lo_ = hl[:, bass.ds(i, 1), :].rearrange("p a t -> p (a t)")
                        nc.vector.tensor_tensor(lo_[:, 0:PR], cv[:, 0, 0:PR], hi_[:, 0:PR].bitcast(F32), ALU.subtract)
                        nc.vector.tensor_tensor(smp(lo_[:, PR:T]), smp(cv[:, 0, PR:PR + NS * (FB + DS)], FB + DS)[:, :, FB:],
                                                smp(hi_[:, PR:T].bitcast(F32)), ALU.subtract).then_inc(h_lo_ready, 1)

                    first = 0
                    if g == 0:
                        factors(r)
                        dve.wait_ge(rstd_ready, r + 1 if layer == 0 else r + 1)
                        step(0)
                        first = 1
                    with dve.Fori(first, GT) as i:
                        step(i)
                    ud = u0 + 2 * GT
                    for m in range(KD):
                        residual(ud + m, m)
                        if g == 1 and layer == 0:
                            x_lo(2, m, "mix_norm", KD + m)

            ffn(0)

            dve.wait_ge(st_ffn, 48)
            factors(3)
            dve.wait_ge(rstd_ready, 4)
            for m in range(KD):
                scaled(U_IN1 + m, V[:, m, :])
            uu = U_IN1 + KD

            def u_take(m):
                if m == 0:
                    dve.wait_ge(gw_T, 1)
                scaled(uu + m, U[:, m, :])

            def v_norm(m):
                nc.vector.tensor_tensor(V[:, m, :], V[:, m, :], rstd_v[:, :], ALU.mult).then_inc(vn_ready, 1)

            def z_bias(m):
                dve.wait_ge(z_mm, m + 1)
                nc.vector.tensor_tensor(V[:, m, 0:PR].rearrange("p (c i) -> p c i", c=CH),
                                        PS[:, S0, :].rearrange("p (c i) -> p c i", c=CH),
                                        gate_b[:, m:m + 1, :].to_broadcast([P, CH, P]), ALU.add).then_inc(zb_ready, 1)
                nc.vector.tensor_tensor(smp(V[:, m, PR:T]), smp(PS[:, S1, 0:SM]),
                                        gate_b[:, m:m + 1, 0:DS].to_broadcast([P, NS, DS]), ALU.add).then_inc(zb_ready, 1)

            def uz(m):
                dve.wait_ge(zb_ready, 2 * m + 2)
                dve.wait_ge(acc_free, uu + m + 1)
                nc.vector.tensor_tensor(U[:, m, :], U[:, m, :], V[:, m, :], ALU.mult).then_inc(uz_ready, 1)

            def uz_lo(m):
                dve.wait_ge(uz_ready, m + 1)
                dve.wait_ge(hh_ready, H_MIX[1] + m + 1)
                nc.vector.tensor_tensor(hl[:, m, :], U[:, m, :], hh[:, m, :].bitcast(F32), ALU.subtract)\
                    .then_inc(h_lo_ready, 1)

            u_take(0)
            dve.wait_ge(mean_mm, 2)
            for m in range(KD):
                nc.vector.scalar_tensor_tensor(out=halves(V[:, m, :]), in0=PS[:, S0:S1 + 1, 0:HALF],
                                               scalar=-1.0 / D, in1=halves(V[:, m, :]), op0=ALU.mult,
                                               op1=ALU.add).then_inc(cent_ready, 1)
            u_take(1)
            u_take(2)
            factors(4)
            dve.wait_ge(rstd_ready, 5)
            for m in range(2):
                v_norm(m)
            u_take(3)
            for m in range(2, KD):
                v_norm(m)
            u_take(4)
            dve.wait_ge(ld_gb, 16)
            u_take(5)
            z_bias(0)
            uz(0)
            u_take(6)
            uz_lo(0)
            z_bias(1)
            uz(1)
            u_take(7)
            for m in range(2, KD):
                z_bias(m)
                uz_lo(m - 1)
                uz(m)
            uz_lo(KD - 1)
            for m in range(KD):
                residual(U_OUT1 + m, m)
                x_lo(3, m, "ffn_norm", KD + m)

            ffn(1)
            factors(6)
            dve.wait_ge(yrow_ready, 2 * KD)
            for n, r in enumerate((0, 2, CH)):
                if r < CH:
                    rows = y_rows[:, r, :]
                    nc.vector.tensor_scalar(rows, rows, rinv[:, r:r + 1], None, ALU.mult).then_inc(y_row_done, 1)
                else:
                    rows = y_rows[P - SM:P, CH, :]
                    nc.vector.tensor_scalar(rows, rows, rinv[P - SM:P, CH:CH + 1], None, ALU.mult).then_inc(y_row_done, 1)


_INS = ["x_prompt", "x_sample", "state_pool", "state_conv", "state_ffn", "mix_norm", "w_in_ab", "pool_w",
        "pool_scale", "conv_w", "conv_b", "conv_norm_g", "conv_norm_b", "w_out_ab", "w_in_c", "sgu_norm_g",
        "sgu_norm_b", "sgu_w", "sgu_bias", "w_out_c", "ffn_norm", "w_up", "ffn_conv_w", "ffn_conv_b", "w_down",
        "final_norm"]

def kernel(**inputs):
    import numpy as np
    import concourse.bacc as bacc
    from concourse.bass_utils import run_bass_kernel_spmd

    nc = bacc.Bacc("TRN2", target_bir_lowering=False, num_devices=1)
    arrays, args = {}, {}
    for name in _INS:
        a = np.ascontiguousarray(inputs[name])
        arrays[f"in_{name}"] = a
        args[name] = nc.dram_tensor(f"in_{name}", a.shape, mybir.dt.from_np(a.dtype), kind="ExternalInput").ap()
    xp, xs = arrays["in_x_prompt"].shape, arrays["in_x_sample"].shape
    sp, sc, sf = (arrays[f"in_state_{n}"].shape for n in ("pool", "conv", "ffn"))
    outs = {
        "y_prompt": xp, "y_sample": xs,
        "pool_prompt": (sp[0], xp[0], *sp[2:]), "pool_sample": sp,
        "conv_prompt": (sc[0], xp[0], *sc[2:]), "conv_sample": sc,
        "sgu_v_prompt": (1, xp[0], P, xp[2]), "sgu_v_sample": (1, *xs),
        "ffn_prompt": (sf[0], xp[0], *sf[2:]), "ffn_sample": sf,
    }
    for name, shape in outs.items():
        args[name] = nc.dram_tensor(f"out_{name}", shape, F32, kind="ExternalOutput").ap()
    hybrid_trunk(nc, **args)
    r = run_bass_kernel_spmd(nc, [arrays], core_ids=[0])
    return tuple(r.results[0][f"out_{name}"] for name in outs)
```

```python
from contextlib import ExitStack

import concourse.bass as bass
from concourse import mybir

F32 = mybir.dt.float32
F32R = mybir.dt.float32r
ALU = mybir.AluOpType
ACT = mybir.ActivationFunctionType
P = 128

PSUM_BANK = 512
WINDOWS = (2, 4, 8, 16)


def hybrid_trunk(nc, x_prompt, x_sample, state_pool, state_conv, state_ffn, mix_norm, w_in_ab, pool_w,
                 pool_scale, conv_w, conv_b, conv_norm_g, conv_norm_b, w_out_ab, w_in_c, sgu_norm_g,
                 sgu_norm_b, sgu_w, sgu_bias, w_out_c, ffn_norm, w_up, ffn_conv_w, ffn_conv_b, w_down,
                 final_norm, y_prompt, y_sample, pool_prompt, pool_sample, conv_prompt, conv_sample,
                 sgu_v_prompt, sgu_v_sample, ffn_prompt, ffn_sample):
    _, PR, D = x_prompt.shape
    NS, DS, _ = x_sample.shape
    SM = NS * DS
    T = PR + SM
    HALF = T // 2
    KD = D // P
    DH = D // 2
    KH = DH // P
    DF = w_down.shape[1]
    KF = DF // P
    GROUPS = ((0, 8), (8, 8), (16, KF - 16))
    PB = state_pool.shape[2]
    CB = state_conv.shape[2]
    TAPS = CB + 1
    PE_TAPS = 7
    V_TAPS = TAPS - PE_TAPS
    FB = state_ffn.shape[2]
    FK = FB + 1
    CH = PR // P
    EPS = 1e-6
    RT = CH + 1

    U_IN0 = 0
    N_IN0 = 3 * KH
    U_OUT0 = U_IN0 + N_IN0
    U_FFN0 = U_OUT0 + 2 * KD
    N_FFN = 2 * KF + len(GROUPS) * KD
    U_IN1 = U_FFN0 + N_FFN
    U_OUT1 = U_IN1 + 2 * KD
    U_FFN1 = U_OUT1 + KD
    U_FFN = (U_FFN0, U_FFN1)
    N_UNITS = U_FFN1 + N_FFN
    U_GROUP = [sum(2 * n + KD for _, n in GROUPS[:g]) for g in range(len(GROUPS))]
    POOL_ORDER = tuple(reversed(range(KH)))
    PAIR_UNIT = (0, 2, 4, 8)
    POOL_UNIT = (6, 7, 10, 11)
    IN0 = [None] * N_IN0
    for c, u in enumerate(PAIR_UNIT):
        IN0[u], IN0[u + 1] = KH + c, 2 * KH + c
    for g, u in zip(POOL_ORDER, POOL_UNIT):
        IN0[u] = g
    assert KH == 4 and not any(u % 4 for u in (U_OUT0, U_FFN0, U_IN1, U_OUT1, U_FFN1, *U_GROUP))

    def tiles_of(u):
        if U_OUT0 <= u < U_FFN0:
            return KH
        for f in U_FFN:
            for b, (_, n) in zip(U_GROUP, GROUPS):
                if f + b + 2 * n <= u < f + b + 2 * n + KD:
                    return n
        return KD

    H_MIX = (0, KH + KF)
    H_FFN = (KH, KH + KF + KD)
    X_FINAL = (None, U_OUT0 + KD, U_IN1 - KD, U_OUT1, N_UNITS - KD)

    rows0 = [("mix_norm", mix_norm, 2 * KD), ("ffn_norm", ffn_norm, 2 * KD), ("final_norm", final_norm, KD),
             ("pool_scale", pool_scale, KH), ("conv_b", conv_b, KH), ("conv_norm_g", conv_norm_g, KH),
             ("conv_norm_b", conv_norm_b, KH), ("sgu_norm_g", sgu_norm_g, KD), ("sgu_norm_b", sgu_norm_b, KD)]
    PC = {}
    at = 0
    for name, _, n in rows0:
        PC[name] = at
        at += n
    NP0 = at
    PC["conv_w"] = NP0
    PC["ffn_conv_w"] = PC["conv_w"] + TAPS * KH
    PC["ffn_conv_b"] = PC["ffn_conv_w"] + 2 * FK * 2 * KF
    NPAR = PC["ffn_conv_b"] + 2 * 2 * KF
    FBLK = 2 * 2 * KF

    GL = CB + PR + NS * (CB + DS)
    XL = PB + PR + NS * (PB + DS)
    UL = FB + PR + NS * (FB + DS)
    CL = UL - FB

    flat = lambda ap: ap.rearrange("l (t p) -> (l t) p", p=P) if len(ap.shape) == 2 else ap.rearrange("(t p) -> t p", p=P)
    wblocks = lambda w: w.rearrange("(k p) n -> p k n", p=P)
    xp_rows = x_prompt.rearrange("b (r p) d -> p (b r) d", p=P)
    xs_rows = x_sample.rearrange("s t d -> (s t) d")
    yp_rows = y_prompt.rearrange("b (r p) d -> p (b r) d", p=P)
    ys_rows = y_sample.rearrange("s t d -> (s t) d")

    with ExitStack() as ctx:
        def sb(name, shape, dt=F32):
            return ctx.enter_context(nc.sbuf_tensor(name, shape, dt))

        def sem(name):
            return ctx.enter_context(nc.semaphore(name))

        ctx.enter_context(nc.allow_non_contiguous_dma(reason="small state rows"))
        X = sb("residual", [P, KD, T])
        xh = sb("x_hi", [P, KD, T], F32R)
        xl = sb("x_lo", [P, KD, T], F32R)
        hh = sb("h_hi", [P, KD, T], F32R)
        hl = sb("h_lo", [P, KD, T], F32R)
        w_raw = [sb(f"w_raw{s}", [P, KD * P]) for s in range(2)]
        w_hi = [sb(f"w_hi{s}", [P, KD * P], F32R) for s in range(4)]
        w_lo = [sb(f"w_lo{s}", [P, KD * P], F32R) for s in range(4)]
        par = sb("params", [P, NPAR])
        state_T = sb("ffn_state_T", [P, 2, NS * FB, 2 * KF])
        ident = sb("ident", [P, P])
        ones = sb("ones", [P, P])
        rstd = sb("rstd", [P, T])
        sq = sb("squares", [P, 2, T])
        sqacc = sb("squares_sum", [P, T])
        poolw = sb("pool_w_sb", [P, KH, P])
        eps = sb("eps", [P, 1])
        std = sb("std", [P, RT])
        rinv = sb("rinv", [P, RT])
        corr = sb("count_corr", [P, sum(WINDOWS) - len(WINDOWS)])
        ARENA = 14800
        arena = sb("arena", [P, ARENA])
        diag = sq[:, :, :].rearrange("p a t -> p (a t)")[:, 0:RT * P].rearrange("p (r c) -> p r c", r=RT)

        def cut(start, *dims):
            n = 1
            for d in dims:
                n *= d
            assert start + n <= ARENA, (start, n)
            v = arena[:, start:start + n]
            if len(dims) == 2:
                v = v.rearrange("p (a b) -> p a b", a=dims[0])
            return v

        x_rows = cut(0, RT, D)
        conv_o = cut(0, KH, T)
        ag = cut(KH * T, 4, T)
        X1 = RT * D
        par_rows = cut(X1, 6, P)
        pool_rows = cut(X1 + 6 * P, DH)
        conv_rows = cut(X1 + 6 * P + DH, 2, DH)
        pool_tmp = [cut(2 * KH * T, XL), cut(2 * KH * T + XL, XL)]
        D0 = 2 * KH * T + 2 * XL + 2
        d_t = [cut(D0, T), cut(D0 + T, T), sq[:, 0, :], sq[:, 1, :]]
        XA0 = X1 + 6 * P + 3 * DH
        xa = cut(XA0, KH, XL)
        glu = cut(XA0 + KH * XL, KH, GL)
        tap_w = cut(XA0 + KH * XL + KH * GL, PE_TAPS, P)
        new_x = sqacc[:, 0:KH * SM].rearrange("p (a b) -> p a b", a=KH)
        new_glu = sqacc[:, KH * SM:2 * KH * SM].rearrange("p (a b) -> p a b", a=KH)
        out_rows0 = [ag[:, 0, 0:DH], ag[:, 1, 0:DH], pool_tmp[0][:, 0:DH], pool_tmp[1][:, 0:DH]]
        state_rows = cut(XA0 + KH * XL, 2 * NS * FB * 2 * KF // P, P)
        up = cut(0, 2, UL)
        cv = cut(2 * UL, 3, CL)
        F0 = 2 * UL + 3 * CL
        stash = cut(F0, (FB + NS * FB), 2 * KF)
        stash_rows = cut(F0 + (FB + NS * FB) * 2 * KF, 7, P)
        F1 = F0 + (FB + NS * FB) * 2 * KF + 7 * P
        xg = cut(F1, 2, T)
        y_rows = cut(F1 + 2 * T, RT, D)
        V = cut(0, KD, T)
        U = cut(KD * T, KD, T)
        gate_w_rows = cut(KD * T, KD, P)
        v_rows = [cut(2 * KD * T + i * RT * P, RT, P) for i in range(2)]
        G0 = 2 * KD * T + 2 * RT * P
        gate_w_T = cut(G0, KD, P)
        gate_b = cut(G0 + KD * P, KD, P)
        rstd_v = cut(G0 + 2 * KD * P, T)
        block_w = state_T[0:SM, 0, :, :].rearrange("p a b -> p (a b)")[:, 0:KD * SM].rearrange("p (h i) -> p h i", h=KD)

        PS = ctx.enter_context(nc.psum_tensor("psum", [P, 8, PSUM_BANK], F32))
        acc = lambda slot: PS[:, 2 * slot:2 * slot + 2, 0:HALF]
        S0, S1, M0, M1 = 4, 5, 6, 7
        halves = lambda v: v.rearrange("p (a t) -> p a t", a=2)
        smp = lambda v, n=DS: v.rearrange("p (s t) -> p s t", t=n)

        ld_x = [sem(f"ld_x{q}") for q in range(KD // 2)]
        ld_p0, ld_par, ld_pw = sem("ld_p0"), sem("ld_par"), sem("ld_pool_w")
        ld_cs, ld_fs, ld_gw, ld_gb = sem("ld_conv_state"), sem("ld_ffn_state"), sem("ld_gate_w"), sem("ld_gate_b")
        raw_ready = [sem("raw_ready0"), sem("raw_ready1")]
        hi_ready, lo_ready, unit_done, acc_free = sem("w_hi_ready"), sem("w_lo_ready"), sem("unit_done"), sem("acc_free")
        const_ready, ident_ready, corr_ready = sem("const_ready"), sem("ident_ready"), sem("corr_ready")
        p0_T, p0_ready, xs_ready, xT = sem("p0_T"), sem("p0_ready"), sem("xs_ready"), sem("x_T")
        setup_T, setup_ready = sem("setup_T"), sem("setup_ready")
        x_ready, xh_ready, xl_ready = sem("x_ready"), sem("xh_ready"), sem("xl_ready")
        sq_ready, sq_added = sem("sq_ready"), sem("sq_added")
        var_mm, std_ready, rinv_ready, diag_ready = sem("var_mm"), sem("std_ready"), sem("rinv_ready"), sem("diag_ready")
        bc_mm, rstd_ready = sem("bc_mm"), sem("rstd_ready")
        sig_ready, glu_ready = sem("sig_ready"), sem("glu_ready")
        conv_step, pads_zero = sem("conv_step"), sem("pads_zero")
        tap_w_ready, conv_mm, conv_whole = sem("tap_w_ready"), sem("conv_mm"), sem("conv_whole")
        new_packed = sem("new_packed")
        win_step, d_ready = sem("win_step"), sem("d_ready")
        pool_mm, hh_ready, h_lo_ready = sem("pool_mm"), sem("hh_ready"), sem("h_lo_ready")
        ya_read, ya_hi, ya_ready = sem("ya_read"), sem("ya_hi"), sem("ya_ready")
        mean_mm, cent_ready = sem("mean_mm"), sem("cent_ready")
        csq_ready, csq_used = sem("csq_ready"), sem("csq_used")
        cn_ready, cs_ready = sem("cn_ready"), sem("cs_ready")
        so_T, so_rows, st_out = sem("state_out_T"), sem("state_out_rows"), sem("st_out")
        fs_T, fs_ready = sem("ffn_state_T_mm"), sem("ffn_state_ready")
        tap0_ready, tap1_ready, tap_ready = sem("tap0_ready"), sem("tap1_ready"), sem("tap_ready")
        silu_ready, h_ready, pad_ready, stash_ready = sem("silu_ready"), sem("h_ready"), sem("pad_ready"), sem("stash_ready")
        stash_T, stash_rows_ready, st_ffn = sem("stash_T"), sem("stash_rows_ready"), sem("st_ffn")
        gw_T, gw_copied, gw_ready = sem("gate_w_T_mm"), sem("gate_w_copied"), sem("gate_w_ready")
        bw_zero, bw_ready = sem("block_w_zero"), sem("block_w_ready")
        vsum = sem("vsum")
        vsq_ready, vsq_added = sem("vsq_ready"), sem("vsq_added")
        vn_ready, va_ready, v_T = sem("vn_ready"), sem("va_ready"), sem("v_T")
        vrow_ready, st_v, z_mm, zb_ready = sem("vrow_ready"), [sem("st_v0"), sem("st_v1")], sem("z_mm"), sem("zb_ready")
        uz_ready = sem("uz_ready")
        y_row_done = sem("y_row_done")
        xg_ready, y_T, yrow_ready, y_scaled, st_y = sem("xg_ready"), sem("y_T"), sem("yrow_ready"), sem("y_scaled"), sem("st_y")
        st_state = sem("st_state")

        block = ctx.enter_context(nc.Block())

        def sums(r):
            return r if r < 2 else r - 1

        def pcol(name, i):
            if isinstance(i, int):
                return par[:, PC[name] + i:PC[name] + i + 1]
            return par[:, bass.ds(i + PC[name], 1)]

        @block.sync
        def _(sp):
            for q in range(KD // 2):
                cols = slice(2 * q * P, 2 * (q + 1) * P)
                sp.dma_start(x_rows[0:SM, CH, cols], xs_rows[:, cols]).then_inc(ld_x[q], 16)
                sp.dma_start(x_rows[:, 0:CH, cols], xp_rows[:, :, cols]).then_inc(ld_x[q], 16)

            def load(slot, u, src, nk):
                if not isinstance(u, int) or u >= 2:
                    sp.wait_ge(lo_ready, u - 1)
                sp.dma_start(w_raw[slot][:, 0:nk * P].rearrange("p (k n) -> p k n", k=nk), src)\
                    .then_inc(raw_ready[slot], 16)

            def col(w, t):
                v = wblocks(w)
                return v[:, :, t * P:(t + 1) * P] if isinstance(t, int) else v[:, :, bass.ds(t * P, P)]

            def load_rows(u0, n, w, t0=0):
                with sp.Fori(0, n // 2) as i:
                    for j in range(2):
                        load(j, i * 2 + (u0 + j), col(w, i * 2 + (t0 + j)), w.shape[0] // P)

            for u in range(N_IN0):
                load(u % 2, U_IN0 + u, col(w_in_ab[0], IN0[u]), KD)
                if u == 1:
                    for b in range(2):
                        sp.dma_start(conv_rows[0:4 * CB, b, :],
                                     state_conv[0, 4 * b:4 * b + 4].rearrange("s r d -> (s r) d")).then_inc(ld_cs, 16)
            load_rows(U_OUT0, KD, w_out_ab[0, 0:DH])
            load_rows(U_OUT0 + KD, 4, w_out_ab[0, DH:D])
            sp.wait_ge(conv_whole, KH)
            sp.wait_ge(so_T, 2)
            sp.dma_start(state_rows, state_ffn.rearrange("l s r (t p) -> (l s r t) p", p=P)
                         .rearrange("(b q) p -> q b p", q=P)).then_inc(ld_fs, 16)
            load_rows(U_OUT0 + KD + 4, 4, w_out_ab[0, DH:D], 4)
            for layer in range(2):
                if layer == 1:
                    load_rows(U_IN1, KD, w_in_c[0], KD)
                    load_rows(U_IN1 + KD, KD, w_in_c[0])
                    load_rows(U_OUT1, KD, w_out_c[0])
                for (t0, n), ub in zip(GROUPS, U_GROUP):
                    u0 = U_FFN[layer] + ub
                    with sp.Fori(0, n) as i:
                        for j in range(2):
                            load(j, i * 2 + (u0 + j), col(w_up[layer], i + (t0 + j * KF)), KD)
                    load_rows(u0 + 2 * n, KD, w_down[layer, t0 * P:(t0 + n) * P])
            for n, r in enumerate((0, 2, CH)):
                sp.wait_ge(y_row_done, n + 1)
                if r < CH:
                    sp.dma_start(yp_rows[:, r, :], y_rows[:, r, :]).then_inc(st_y, 16)
                else:
                    sp.dma_start(ys_rows, y_rows[P - SM:P, CH, :]).then_inc(st_y, 16)
            sp.wait_ge(st_state, 16 * 2)
            sp.wait_ge(st_out, 16 * 4)
            sp.wait_ge(st_ffn, 16 * 6)
            sp.wait_ge(st_v[0], 16 * KD)
            sp.wait_ge(st_v[1], 16 * KD)
            sp.wait_ge(st_y, 16 * RT)

        @block.tensor
        def _(pe):
            def products(q, k, r_at, nk, rh, rl, first, final):
                for n, (w, r) in enumerate(((w_hi, rh), (w_hi, rl), (w_lo, rh))):
                    for half in range(2):
                        last = nc.tensor.matmul(PS[:, 2 * (q % 2) + half, 0:HALF], w[q][:, k * P:(k + 1) * P],
                                                r[:, r_at, half * HALF:(half + 1) * HALF],
                                                start=(first and n == 0), stop=(final and n == 2))
                return last

            def weights(u):
                pe.wait_ge(lo_ready, u + 1)
                if not isinstance(u, int) or u >= 2:
                    pe.wait_ge(acc_free, u - 1)

            def unit(q, u, nk, rh, rl, ready=None, base=0, middle=None, r0=0, order=None):
                weights(u)
                order = order or range(nk)
                for at, k in enumerate(order):
                    if ready is not None:
                        pe.wait_ge(ready, base + at + 1)
                    last = products(q, k, r0 + k, nk, rh, rl, at == 0, at == nk - 1)
                    if middle is not None and at == nk // 2:
                        middle()
                last.then_inc(unit_done, 1)

            def two_units(u, nk, rh, rl, ready, base):
                for q in range(2):
                    weights(u + q)
                    for k in range(nk - 1):
                        if q == 0:
                            pe.wait_ge(ready, base + k + 1)
                        products((u + q) % 4, k, k, nk, rh, rl, k == 0, False)
                pe.wait_ge(ready, base + nk)
                for q in range(2):
                    products((u + q) % 4, nk - 1, nk - 1, nk, rh, rl, False, True).then_inc(unit_done, 1)

            def row_sums(src, first=True, final=True):
                for r in range(RT):
                    lo = r * P if r < CH else T - P
                    last = nc.tensor.matmul(PS[:, S0, r:r + 1], src[:, lo:lo + P], ones[:, 0:1],
                                            start=(first and r == 0), stop=(final and r == RT - 1),
                                            skip_group_check=True)
                return last

            def spread(r):
                pe.wait_ge(diag_ready, r + 1)
                nc.tensor.matmul(PS[:, M0, 0:PR], ones[:, :], diag[:, 0:CH, :], start=True, stop=True)
                nc.tensor.matmul(PS[:, M1, 0:SM], ones[:, :], diag[:, CH, P - SM:P], start=True, stop=True)\
                    .then_inc(bc_mm, 1)

            def norm_sums(n, r):
                pe.wait_ge(sq_added, (KD - 1) * (n + 1))
                row_sums(sqacc).then_inc(var_mm, 1)

            pe.wait_ge(ident_ready, 1)
            pe.wait_ge(ld_p0, 16 * len(rows0))
            nc.tensor.transpose(PS[:, M1, 0:NP0], par_rows[0:NP0, 0, :], ident[0:NP0, 0:NP0]).then_inc(p0_T, 1)
            for k in range(KD):
                b = 2 * (k % 4)
                pe.wait_ge(ld_x[k // 2], 32)
                if b + 1 == M1:
                    pe.wait_ge(p0_ready, 1)
                if k >= 4:
                    pe.wait_ge(x_ready, k - 3)
                    pe.wait_ge(xs_ready, k - 3)
                for r in range(CH):
                    nc.tensor.transpose(PS[:, b, r * P:(r + 1) * P], x_rows[:, r, k * P:(k + 1) * P], ident[:, :])
                nc.tensor.transpose(PS[:, b + 1, 0:SM], x_rows[0:SM, CH, k * P:(k + 1) * P], ident[0:SM, 0:SM])\
                    .then_inc(xT, 1)

            pe.wait_ge(x_ready, KD)
            pe.wait_ge(xs_ready, KD)
            unit(0, U_IN0, KD, xh, xl, xl_ready, 0)
            pe.wait_ge(ld_par, 16 * 6)
            at = 0
            for b, n in ((1, TAPS * KH), (2, FBLK), (3, FBLK), (4, FBLK), (5, FBLK)):
                last = nc.tensor.transpose(PS[:, S0, at:at + n], par_rows[0:n, b, :], ident[0:n, 0:n])
                at += n
            last.then_inc(setup_T, 1)
            for c in range(KH):
                last = nc.tensor.transpose(PS[:, S1, c * NS * PB:(c + 1) * NS * PB],
                                           pool_rows[0:NS * PB, c * P:(c + 1) * P], ident[0:NS * PB, 0:NS * PB])
            last.then_inc(setup_T, 1)
            pe.wait_ge(ld_cs, 32)
            for b in range(2):
                for c in range(KH):
                    last = nc.tensor.transpose(PS[:, M0 + b, c * 4 * CB:(c + 1) * 4 * CB],
                                               conv_rows[0:4 * CB, b, c * P:(c + 1) * P],
                                               ident[0:4 * CB, 0:4 * CB])
                last.then_inc(setup_T, 1)
            pe.wait_ge(setup_ready, 1)
            norm_sums(0, 0)

            def middle0():
                pe.wait_ge(setup_ready, 4)
                spread(0)
            unit(1, U_IN0 + 1, KD, xh, xl, middle=middle0)
            def conv_taps(c):
                pe.wait_ge(glu_ready, 2 * c + 2)
                if c:
                    pe.wait_ge(conv_whole, c)
                for n in range(PE_TAPS):
                    k = V_TAPS + n
                    pe.wait_ge(tap_w_ready, PE_TAPS * c + n + 1)
                    nc.tensor.matmul(PS[:, S0, 0:PR], tap_w[:, n, :], glu[:, c, k:k + PR],
                                     start=(n == 0), stop=(n == PE_TAPS - 1))
                    last = nc.tensor.matmul(PS[:, S1, 0:SM], tap_w[:, n, :],
                                            smp(glu[:, c, CB + PR:GL], CB + DS)[:, :, k:k + DS],
                                            start=(n == 0), stop=(n == PE_TAPS - 1))
                last.then_inc(conv_mm, 1)

            def pool_map(n):
                pe.wait_ge(d_ready, n + 1)
                if n == 0:
                    pe.wait_ge(ld_pw, 16)
                    pe.wait_ge(rstd_ready, 1)
                else:
                    pe.wait_ge(ya_read, n)
                for half in range(2):
                    last = nc.tensor.matmul(PS[:, M0 + half, 0:HALF], poolw[:, POOL_ORDER[n], :],
                                            d_t[n][:, half * HALF:(half + 1) * HALF], start=True, stop=True)
                last.then_inc(pool_mm, 1)

            def conv_mean(c):
                for half in range(2):
                    last = nc.tensor.matmul(PS[:, M0 + half, 0:HALF], ones[:, :],
                                            conv_o[:, c, half * HALF:(half + 1) * HALF],
                                            start=(c == 0), stop=(c == KH - 1))
                return last

            def in_units(*us):
                for u in us:
                    unit(u % 4, U_IN0 + u, KD, xh, xl)

            in_units(2, 3)
            conv_taps(0)
            in_units(4, 5, 6, 7)
            conv_taps(1)
            in_units(8, 9)
            pool_map(0)
            conv_taps(2)
            in_units(10)
            pool_map(1)
            in_units(11)
            pool_map(2)
            conv_taps(3)
            pool_map(3)
            pe.wait_ge(ya_read, KH)
            for c in range(KH - 1):
                pe.wait_ge(conv_whole, c + 1)
                conv_mean(c)

            def ya_unit(m):
                unit(m % 4, U_OUT0 + m, KH, hh, hl, ya_ready if m == 0 else None, 0, order=POOL_ORDER)

            ya_unit(0)
            ya_unit(1)
            pe.wait_ge(conv_whole, KH)
            conv_mean(KH - 1).then_inc(mean_mm, 1)
            ya_unit(2)
            ya_unit(3)
            for c in range(KH):
                pe.wait_ge(csq_ready, c + 1)
                row_sums(sq[:, c % 2, :], first=(c == 0), final=(c == KH - 1)).then_inc(csq_used, 1)
            pe.wait_ge(cent_ready, KH)
            for g in range(KH):
                nc.tensor.transpose(PS[0:PB, M0, g * P:(g + 1) * P], xa[:, g, PR:PR + PB], ident[:, :])
            pe.wait_ge(new_packed, KH)
            for g in range(KH):
                last = nc.tensor.transpose(PS[0:SM, M1, g * P:(g + 1) * P], new_x[:, g, :], ident[:, :])
            last.then_inc(so_T, 1)
            ya_unit(4)
            ya_unit(5)
            pe.wait_ge(so_rows, 2)
            spread(1)
            ya_unit(6)
            ya_unit(7)

            def yb_unit(m):
                unit(m % 4, U_OUT0 + KD + m, KH, hh, hl, h_lo_ready if m == 0 else None, 0, r0=KH)

            yb_unit(0)
            pe.wait_ge(rstd_ready, 2)
            for c in range(KH):
                nc.tensor.transpose(PS[0:CB, M0, c * P:(c + 1) * P], glu[:, c, PR:PR + CB], ident[:, :])
            pe.wait_ge(new_packed, KH + 1)
            for c in range(KH):
                last = nc.tensor.transpose(PS[0:SM, M1, c * P:(c + 1) * P], new_glu[:, c, :], ident[:, :])
            last.then_inc(so_T, 1)
            for m in range(1, 6):
                yb_unit(m)
            nb = 2 * NS * FB * 2 * KF // P
            pe.wait_ge(so_rows, 4)
            pe.wait_ge(ld_fs, 16)
            for b in range(nb):
                bank, c = (M0, M1, S1)[b // 4], b % 4
                last = nc.tensor.transpose(PS[:, bank, c * P:(c + 1) * P], state_rows[:, b, :], ident[:, :])
            last.then_inc(fs_T, 1)
            yb_unit(6)
            yb_unit(7)

            def plain_units(u0, nk, rh, rl, n):
                with pe.Fori(0, n // 4) as i:
                    for q in range(4):
                        unit(q, i * 4 + (u0 + q), nk, rh, rl)

            def ffn(layer):
                n = 2 * layer + 1
                r = (2, 5)[layer]
                for g, ((t0, nt), ub) in enumerate(zip(GROUPS, U_GROUP)):
                    u0 = U_FFN[layer] + ub
                    last_group = g == len(GROUPS) - 1
                    if g == 0:
                        unit(0, u0, KD, xh, xl, xl_ready, KD * n)
                        norm_sums(n, r)

                        def middle():
                            if layer == 0:
                                pe.wait_ge(fs_ready, 3)
                            else:
                                pe.wait_ge(vrow_ready, 2 * KD)
                            spread(r)
                        unit(1, u0 + 1, KD, xh, xl, middle=middle)
                        unit(2, u0 + 2, KD, xh, xl)
                        unit(3, u0 + 3, KD, xh, xl)
                        plain_units(u0 + 4, KD, xh, xl, 2 * nt - 4)
                    else:
                        plain_units(u0, KD, xh, xl, 2 * nt)
                    ud = u0 + 2 * nt
                    two_units(ud, nt, hh, hl, h_lo_ready, H_FFN[layer] + t0)
                    if last_group:
                        pe.wait_ge(stash_ready, 2 * 2 * KF * (layer + 1))
                        flat_stash = stash.rearrange("p a b -> p (a b)")
                        at = 0
                        for b in range(7):
                            n_ = FB * 2 * KF if b == 0 else min(P, (FB + NS * FB) * 2 * KF - at)
                            last = nc.tensor.transpose(PS[0:n_, (M0, M1)[b // 4], (b % 4) * P:(b % 4 + 1) * P],
                                                       flat_stash[:, at:at + n_], ident[:, :])
                            at += n_
                        last.then_inc(stash_T, 1)
                    if not last_group or layer == 0:
                        unit(2, ud + 2, nt, hh, hl)
                        unit(3, ud + 3, nt, hh, hl)
                        for q in range(4):
                            unit(q, ud + 4 + q, nt, hh, hl)

            def out_rows(j, m):
                pe.wait_ge(xg_ready, m + 1)
                if isinstance(m, int) and m == 0:
                    pe.wait_ge(stash_rows_ready, 4)
                else:
                    pe.wait_ge(yrow_ready, m * 2)
                for r in range(CH):
                    nc.tensor.transpose(PS[:, M0, r * P:(r + 1) * P], xg[:, j, r * P:(r + 1) * P], ident[:, :])
                nc.tensor.transpose(PS[:, M1, 0:P], xg[:, j, T - P:T], ident[:, :]).then_inc(y_T, 1)

            ffn(0)

            unit(0, U_IN1, KD, xh, xl, xl_ready, KD * 2)
            norm_sums(2, 3)

            def middle1():
                pe.wait_ge(stash_rows_ready, 2)
                spread(3)
            unit(1, U_IN1 + 1, KD, xh, xl, middle=middle1)
            pe.wait_ge(ld_gw, 16)
            pe.wait_ge(rstd_ready, 4)
            for h in range(KD):
                last = nc.tensor.transpose(PS[:, M0 + h // 4, (h % 4) * P:(h % 4 + 1) * P], gate_w_rows[:, h, :],
                                           ident[:, :])
            last.then_inc(gw_T, 1)
            unit(2, U_IN1 + 2, KD, xh, xl)
            unit(3, U_IN1 + 3, KD, xh, xl)
            plain_units(U_IN1 + 4, KD, xh, xl, KD - 4)

            def v_turn(m):
                pe.wait_ge(va_ready, m + 1)
                if m == 0:
                    pe.wait_ge(rstd_ready, 5)
                else:
                    pe.wait_ge(vrow_ready, 2 * m)
                for r in range(CH):
                    nc.tensor.transpose(PS[:, M0, r * P:(r + 1) * P], V[:, m, r * P:(r + 1) * P], ident[:, :])
                nc.tensor.transpose(PS[0:SM, M1, 0:P], V[:, m, PR:T], ident[:, :]).then_inc(v_T, 1)

            def gate(m):
                pe.wait_ge(vrow_ready, 2 * m + 2)
                if m == 0:
                    pe.wait_ge(gw_ready, 1)
                    pe.wait_ge(bw_ready, 16 * NS)
                    pe.wait_ge(std_ready, 5)
                else:
                    pe.wait_ge(zb_ready, 2 * m)
                for c in range(CH):
                    nc.tensor.matmul(PS[:, S0, c * P:(c + 1) * P], v_rows[m % 2][:, c, :], gate_w_T[:, m, :],
                                     start=True, stop=True)
                nc.tensor.matmul(PS[:, S1, 0:SM], v_rows[m % 2][0:SM, CH, :], block_w[:, m, :],
                                 start=True, stop=True).then_inc(z_mm, 1)

            u0 = U_IN1 + KD
            unit(0, u0, KD, xh, xl)
            pe.wait_ge(vsum, KD - 1)
            for half in range(2):
                last = nc.tensor.matmul(PS[:, S0 + half, 0:HALF], ones[:, :], sq[:, 0, half * HALF:(half + 1) * HALF],
                                        start=True, stop=True)
            last.then_inc(mean_mm, 1)
            unit(1, u0 + 1, KD, xh, xl)
            unit(2, u0 + 2, KD, xh, xl)
            pe.wait_ge(vsq_added, KD - 1)
            pe.wait_ge(cent_ready, KH + KD)
            row_sums(sqacc).then_inc(var_mm, 1)
            unit(3, u0 + 3, KD, xh, xl, middle=lambda: spread(4))
            unit(0, u0 + 4, KD, xh, xl)
            v_turn(0)
            unit(1, u0 + 5, KD, xh, xl)
            v_turn(1)
            gate(0)
            unit(2, u0 + 6, KD, xh, xl)
            v_turn(2)
            gate(1)
            unit(3, u0 + 7, KD, xh, xl)
            for m in range(3, KD):
                v_turn(m)
                gate(m - 1)
            gate(KD - 1)

            two_units(U_OUT1, KD, hh, hl, h_lo_ready, H_MIX[1])
            unit(2, U_OUT1 + 2, KD, hh, hl)
            unit(3, U_OUT1 + 3, KD, hh, hl)
            plain_units(U_OUT1 + 4, KD, hh, hl, KD - 4)

            ffn(1)
            ud = N_UNITS - KD
            nt = GROUPS[-1][1]
            for m in range(2, KD):
                out_rows(m % 2, m - 2)
                unit(m % 4, ud + m, nt, hh, hl)
            out_rows(0, KD - 2)
            out_rows(1, KD - 1)
            norm_sums(4, 6)

        @block.scalar
        def _(act):
            at = 0
            for name, ap, n in rows0:
                act.dma_start(par_rows[at:at + n, 0, :], flat(ap)).then_inc(ld_p0, 16)
                at += n
            act.dma_start(par_rows[0:TAPS * KH, 1, :], conv_w.rearrange("l k (t p) -> (l k t) p", p=P)).then_inc(ld_par, 16)
            cw = ffn_conv_w.rearrange("l k (t p) -> (l k t) p", p=P)
            for b in range(3):
                n = FBLK
                act.dma_start(par_rows[0:n, 2 + b, :], cw[b * n:(b + 1) * n, :]).then_inc(ld_par, 16)
            act.dma_start(par_rows[0:FBLK, 5, :], flat(ffn_conv_b)).then_inc(ld_par, 16)
            act.dma_start(pool_rows[0:NS * PB, :], state_pool.rearrange("l s r d -> (l s r) d")).then_inc(ld_par, 16)
            act.dma_start(poolw[:, :, :], pool_w[0].rearrange("g i o -> i g o")).then_inc(ld_pw, 16)
            act.dma_start(pool_sample[0, :, 0:PB - DS, :], state_pool[0, :, DS:PB, :]).then_inc(st_state, 16)
            act.dma_start(conv_sample[0, :, 0:CB - DS, :], state_conv[0, :, DS:CB, :]).then_inc(st_state, 16)

            def split(slot, u, pair, nk):
                act.wait_ge(raw_ready[slot % 2], (pair + 1) * 16)
                if not isinstance(u, int) or u >= 4:
                    act.wait_ge(unit_done, u - 3)
                nc.scalar.activation(w_hi[slot][:, 0:nk * P], w_raw[slot % 2][:, 0:nk * P], ACT.Copy).then_inc(hi_ready, 1)

            def split_n(u):
                if u < N_UNITS:
                    split(u % 4, u, u // 2, tiles_of(u))

            def norm_in(n, m, r, gname, gi):
                gain_hi(n, m, gname, gi)
                square(n, m, r)

            def gain_hi(n, m, gname, gi):
                act.wait_ge(*((x_ready, m + 1) if n == 0 else (acc_free, X_FINAL[n] + m + 1)))
                nc.scalar.activation(xh[:, m, :], X[:, m, :], ACT.Identity, bias=0.0,
                                     scale=pcol(gname, gi)).then_inc(xh_ready, 1)

            def square(n, m, r):
                if m == 0:
                    if r:
                        act.wait_ge(var_mm, sums(r))
                        act.wait_ge(bc_mm, r)
                elif m >= 3:
                    act.wait_ge(sq_added, (KD - 1) * n + m - 2)
                dst = sqacc[:, :] if m == 0 else sq[:, m % 2, :]
                nc.scalar.activation(dst, X[:, m, :], ACT.Square).then_inc(sq_ready, 1)

            def root(r, width):
                act.wait_ge(var_mm, sums(r + 1))
                nc.scalar.activation(std[:, :], PS[:, S0, 0:RT], ACT.Sqrt, bias=eps[:, 0:1],
                                     scale=1.0 / width).then_inc(std_ready, 1)

            def take_rstd(r, dst):
                act.wait_ge(bc_mm, r + 1)
                nc.scalar.activation(dst[:, 0:PR], PS[:, M0, 0:PR], ACT.Copy)
                nc.scalar.activation(dst[:, PR:T], PS[:, M1, 0:SM], ACT.Copy).then_inc(rstd_ready, 1)

            act.wait_ge(p0_T, 1)
            nc.scalar.activation(par[:, 0:NP0], PS[:, M1, 0:NP0], ACT.Copy).then_inc(p0_ready, 1)
            act.wait_ge(p0_ready, 1)
            for m in range(KD):
                act.wait_ge(xT, m + 1)
                nc.scalar.activation(X[:, m, PR:T], PS[:, 2 * (m % 4) + 1, 0:SM], ACT.Copy).then_inc(xs_ready, 1)
                act.wait_ge(xs_ready, m + 1)
                gain_hi(0, m, "mix_norm", m)
                if m in (0, 4):
                    split_n(m // 4)
            for m in range(KD):
                square(0, m, 0)
                if m == 4:
                    split_n(2)
            act.wait_ge(setup_T, 1)
            nc.scalar.activation(par[:, NP0:NPAR], PS[:, S0, 0:NPAR - NP0], ACT.Copy).then_inc(setup_ready, 1)
            act.wait_ge(setup_T, 2)
            for c in range(KH):
                last = nc.scalar.activation(
                    smp(xa[:, c, PB + PR:XL], PB + DS)[:, :, 0:PB],
                    smp(PS[:, S1, c * NS * PB:(c + 1) * NS * PB], PB), ACT.Copy)
            last.then_inc(setup_ready, 1)
            for b in range(2):
                act.wait_ge(setup_T, 3 + b)
                for c in range(KH):
                    last = nc.scalar.activation(
                        smp(glu[:, c, CB + PR:GL], CB + DS)[:, 4 * b:4 * b + 4, 0:CB],
                        smp(PS[:, M0 + b, c * 4 * CB:(c + 1) * 4 * CB], CB), ACT.Copy)
                last.then_inc(setup_ready, 1)
            root(0, D)
            split_n(3)
            take_rstd(0, rstd)

            def diagonals(c):
                if c:
                    act.wait_ge(conv_mm, c)
                else:
                    act.wait_ge(setup_ready, 1)
                for n in range(PE_TAPS):
                    nc.scalar.activation(tap_w[:, n, :], ident[:, :], ACT.Copy,
                                         scale=pcol("conv_w", (V_TAPS + n) * KH + c)).then_inc(tap_w_ready, 1)

            def sigmoid(p):
                act.wait_ge(acc_free, PAIR_UNIT[p] + 2)
                gate_t = ag[:, 2 * (p % 2) + 1, :]
                nc.scalar.activation(gate_t, gate_t, ACT.Sigmoid).then_inc(sig_ready, 1)

            def pool_hi(n):
                g = POOL_ORDER[n]
                act.wait_ge(pool_mm, n + 1)
                nc.scalar.activation(halves(d_t[n]), PS[:, M0:M1 + 1, 0:HALF], ACT.Identity, bias=0.0,
                                     scale=pcol("pool_scale", g)).then_inc(ya_read, 1)
                act.wait_ge(ya_read, n + 1)
                nc.scalar.activation(hh[:, g, :], d_t[n], ACT.Copy).then_inc(ya_hi, 1)

            diagonals(0)
            for u in range(1, N_IN0):
                split_n(u + 3)
                if u == 1:
                    sigmoid(0)
                if u == 3:
                    sigmoid(1)
                if u == 4:
                    diagonals(1)
                if u == 5:
                    sigmoid(2)
                if u == 8:
                    diagonals(2)
                if u == 9:
                    sigmoid(3)
                if u == 10:
                    pool_hi(0)
                    diagonals(3)
                if u == 11:
                    pool_hi(1)
            pool_hi(2)
            split_n(U_OUT0 + 3)
            pool_hi(3)

            def state_rows_out(first, bank, n, dst_rows, dst):
                nc.scalar.activation(dst_rows[0:n, :], PS[0:n, bank, :], ACT.Copy).then_inc(so_rows, 1)
                act.wait_ge(so_rows, first)
                act.dma_start(dst, dst_rows[0:n, :]).then_inc(st_out, 16)

            def conv_square(c):
                act.wait_ge(cent_ready, c + 1)
                if c == 0:
                    act.wait_ge(ya_ready, KH)
                if c >= 2:
                    act.wait_ge(csq_used, c - 1)
                nc.scalar.activation(sq[:, c % 2, :], conv_o[:, c, :], ACT.Square).then_inc(csq_ready, 1)

            for m in range(1, KD):
                split_n(U_OUT0 + m + 3)
                if m == 2:
                    conv_square(0)
                    conv_square(1)
                if m == 3:
                    conv_square(2)
                    conv_square(3)
                if m == 4:
                    act.wait_ge(csq_used, KH)
                    nc.scalar.activation(std[:, :], PS[:, S0, 0:RT], ACT.Sqrt, bias=eps[:, 0:1],
                                         scale=1.0 / DH).then_inc(std_ready, 1)
                    act.wait_ge(so_T, 1)
                    state_rows_out(1, M0, PB, out_rows0[2], pool_prompt[0, 0])
                    state_rows_out(2, M1, SM, out_rows0[3], pool_sample[0, :, PB - DS:PB, :])
                if m == 6:
                    take_rstd(1, rstd)
                    for c in range(KH):
                        act.wait_ge(cn_ready, c + 1)
                        nc.scalar.activation(conv_o[:, c, :], conv_o[:, c, :], ACT.Silu, bias=pcol("conv_norm_b", c),
                                             scale=pcol("conv_norm_g", c)).then_inc(cs_ready, 1)
                        act.wait_ge(cs_ready, c + 1)
                        nc.scalar.activation(hh[:, KH + c, :], conv_o[:, c, :], ACT.Copy).then_inc(hh_ready, 1)
            for m in range(KD):
                split_n(U_OUT0 + KD + m + 3)
                if m == 0:
                    act.wait_ge(so_T, 2)
                    state_rows_out(3, M0, CB, out_rows0[0], conv_prompt[0, 0])
                    state_rows_out(4, M1, SM, out_rows0[1], conv_sample[0, :, CB - DS:CB, :])
                if m == 6:
                    act.wait_ge(fs_T, 1)
                    st = state_T[:, :, :, :].rearrange("p l a b -> p (l a b)")
                    for b, (bank, n) in enumerate(((M0, 4 * P), (M1, 4 * P), (S1, 3 * P))):
                        nc.scalar.activation(st[:, b * 4 * P:b * 4 * P + n], PS[:, bank, 0:n], ACT.Copy)\
                            .then_inc(fs_ready, 1)
                norm_in(1, m, 2, "ffn_norm", m)

            def ffn(layer):
                n = 2 * layer + 1
                r = (2, 5)[layer]
                for g, ((t0, nt), ub) in enumerate(zip(GROUPS, U_GROUP)):
                    u0 = U_FFN[layer] + ub
                    c0 = layer * KF + t0

                    def product_hi(i):
                        act.wait_ge(h_ready, i + (c0 + 1))
                        dst = hh[:, i, :] if isinstance(i, int) else \
                            hh[:, bass.ds(i, 1), :].rearrange("p a t -> p (a t)")
                        nc.scalar.activation(dst[:, 0:PR], cv[:, 2, 0:PR], ACT.Copy)
                        nc.scalar.activation(smp(dst[:, PR:T]), smp(cv[:, 2, PR:PR + NS * (FB + DS)], FB + DS)[:, :, FB:],
                                             ACT.Copy).then_inc(hh_ready, 1)

                    def step(i, ahead, before=None, start=False):
                        for j in range(2):
                            ahead(j)
                            if start and j == 0:
                                root(r, D)
                                take_rstd(r, rstd)
                            if j == 0 and before is not None:
                                product_hi(before)
                            act.wait_ge(acc_free, i * 2 + (u0 + j + 1))
                            act.wait_ge(pad_ready, (i + c0) * 2 + (j + 1))
                            ti = i + (t0 + j * KF)
                            nc.scalar.activation(cv[:, j, :], up[:, j, 0:CL], ACT.Identity,
                                                 bias=pcol("ffn_conv_b", ti + layer * 2 * KF),
                                                 scale=pcol("ffn_conv_w", ti + layer * FK * 2 * KF)).then_inc(tap0_ready, 1)
                            if j == 0:
                                act.wait_ge(tap_ready, (i + c0) * 2 + 1)
                                nc.scalar.activation(cv[:, 0, :], cv[:, 0, :], ACT.Silu).then_inc(silu_ready, 1)

                    for e in range(2):
                        step(e, lambda j: split_n(u0 + 2 * e + j + 3), e - 1 if e else None, start=(g == 0 and e == 0))
                    more = nt // 2 - 1 if nt == KD else nt // 2 - 2
                    with act.Fori(0, more) as b:
                        for e in range(2):
                            step(b * 2 + (2 + e), lambda j: split((2 * e + j + 3) % 4, b * 4 + (u0 + 4 + 2 * e + j + 3),
                                                                  b * 2 + (u0 + 4 + 2 * e + j + 3) // 2, KD),
                                 b * 2 + (1 + e))
                    for i in range(2 * more + 2, nt):
                        step(i, lambda j: split_n(u0 + 2 * i + j + 3), i - 1)
                    product_hi(nt - 1)
                    ud = u0 + 2 * nt
                    for m in range(KD):
                        split_n(ud + m + 3)
                        if g < len(GROUPS) - 1:
                            continue
                        if m == 2:
                            stash_rows_out(layer)
                        if layer == 0:
                            if m == 4:
                                act.wait_ge(st_ffn, 48)
                                act.wait_ge(h_lo_ready, H_FFN[0] + KF)
                                act.dma_start(gate_w_rows, sgu_w[0].rearrange("h i j -> i h j")).then_inc(ld_gw, 16)
                                act.dma_start(gate_b.rearrange("p h i -> p (h i)"),
                                              sgu_bias.rearrange("l h i -> l (h i)").to_broadcast([P, KD * P]))\
                                    .then_inc(ld_gb, 16)
                            norm_in(2, m, r + 1, "mix_norm", KD + m)
                        else:
                            if m >= 2:
                                take_y(m - 2)
                            act.wait_ge(acc_free, X_FINAL[4] + m + 1)
                            nc.scalar.activation(xg[:, m % 2, :], X[:, m, :], ACT.Identity, bias=0.0,
                                                 scale=pcol("final_norm", m)).then_inc(xg_ready, 1)
                            square(4, m, r + 1)
                for m in range(KD - 2, KD) if layer else ():
                    take_y(m)

            def stash_rows_out(layer):
                act.wait_ge(stash_T, layer + 1)
                sr = stash_rows.rearrange("p a b -> p (a b)")
                np_, ns_ = FB * 2 * KF, NS * FB * 2 * KF
                last_n = ns_ % P
                nc.scalar.activation(sr[0:np_, 0:P], PS[0:np_, M0, 0:P], ACT.Copy)
                nc.scalar.activation(sr[:, P:4 * P], PS[:, M0, P:4 * P], ACT.Copy).then_inc(stash_rows_ready, 1)
                nc.scalar.activation(sr[:, 4 * P:6 * P], PS[:, M1, 0:2 * P], ACT.Copy)
                nc.scalar.activation(sr[0:last_n, 6 * P:7 * P], PS[0:last_n, M1, 2 * P:3 * P], ACT.Copy)\
                    .then_inc(stash_rows_ready, 1)
                act.wait_ge(stash_rows_ready, 2 * layer + 2)
                fp = ffn_prompt[layer].rearrange("b r (t p) -> (b r t) p", p=P)
                fs = ffn_sample[layer].rearrange("s r (t p) -> (s r t) p", p=P)
                act.dma_start(fp, stash_rows[0:np_, 0, :]).then_inc(st_ffn, 16)
                nf = ns_ // P
                act.dma_start(fs[0:nf * P, :].rearrange("(b q) p -> q b p", q=P),
                              stash_rows[:, 1:1 + nf, :]).then_inc(st_ffn, 16)
                act.dma_start(fs[nf * P:ns_, :], stash_rows[0:last_n, 1 + nf, :]).then_inc(st_ffn, 16)

            def take_y(m):
                act.wait_ge(y_T, m + 1)
                nc.scalar.activation(y_rows[:, 0:CH, m * P:(m + 1) * P],
                                     PS[:, M0, :].rearrange("p (r c) -> p r c", r=CH), ACT.Copy).then_inc(yrow_ready, 1)
                nc.scalar.activation(y_rows[P - SM:P, CH, m * P:(m + 1) * P], PS[P - SM:P, M1, 0:P], ACT.Copy)\
                    .then_inc(yrow_ready, 1)

            ffn(0)

            def v_square(m):
                act.wait_ge(cent_ready, KH + m + 1)
                if m == 0:
                    act.wait_ge(bc_mm, 4)
                    act.wait_ge(var_mm, sums(4))
                elif m >= 3:
                    act.wait_ge(vsq_added, m - 2)
                dst = sqacc[:, :] if m == 0 else sq[:, m % 2, :]
                nc.scalar.activation(dst, V[:, m, :], ACT.Square).then_inc(vsq_ready, 1)

            split_n(U_IN1 + 3)
            root(3, D)
            take_rstd(3, rstd)
            split_n(U_IN1 + 4)
            act.wait_ge(gw_T, 1)
            act.wait_ge(ld_gb, 16)
            nc.scalar.activation(gate_w_T[:, 0:4, :], PS[:, M0, :].rearrange("p (h i) -> p h i", h=4), ACT.Copy)
            nc.scalar.activation(gate_w_T[:, 4:8, :], PS[:, M1, :].rearrange("p (h i) -> p h i", h=4), ACT.Copy)\
                .then_inc(gw_copied, 1)
            for m in range(2, KD):
                split_n(U_IN1 + m + 3)
                if m == 5:
                    act.wait_ge(gw_ready, 1)
                    act.wait_ge(bw_zero, 1)
                    for s in range(NS):
                        act.dma_start(block_w[s * DS:(s + 1) * DS, :, s * DS:(s + 1) * DS],
                                      gate_w_T[0:DS, :, 0:DS]).then_inc(bw_ready, 16)

            def v_affine(m):
                act.wait_ge(vn_ready, m + 1)
                nc.scalar.activation(V[:, m, :], V[:, m, :], ACT.Identity, bias=pcol("sgu_norm_b", m),
                                     scale=pcol("sgu_norm_g", m)).then_inc(va_ready, 1)

            def v_take(m):
                act.wait_ge(v_T, m + 1)
                if m >= 2:
                    act.wait_ge(st_v[m % 2], 32 * (m // 2))
                    act.wait_ge(z_mm, m - 1)
                nc.scalar.activation(v_rows[m % 2][:, 0:CH, :], PS[:, M0, :].rearrange("p (r c) -> p r c", r=CH), ACT.Copy)\
                    .then_inc(vrow_ready, 1)
                nc.scalar.activation(v_rows[m % 2][0:SM, CH, :], PS[0:SM, M1, 0:P], ACT.Copy).then_inc(vrow_ready, 1)
                act.wait_ge(vrow_ready, 2 * m + 2)
                act.dma_start(sgu_v_prompt[0, 0, :, m * P:(m + 1) * P], v_rows[m % 2][:, CH - 1, :]).then_inc(st_v[m % 2], 16)
                act.dma_start(sgu_v_sample[0, :, :, m * P:(m + 1) * P].rearrange("s t p -> (s t) p"),
                              v_rows[m % 2][0:SM, CH, :]).then_inc(st_v[m % 2], 16)

            def uz_hi(m):
                act.wait_ge(uz_ready, m + 1)
                nc.scalar.activation(hh[:, m, :], U[:, m, :], ACT.Copy).then_inc(hh_ready, 1)

            uu = U_IN1 + KD
            split_n(uu + 3)
            for m in range(4):
                v_square(m)
            split_n(uu + 4)
            for m in range(4, KD):
                v_square(m)
            split_n(uu + 5)
            root(4, D)
            split_n(uu + 6)
            take_rstd(4, rstd_v)
            for m in range(3):
                v_affine(m)
            split_n(uu + 7)
            v_take(0)
            for m in range(3, KD):
                v_affine(m)
            split_n(uu + 8)
            v_take(1)
            split_n(uu + 9)
            v_take(2)
            uz_hi(0)
            split_n(uu + 10)
            for m in range(3, KD):
                v_take(m)
                uz_hi(m - 2)
            uz_hi(KD - 2)
            uz_hi(KD - 1)
            for m in range(KD):
                split_n(U_OUT1 + m + 3)
                norm_in(3, m, 5, "ffn_norm", KD + m)

            ffn(1)
            root(6, D)
            act.wait_ge(rinv_ready, 7)
            for r in (1, 3):
                nc.scalar.activation(y_rows[:, r, :], y_rows[:, r, :], ACT.Copy, scale=rinv[:, r:r + 1])\
                    .then_inc(y_scaled, 1)
                act.wait_ge(y_scaled, (r + 1) // 2)
                act.dma_start(yp_rows[:, r, :], y_rows[:, r, :]).then_inc(st_y, 16)

        @block.gpsimd
        def _(pool):
            nc.gpsimd.memset(ones[:, :], 1.0).then_inc(const_ready, 1)
            pool.wait_ge(const_ready, 1)
            nc.gpsimd.affine_select(out=ident[:, :], in_=ones[:, :], compare_op=ALU.is_equal, fill=0.0, base=0,
                                    pattern=[[-1, P]], channel_multiplier=1).then_inc(ident_ready, 1)
            nc.gpsimd.memset(eps[:, :], EPS).then_inc(const_ready, 1)
            at = 0
            for w in WINDOWS:
                for j in range(w - 1):
                    nc.gpsimd.memset(corr[:, at:at + 1], w / (j + 1)).then_inc(corr_ready, 1)
                    at += 1

            def split(slot, u, nk):
                pool.wait_ge(hi_ready, u + 1)
                nc.gpsimd.tensor_tensor(w_lo[slot][:, 0:nk * P], w_raw[slot % 2][:, 0:nk * P],
                                        w_hi[slot][:, 0:nk * P].bitcast(F32), ALU.subtract).then_inc(lo_ready, 1)

            def split_n(u):
                if u < N_UNITS:
                    split(u % 4, u, tiles_of(u))

            def add_square(n, m):
                pool.wait_ge(sq_ready, KD * n + m + 1)
                if m > 1:
                    pool.wait_ge(sq_added, (KD - 1) * n + m - 1)
                nc.gpsimd.tensor_tensor(sqacc[:, :], sqacc[:, :], sq[:, m % 2, :], ALU.add).then_inc(sq_added, 1)

            split_n(0)
            split_n(1)
            for m in range(1, KD):
                add_square(0, m)
                if m == 4:
                    split_n(2)
            nc.gpsimd.memset(xa[:, :, 0:PB], 0.0).then_inc(pads_zero, 1)
            nc.gpsimd.memset(glu[:, :, 0:CB], 0.0).then_inc(pads_zero, 1)

            steps = [0]

            def windows(n):
                g = POOL_ORDER[n]
                pool.wait_ge(acc_free, U_IN0 + POOL_UNIT[n] + 1)
                if n == 0:
                    pool.wait_ge(corr_ready, sum(WINDOWS) - len(WINDOWS))
                    pool.wait_ge(setup_ready, 4)
                    pool.wait_ge(bc_mm, 1)
                else:
                    pool.wait_ge(d_ready, n)
                nc.gpsimd.tensor_copy(smp(new_x[:, g, :]), smp(xa[:, g, PB + PR:XL], PB + DS)[:, :, PB:])\
                    .then_inc(new_packed, 1)
                src, lo, width = xa[:, g, :], 0, 1
                for level in range(g + 1):
                    dst = pool_tmp[level % 2]
                    lo += width
                    nc.gpsimd.tensor_tensor(dst[:, lo:XL], src[:, lo:XL], src[:, lo - width:XL - width], ALU.add)\
                        .then_inc(win_step, 1)
                    steps[0] += 1
                    pool.wait_ge(win_step, steps[0])
                    src, width = dst, 2 * width
                w = WINDOWS[g]
                c0 = sum(WINDOWS[:g]) - g
                nc.gpsimd.tensor_tensor(src[:, PB:PB + w - 1], src[:, PB:PB + w - 1], corr[:, c0:c0 + w - 1], ALU.mult)\
                    .then_inc(win_step, 1)
                pool.wait_ge(win_step, steps[0] + 1)
                nc.gpsimd.tensor_scalar(src[:, PB:XL], src[:, PB:XL], 1.0 / w, 1.0, ALU.mult, ALU.mult)\
                    .then_inc(win_step, 1)
                steps[0] += 2
                pool.wait_ge(win_step, steps[0])
                nc.gpsimd.tensor_tensor(d_t[n][:, 0:PR], src[:, PB:PB + PR], xa[:, g, PB:PB + PR], ALU.subtract)
                new = lambda v: smp(v[:, PB + PR:XL], PB + DS)[:, :, PB:]
                nc.gpsimd.tensor_tensor(smp(d_t[n][:, PR:T]), new(src), new(xa[:, g, :]), ALU.subtract)\
                    .then_inc(d_ready, 1)

            def pool_lo(n):
                g = POOL_ORDER[n]
                pool.wait_ge(ya_hi, n + 1)
                nc.gpsimd.tensor_tensor(hl[:, g, :], d_t[n], hh[:, g, :].bitcast(F32), ALU.subtract)\
                    .then_inc(ya_ready, 1)

            for u in range(N_IN0):
                split_n(u + 3)
                if u == 7:
                    windows(0)
                if u == 8:
                    windows(1)
            windows(2)
            windows(3)
            for n in range(3):
                pool_lo(n)
            split_n(U_OUT0 + 3)
            pool_lo(3)
            pool.wait_ge(glu_ready, 2 * KH)
            for c in range(KH):
                last = nc.gpsimd.tensor_copy(smp(new_glu[:, c, :]), smp(glu[:, c, CB + PR:GL], CB + DS)[:, :, CB:])
            last.then_inc(new_packed, 1)
            for m in range(1, 2 * KD):
                split_n(U_OUT0 + m + 3)
                if m > KD:
                    add_square(1, m - KD)
            pool.wait_ge(st_out, 16 * 4)
            pool.wait_ge(xl_ready, 2 * KD)
            nc.gpsimd.memset(up[:, :, 0:FB], 0.0).then_inc(pads_zero, 1)

            def ffn(layer):
                for g, ((t0, nt), ub) in enumerate(zip(GROUPS, U_GROUP)):
                    u0 = U_FFN[layer] + ub
                    c0 = layer * KF + t0
                    so = state_T[:, layer, :, :]

                    def pads(j, i):
                        ti = i + (t0 + j * KF)
                        src = so[:, :, ti:ti + 1] if isinstance(ti, int) else so[:, :, bass.ds(ti, 1)]
                        nc.gpsimd.tensor_copy(smp(up[:, j, FB + PR:UL], FB + DS)[:, :, 0:FB],
                                              src.rearrange("p (s r) o -> p s (r o)", r=FB)).then_inc(pad_ready, 1)

                    def step(i, ahead, start=False):
                        for j in range(2):
                            if start and layer == 0 and j == 0:
                                pool.wait_ge(fs_ready, 3)
                            if not (layer == 0 and start):
                                pool.wait_ge(tap_ready, (i + c0) * 2 + (j - 1))
                            pads(j, i)
                            ahead(j)
                            pool.wait_ge(acc_free, i * 2 + (u0 + j + 1))
                            ti = i + (t0 + j * KF)
                            dst = stash[:, :, ti:ti + 1] if isinstance(ti, int) else stash[:, :, bass.ds(ti, 1)]
                            nc.gpsimd.tensor_copy(dst[:, 0:FB, :].rearrange("p r o -> p (r o)"), up[:, j, PR:PR + FB])\
                                .then_inc(stash_ready, 1)
                            nc.gpsimd.tensor_copy(
                                dst[:, FB:, :].rearrange("p (s r) o -> p s (r o)", r=FB),
                                smp(up[:, j, FB + PR:UL], FB + DS)[:, :, DS:DS + FB]).then_inc(stash_ready, 1)

                    first = 0
                    if g == 0:
                        for e in range(2):
                            step(e, lambda j: split_n(u0 + 2 * e + j + 3), start=(e == 0))
                        first = 1
                    end = nt // 2 if nt == KD else nt // 2 - 1
                    with pool.Fori(first, end) as b:
                        for e in range(2):
                            step(b * 2 + e, lambda j: split((2 * e + j + 3) % 4, b * 4 + (u0 + 2 * e + j + 3), KD))
                    for i in range(2 * end, nt):
                        step(i, lambda j: split_n(u0 + 2 * i + j + 3))
                    ud = u0 + 2 * nt
                    for m in range(KD):
                        split_n(ud + m + 3)
                        if g == len(GROUPS) - 1 and m:
                            add_square(2 * layer + 2, m)

            ffn(0)
            nc.gpsimd.memset(block_w, 0.0).then_inc(bw_zero, 1)
            for m in range(KD):
                split_n(U_IN1 + m + 3)
                if m == 2:
                    pool.wait_ge(gw_copied, 1)
                    nc.gpsimd.affine_select(out=gate_w_T, in_=gate_w_T, compare_op=ALU.is_ge, fill=0.0, base=0,
                                            pattern=[[0, KD], [1, P]], channel_multiplier=-1).then_inc(gw_ready, 1)
                if m == 1:
                    pool.wait_ge(acc_free, U_IN1 + 2)
                    pool.wait_ge(bc_mm, 4)
                    nc.gpsimd.tensor_tensor(sq[:, 0, :], V[:, 0, :], V[:, 1, :], ALU.add).then_inc(vsum, 1)
                elif m > 1:
                    pool.wait_ge(acc_free, U_IN1 + m + 1)
                    pool.wait_ge(vsum, m - 1)
                    nc.gpsimd.tensor_tensor(sq[:, 0, :], sq[:, 0, :], V[:, m, :], ALU.add).then_inc(vsum, 1)

            def add_v_square(m):
                pool.wait_ge(vsq_ready, m + 1)
                if m > 1:
                    pool.wait_ge(vsq_added, m - 1)
                nc.gpsimd.tensor_tensor(sqacc[:, :], sqacc[:, :], sq[:, m % 2, :], ALU.add).then_inc(vsq_added, 1)

            uu = U_IN1 + KD
            split_n(uu + 3)
            for m in range(1, 4):
                add_v_square(m)
            split_n(uu + 4)
            for m in range(4, KD):
                add_v_square(m)
            for m in range(2, KD):
                split_n(uu + m + 3)
            for m in range(KD):
                split_n(U_OUT1 + m + 3)
                if m:
                    add_square(3, m)
            pool.wait_ge(xl_ready, 4 * KD)
            pool.wait_ge(st_v[0], 16 * KD)
            pool.wait_ge(st_v[1], 16 * KD)
            nc.gpsimd.memset(up[:, :, 0:FB], 0.0).then_inc(pads_zero, 1)
            ffn(1)

        @block.vector
        def _(dve):
            def x_lo(n, m, gname, gi):
                dve.wait_ge(xh_ready, KD * n + m + 1)
                nc.vector.scalar_tensor_tensor(out=xl[:, m, :], in0=X[:, m, :], scalar=pcol(gname, gi),
                                               in1=xh[:, m, :].bitcast(F32), op0=ALU.mult, op1=ALU.subtract)\
                    .then_inc(xl_ready, 1)

            def residual(u, m):
                dve.wait_ge(unit_done, u + 1)
                nc.vector.tensor_tensor(halves(X[:, m, :]), acc(u % 2), halves(X[:, m, :]), ALU.add)\
                    .then_inc(acc_free, 1)

            def factors(r):
                dve.wait_ge(std_ready, r + 1)
                nc.vector.reciprocal(rinv[:, :], std[:, :]).then_inc(rinv_ready, 1)
                dve.wait_ge(rinv_ready, r + 1)
                if r < 6:
                    for t in range(RT):
                        last = nc.vector.tensor_scalar(diag[:, t, :], ident[:, :], rinv[:, t:t + 1], None, ALU.mult)
                    last.then_inc(diag_ready, 1)

            def scaled(u, dst):
                dve.wait_ge(unit_done, u + 1)
                nc.vector.tensor_tensor(halves(dst), acc(u % 2), halves(rstd[:, :]), ALU.mult).then_inc(acc_free, 1)

            def scaled_padded(slot, u, dst, pad):
                dve.wait_ge(unit_done, u + 1)
                nc.vector.tensor_tensor(dst[:, pad:pad + HALF], PS[:, 2 * slot, 0:HALF], rstd[:, 0:HALF], ALU.mult)
                nc.vector.tensor_tensor(dst[:, pad + HALF:pad + PR], PS[:, 2 * slot + 1, 0:PR - HALF],
                                        rstd[:, HALF:PR], ALU.mult)
                n = NS * (pad + DS)
                nc.vector.tensor_tensor(smp(dst[:, pad + PR:pad + PR + n], pad + DS)[:, :, pad:],
                                        smp(PS[:, 2 * slot + 1, PR - HALF:HALF]), smp(rstd[:, PR:T]), ALU.mult)\
                    .then_inc(acc_free, 1)

            for k in range(KD):
                dve.wait_ge(xT, k + 1)
                nc.vector.tensor_copy(X[:, k, 0:PR], PS[:, 2 * (k % 4), :]).then_inc(x_ready, 1)
                if k >= 2:
                    x_lo(0, k - 2, "mix_norm", k - 2)
            for m in range(KD - 2, KD):
                x_lo(0, m, "mix_norm", m)
            factors(0)
            dve.wait_ge(rstd_ready, 1)

            def evacuate(u):
                if u in POOL_UNIT:
                    scaled_padded(u % 2, U_IN0 + u, xa[:, IN0[u], :], PB)
                    return
                p = PAIR_UNIT.index(u - u % 2)
                if p >= 2:
                    dve.wait_ge(glu_ready, 2 * p - 2)
                scaled(U_IN0 + u, ag[:, 2 * (p % 2) + u % 2, :])

            def make_glu(c):
                if c == 0:
                    dve.wait_ge(pads_zero, 2)
                    dve.wait_ge(setup_ready, 4)
                a_t, g_t = ag[:, 2 * (c % 2), :], ag[:, 2 * (c % 2) + 1, :]
                dve.wait_ge(sig_ready, c + 1)
                nc.vector.tensor_tensor(glu[:, c, CB:CB + PR], a_t[:, 0:PR], g_t[:, 0:PR], ALU.mult)\
                    .then_inc(glu_ready, 1)
                nc.vector.tensor_tensor(smp(glu[:, c, CB + PR:GL], CB + DS)[:, :, CB:], smp(a_t[:, PR:T]),
                                        smp(g_t[:, PR:T]), ALU.mult).then_inc(glu_ready, 1)

            steps_made = [0]

            def conv(c, third):
                dve.wait_ge(glu_ready, 2 * c + 2)
                for k in range(third * V_TAPS // 3, (third + 1) * V_TAPS // 3):
                    w = pcol("conv_w", k * KH + c)
                    sides = ((conv_o[:, c, 0:PR], glu[:, c, k:k + PR]),
                             (smp(conv_o[:, c, PR:T]), smp(glu[:, c, CB + PR:GL], CB + DS)[:, :, k:k + DS]))
                    for o, win in sides:
                        if k == 0:
                            ins = nc.vector.tensor_scalar(o, win, w, pcol("conv_b", c), ALU.mult, ALU.add)
                        else:
                            dve.wait_ge(conv_step, steps_made[0] - 1)
                            ins = nc.vector.scalar_tensor_tensor(out=o, in0=win, scalar=w, in1=o,
                                                                 op0=ALU.mult, op1=ALU.add)
                        ins.then_inc(conv_step, 1)
                        steps_made[0] += 1

            def combine(c):
                dve.wait_ge(conv_mm, c + 1)
                dve.wait_ge(conv_step, 2 * V_TAPS * (c + 1))
                nc.vector.tensor_tensor(conv_o[:, c, 0:PR], PS[:, S0, 0:PR], conv_o[:, c, 0:PR], ALU.add)
                nc.vector.tensor_tensor(conv_o[:, c, PR:T], PS[:, S1, 0:SM], conv_o[:, c, PR:T], ALU.add)\
                    .then_inc(conv_whole, 1)

            evacuate(0)
            evacuate(1)
            make_glu(0)
            conv(0, 0)
            evacuate(2)
            conv(0, 1)
            evacuate(3)
            make_glu(1)
            conv(0, 2)
            conv(1, 0)
            evacuate(4)
            combine(0)
            conv(1, 1)
            evacuate(5)
            conv(1, 2)
            evacuate(6)
            make_glu(2)
            conv(2, 0)
            evacuate(7)
            combine(1)
            conv(2, 1)
            evacuate(8)
            conv(2, 2)
            evacuate(9)
            make_glu(3)
            conv(3, 0)
            evacuate(10)
            combine(2)
            conv(3, 1)
            evacuate(11)
            conv(3, 2)
            combine(3)

            residual(U_OUT0, 0)
            residual(U_OUT0 + 1, 1)
            dve.wait_ge(mean_mm, 1)
            for c in range(KH):
                nc.vector.scalar_tensor_tensor(out=halves(conv_o[:, c, :]), in0=PS[:, M0:M1 + 1, 0:HALF],
                                               scalar=-1.0 / DH, in1=halves(conv_o[:, c, :]), op0=ALU.mult,
                                               op1=ALU.add).then_inc(cent_ready, 1)
            residual(U_OUT0 + 2, 2)
            residual(U_OUT0 + 3, 3)
            factors(1)
            residual(U_OUT0 + 4, 4)
            residual(U_OUT0 + 5, 5)
            dve.wait_ge(rstd_ready, 2)
            for c in range(KH):
                nc.vector.tensor_tensor(conv_o[:, c, :], conv_o[:, c, :], rstd[:, :], ALU.mult).then_inc(cn_ready, 1)
            residual(U_OUT0 + 6, 6)
            for c in range(KH):
                dve.wait_ge(hh_ready, c + 1)
                nc.vector.tensor_tensor(hl[:, KH + c, :], conv_o[:, c, :], hh[:, KH + c, :].bitcast(F32), ALU.subtract)\
                    .then_inc(h_lo_ready, 1)
            residual(U_OUT0 + 7, 7)
            for m in range(KD):
                dve.wait_ge(acc_free, U_OUT0 + m + 1)
                residual(U_OUT0 + KD + m, m)
                x_lo(1, m, "ffn_norm", m)

            def ffn(layer):
                n = 2 * layer + 1
                r = (2, 5)[layer]
                for g, ((t0, nt), ub) in enumerate(zip(GROUPS, U_GROUP)):
                    u0 = U_FFN[layer] + ub
                    c0 = layer * KF + t0

                    def product_lo(i):
                        dve.wait_ge(hh_ready, i + (H_FFN[layer] + t0 + 1))
                        if isinstance(i, int):
                            hi_, lo_ = hh[:, i, :], hl[:, i, :]
                        else:
                            hi_ = hh[:, bass.ds(i, 1), :].rearrange("p a t -> p (a t)")
                            lo_ = hl[:, bass.ds(i, 1), :].rearrange("p a t -> p (a t)")
                        nc.vector.tensor_tensor(lo_[:, 0:PR], cv[:, 2, 0:PR], hi_[:, 0:PR].bitcast(F32), ALU.subtract)
                        nc.vector.tensor_tensor(smp(lo_[:, PR:T]), smp(cv[:, 2, PR:PR + NS * (FB + DS)], FB + DS)[:, :, FB:],
                                                smp(hi_[:, PR:T].bitcast(F32)), ALU.subtract).then_inc(h_lo_ready, 1)

                    def step(i, before=None):
                        for j in range(2):
                            u = i * 2 + (u0 + j)
                            if layer or g or not isinstance(i, int) or i > 0:
                                dve.wait_ge(stash_ready, (i + c0) * 4 + (2 * j - 2))
                            scaled_padded(j, u, up[:, j, :], FB)
                            if j == 0 and before is not None:
                                product_lo(before)
                            dve.wait_ge(tap0_ready, (i + c0) * 2 + (j + 1))
                            ti = i + (t0 + j * KF)
                            for k in range(1, FK):
                                if k > 1:
                                    dve.wait_ge(tap1_ready, (i + c0) * 2 + (j + 1))
                                nc.vector.scalar_tensor_tensor(
                                    out=cv[:, j, :], in0=up[:, j, k:k + CL],
                                    scalar=pcol("ffn_conv_w", ti + (layer * FK + k) * 2 * KF), in1=cv[:, j, :],
                                    op0=ALU.mult, op1=ALU.add).then_inc(tap1_ready if k == 1 else tap_ready, 1)
                        dve.wait_ge(silu_ready, i + c0 + 1)
                        dve.wait_ge(tap_ready, (i + c0) * 2 + 2)
                        nc.vector.tensor_tensor(cv[:, 2, :], cv[:, 0, :], cv[:, 1, :], ALU.mult).then_inc(h_ready, 1)

                    if g == 0:
                        factors(r)
                        dve.wait_ge(rstd_ready, r + 1)
                    step(0)
                    with dve.Fori(0, nt - 1) as i:
                        step(i + 1, i)
                    product_lo(nt - 1)
                    ud = u0 + 2 * nt
                    for m in range(KD):
                        residual(ud + m, m)
                        if g == len(GROUPS) - 1 and layer == 0:
                            x_lo(2, m, "mix_norm", KD + m)

            ffn(0)

            dve.wait_ge(st_ffn, 48)
            factors(3)
            dve.wait_ge(rstd_ready, 4)
            for m in range(KD):
                scaled(U_IN1 + m, V[:, m, :])
            uu = U_IN1 + KD

            def u_take(m):
                if m == 0:
                    dve.wait_ge(gw_T, 1)
                scaled(uu + m, U[:, m, :])

            def v_norm(m):
                nc.vector.tensor_tensor(V[:, m, :], V[:, m, :], rstd_v[:, :], ALU.mult).then_inc(vn_ready, 1)

            def z_bias(m):
                dve.wait_ge(z_mm, m + 1)
                nc.vector.tensor_tensor(V[:, m, 0:PR].rearrange("p (c i) -> p c i", c=CH),
                                        PS[:, S0, :].rearrange("p (c i) -> p c i", c=CH),
                                        gate_b[:, m:m + 1, :].to_broadcast([P, CH, P]), ALU.add).then_inc(zb_ready, 1)
                nc.vector.tensor_tensor(smp(V[:, m, PR:T]), smp(PS[:, S1, 0:SM]),
                                        gate_b[:, m:m + 1, 0:DS].to_broadcast([P, NS, DS]), ALU.add).then_inc(zb_ready, 1)

            def uz(m):
                dve.wait_ge(zb_ready, 2 * m + 2)
                dve.wait_ge(acc_free, uu + m + 1)
                nc.vector.tensor_tensor(U[:, m, :], U[:, m, :], V[:, m, :], ALU.mult).then_inc(uz_ready, 1)

            def uz_lo(m):
                dve.wait_ge(uz_ready, m + 1)
                dve.wait_ge(hh_ready, H_MIX[1] + m + 1)
                nc.vector.tensor_tensor(hl[:, m, :], U[:, m, :], hh[:, m, :].bitcast(F32), ALU.subtract)\
                    .then_inc(h_lo_ready, 1)

            u_take(0)
            dve.wait_ge(mean_mm, 2)
            for m in range(KD):
                nc.vector.scalar_tensor_tensor(out=halves(V[:, m, :]), in0=PS[:, S0:S1 + 1, 0:HALF],
                                               scalar=-1.0 / D, in1=halves(V[:, m, :]), op0=ALU.mult,
                                               op1=ALU.add).then_inc(cent_ready, 1)
            u_take(1)
            u_take(2)
            factors(4)
            dve.wait_ge(rstd_ready, 5)
            for m in range(2):
                v_norm(m)
            u_take(3)
            for m in range(2, KD):
                v_norm(m)
            u_take(4)
            dve.wait_ge(ld_gb, 16)
            u_take(5)
            z_bias(0)
            uz(0)
            u_take(6)
            uz_lo(0)
            z_bias(1)
            uz(1)
            u_take(7)
            for m in range(2, KD):
                z_bias(m)
                uz_lo(m - 1)
                uz(m)
            uz_lo(KD - 1)
            for m in range(KD):
                residual(U_OUT1 + m, m)
                x_lo(3, m, "ffn_norm", KD + m)

            ffn(1)
            factors(6)
            dve.wait_ge(yrow_ready, 2 * KD)
            for n, r in enumerate((0, 2, CH)):
                if r < CH:
                    rows = y_rows[:, r, :]
                    nc.vector.tensor_scalar(rows, rows, rinv[:, r:r + 1], None, ALU.mult).then_inc(y_row_done, 1)
                else:
                    rows = y_rows[P - SM:P, CH, :]
                    nc.vector.tensor_scalar(rows, rows, rinv[P - SM:P, CH:CH + 1], None, ALU.mult).then_inc(y_row_done, 1)


_INS = ["x_prompt", "x_sample", "state_pool", "state_conv", "state_ffn", "mix_norm", "w_in_ab", "pool_w",
        "pool_scale", "conv_w", "conv_b", "conv_norm_g", "conv_norm_b", "w_out_ab", "w_in_c", "sgu_norm_g",
        "sgu_norm_b", "sgu_w", "sgu_bias", "w_out_c", "ffn_norm", "w_up", "ffn_conv_w", "ffn_conv_b", "w_down",
        "final_norm"]

def kernel(**inputs):
    import numpy as np
    import concourse.bacc as bacc
    from concourse.bass_utils import run_bass_kernel_spmd

    nc = bacc.Bacc("TRN2", target_bir_lowering=False, num_devices=1)
    arrays, args = {}, {}
    for name in _INS:
        a = np.ascontiguousarray(inputs[name])
        arrays[f"in_{name}"] = a
        args[name] = nc.dram_tensor(f"in_{name}", a.shape, mybir.dt.from_np(a.dtype), kind="ExternalInput").ap()
    xp, xs = arrays["in_x_prompt"].shape, arrays["in_x_sample"].shape
    sp, sc, sf = (arrays[f"in_state_{n}"].shape for n in ("pool", "conv", "ffn"))
    outs = {
        "y_prompt": xp, "y_sample": xs,
        "pool_prompt": (sp[0], xp[0], *sp[2:]), "pool_sample": sp,
        "conv_prompt": (sc[0], xp[0], *sc[2:]), "conv_sample": sc,
        "sgu_v_prompt": (1, xp[0], P, xp[2]), "sgu_v_sample": (1, *xs),
        "ffn_prompt": (sf[0], xp[0], *sf[2:]), "ffn_sample": sf,
    }
    for name, shape in outs.items():
        args[name] = nc.dram_tensor(f"out_{name}", shape, F32, kind="ExternalOutput").ap()
    hybrid_trunk(nc, **args)
    r = run_bass_kernel_spmd(nc, [arrays], core_ids=[0])
    return tuple(r.results[0][f"out_{name}"] for name in outs)
```

```python
from contextlib import ExitStack

import concourse.bass as bass
from concourse import mybir

F32 = mybir.dt.float32
F32R = mybir.dt.float32r
ALU = mybir.AluOpType
ACT = mybir.ActivationFunctionType
P = 128

PSUM_BANK = 512
WINDOWS = (2, 4, 8, 16)


def hybrid_trunk(nc, x_prompt, x_sample, state_pool, state_conv, state_ffn, mix_norm, w_in_ab, pool_w,
                 pool_scale, conv_w, conv_b, conv_norm_g, conv_norm_b, w_out_ab, w_in_c, sgu_norm_g,
                 sgu_norm_b, sgu_w, sgu_bias, w_out_c, ffn_norm, w_up, ffn_conv_w, ffn_conv_b, w_down,
                 final_norm, y_prompt, y_sample, pool_prompt, pool_sample, conv_prompt, conv_sample,
                 sgu_v_prompt, sgu_v_sample, ffn_prompt, ffn_sample):
    _, PR, D = x_prompt.shape
    NS, DS, _ = x_sample.shape
    SM = NS * DS
    T = PR + SM
    HALF = T // 2
    KD = D // P
    DH = D // 2
    KH = DH // P
    DF = w_down.shape[1]
    KF = DF // P
    GROUPS = ((0, 8), (8, 8), (16, KF - 16))
    PB = state_pool.shape[2]
    CB = state_conv.shape[2]
    TAPS = CB + 1
    PE_TAPS, G_TAPS = 6, 4
    V_TAPS = TAPS - PE_TAPS - G_TAPS
    FB = state_ffn.shape[2]
    FK = FB + 1
    CH = PR // P
    EPS = 1e-6
    RT = CH + 1

    U_IN0 = 0
    N_IN0 = 3 * KH
    U_OUT0 = U_IN0 + N_IN0
    U_FFN0 = U_OUT0 + 2 * KD
    N_FFN = 2 * KF + len(GROUPS) * KD
    U_IN1 = U_FFN0 + N_FFN
    U_OUT1 = U_IN1 + 2 * KD
    U_FFN1 = U_OUT1 + KD
    U_FFN = (U_FFN0, U_FFN1)
    N_UNITS = U_FFN1 + N_FFN
    U_GROUP = [sum(2 * n + KD for _, n in GROUPS[:g]) for g in range(len(GROUPS))]
    POOL_ORDER = tuple(reversed(range(KH)))
    PAIR_UNIT = (0, 3, 6, 9)
    POOL_UNIT = (2, 5, 8, 11)
    IN0 = [None] * N_IN0
    for c, u in enumerate(PAIR_UNIT):
        IN0[u], IN0[u + 1] = KH + c, 2 * KH + c
    for g, u in zip(POOL_ORDER, POOL_UNIT):
        IN0[u] = g
    assert KH == 4 and not any(u % 4 for u in (U_OUT0, U_FFN0, U_IN1, U_OUT1, U_FFN1, *U_GROUP))

    def tiles_of(u):
        if U_OUT0 <= u < U_FFN0:
            return KH
        for f in U_FFN:
            for b, (_, n) in zip(U_GROUP, GROUPS):
                if f + b + 2 * n <= u < f + b + 2 * n + KD:
                    return n
        return KD

    H_MIX = (0, KH + KF)
    H_FFN = (KH, KH + KF + KD)
    X_FINAL = (None, U_OUT0 + KD, U_IN1 - KD, U_OUT1, N_UNITS - KD)

    rows0 = [("mix_norm", mix_norm, 2 * KD), ("ffn_norm", ffn_norm, 2 * KD), ("final_norm", final_norm, KD),
             ("pool_scale", pool_scale, KH), ("conv_b", conv_b, KH), ("conv_norm_g", conv_norm_g, KH),
             ("conv_norm_b", conv_norm_b, KH), ("sgu_norm_g", sgu_norm_g, KD), ("sgu_norm_b", sgu_norm_b, KD)]
    PC = {}
    at = 0
    for name, _, n in rows0:
        PC[name] = at
        at += n
    NP0 = at
    PC["conv_w"] = NP0
    PC["ffn_conv_w"] = PC["conv_w"] + TAPS * KH
    PC["ffn_conv_b"] = PC["ffn_conv_w"] + 2 * FK * 2 * KF
    NPAR = PC["ffn_conv_b"] + 2 * 2 * KF
    FBLK = 2 * 2 * KF

    GL = CB + PR + NS * (CB + DS)
    XL = PB + PR + NS * (PB + DS)
    UL = FB + PR + NS * (FB + DS)
    CL = UL - FB

    flat = lambda ap: ap.rearrange("l (t p) -> (l t) p", p=P) if len(ap.shape) == 2 else ap.rearrange("(t p) -> t p", p=P)
    wblocks = lambda w: w.rearrange("(k p) n -> p k n", p=P)
    xp_rows = x_prompt.rearrange("b (r p) d -> p (b r) d", p=P)
    xs_rows = x_sample.rearrange("s t d -> (s t) d")
    yp_rows = y_prompt.rearrange("b (r p) d -> p (b r) d", p=P)
    ys_rows = y_sample.rearrange("s t d -> (s t) d")

    with ExitStack() as ctx:
        def sb(name, shape, dt=F32):
            return ctx.enter_context(nc.sbuf_tensor(name, shape, dt))

        def sem(name):
            return ctx.enter_context(nc.semaphore(name))

        ctx.enter_context(nc.allow_non_contiguous_dma(reason="small state rows"))
        X = sb("residual", [P, KD, T])
        xh = sb("x_hi", [P, KD, T], F32R)
        xl = sb("x_lo", [P, KD, T], F32R)
        hh = sb("h_hi", [P, KD, T], F32R)
        hl = sb("h_lo", [P, KD, T], F32R)
        w_raw = [sb(f"w_raw{s}", [P, KD * P]) for s in range(2)]
        w_hi = [sb(f"w_hi{s}", [P, KD * P], F32R) for s in range(4)]
        w_lo = [sb(f"w_lo{s}", [P, KD * P], F32R) for s in range(4)]
        par = sb("params", [P, NPAR])
        state_T = sb("ffn_state_T", [P, 2, NS * FB, 2 * KF])
        ident = sb("ident", [P, P])
        ones = sb("ones", [P, P])
        rstd = sb("rstd", [P, T])
        sq = sb("squares", [P, 2, T])
        sqacc = sb("squares_sum", [P, T])
        poolw = sb("pool_w_sb", [P, KH, P])
        eps = sb("eps", [P, 1])
        table = sb("table", [P, 8])
        std = sb("std", [P, RT])
        rinv = sb("rinv", [P, RT])
        corr = sb("count_corr", [P, sum(WINDOWS) - len(WINDOWS)])
        ARENA = 14800
        arena = sb("arena", [P, ARENA])
        diag = sq[:, :, :].rearrange("p a t -> p (a t)")[:, 0:RT * P].rearrange("p (r c) -> p r c", r=RT)

        def cut(start, *dims):
            n = 1
            for d in dims:
                n *= d
            assert start + n <= ARENA, (start, n)
            v = arena[:, start:start + n]
            if len(dims) == 2:
                v = v.rearrange("p (a b) -> p a b", a=dims[0])
            return v

        x_rows = cut(0, RT, D)
        conv_o = cut(0, KH, T)
        ag = cut(KH * T, 4, T)
        X1 = RT * D
        par_rows = cut(X1, 6, P)
        pool_rows = cut(X1 + 6 * P, DH)
        conv_rows = cut(X1 + 6 * P + DH, 2, DH)
        pool_tmp = [cut(2 * KH * T, XL), cut(2 * KH * T + XL, XL)]
        D0 = 2 * KH * T + 2 * XL + 2
        d_t = [cut(D0, T), cut(D0 + T, T), sq[:, 0, :], sq[:, 1, :]]
        XA0 = X1 + 6 * P + 3 * DH
        xa = cut(XA0, KH, XL)
        glu = cut(XA0 + KH * XL, KH, GL)
        g_conv = [conv_o[:, 1, :], conv_o[:, 2, :], ag[:, 0, :], ag[:, 1, :]]
        g_prod = [state_T.rearrange("p l a b -> p (l a b)")[:, q * T:(q + 1) * T] for q in range(2)]
        tap_w = cut(XA0 + KH * XL + KH * GL, PE_TAPS, P)
        new_x = sqacc[:, 0:KH * SM].rearrange("p (a b) -> p a b", a=KH)
        new_glu = sqacc[:, KH * SM:2 * KH * SM].rearrange("p (a b) -> p a b", a=KH)
        out_rows0 = [ag[:, 0, 0:DH], ag[:, 1, 0:DH], pool_tmp[0][:, 0:DH], pool_tmp[1][:, 0:DH]]
        state_rows = cut(XA0 + KH * XL, 2 * NS * FB * 2 * KF // P, P)
        up = cut(0, 2, UL)
        cv = cut(2 * UL, 3, CL)
        F0 = 2 * UL + 3 * CL
        stash = cut(F0, (FB + NS * FB), 2 * KF)
        stash_rows = cut(F0 + (FB + NS * FB) * 2 * KF, 7, P)
        F1 = F0 + (FB + NS * FB) * 2 * KF + 7 * P
        xg = cut(F1, 2, T)
        y_rows = cut(F1 + 2 * T, RT, D)
        V = cut(0, KD, T)
        U = cut(KD * T, KD, T)
        gate_w_rows = cut(KD * T, KD, P)
        v_rows = [cut(2 * KD * T + i * RT * P, RT, P) for i in range(2)]
        G0 = 2 * KD * T + 2 * RT * P
        gate_w_T = cut(G0, KD, P)
        gate_b = cut(G0 + KD * P, KD, P)
        rstd_v = cut(G0 + 2 * KD * P, T)
        block_w = state_T[0:SM, 0, :, :].rearrange("p a b -> p (a b)")[:, 0:KD * SM].rearrange("p (h i) -> p h i", h=KD)

        PS = ctx.enter_context(nc.psum_tensor("psum", [P, 8, PSUM_BANK], F32))
        acc = lambda slot: PS[:, 2 * slot:2 * slot + 2, 0:HALF]
        S0, S1, M0, M1 = 4, 5, 6, 7
        halves = lambda v: v.rearrange("p (a t) -> p a t", a=2)
        smp = lambda v, n=DS: v.rearrange("p (s t) -> p s t", t=n)

        ld_x = [sem(f"ld_x{q}") for q in range(KD // 2)]
        ld_xs, ld_mix = sem("ld_x_samples"), sem("ld_mix_norm")
        ld_p0, ld_par, ld_pw = sem("ld_p0"), sem("ld_par"), sem("ld_pool_w")
        ld_cs, ld_fs, ld_gw, ld_gb = sem("ld_conv_state"), sem("ld_ffn_state"), sem("ld_gate_w"), sem("ld_gate_b")
        raw_ready = [sem("raw_ready0"), sem("raw_ready1")]
        hi_ready, lo_ready, unit_done, acc_free = sem("w_hi_ready"), sem("w_lo_ready"), sem("unit_done"), sem("acc_free")
        const_ready, ident_ready, corr_ready = sem("const_ready"), sem("ident_ready"), sem("corr_ready")
        p0_T, p0_ready, xs_ready, xT = sem("p0_T"), sem("p0_ready"), sem("xs_ready"), sem("x_T")
        setup_T, setup_ready = sem("setup_T"), sem("setup_ready")
        x_ready, xh_ready, xl_ready = sem("x_ready"), sem("xh_ready"), sem("xl_ready")
        sq_ready, sq_added = sem("sq_ready"), sem("sq_added")
        var_mm, std_ready, rinv_ready, diag_ready = sem("var_mm"), sem("std_ready"), sem("rinv_ready"), sem("diag_ready")
        bc_mm, rstd_ready = sem("bc_mm"), sem("rstd_ready")
        sig_ready, glu_ready = sem("sig_ready"), sem("glu_ready")
        conv_step, pads_zero = sem("conv_step"), sem("pads_zero")
        tap_w_ready, conv_mm, conv_whole = sem("tap_w_ready"), sem("conv_mm"), sem("conv_whole")
        tap_product, pool_tap, pe_added = sem("tap_product"), sem("pool_tap"), sem("pe_added")
        new_packed = sem("new_packed")
        wx_ready, win_step, d_ready = sem("window_x_ready"), sem("win_step"), sem("d_ready")
        pool_scale_ready = sem("pool_scale_ready")
        pool_mm, hh_ready, h_lo_ready = sem("pool_mm"), sem("hh_ready"), sem("h_lo_ready")
        ya_read, ya_hi, ya_ready = sem("ya_read"), sem("ya_hi"), sem("ya_ready")
        mean_mm, cent_ready = sem("mean_mm"), sem("cent_ready")
        csq_ready, csq_added = sem("csq_ready"), sem("csq_added")
        cn_ready, cs_ready = sem("cn_ready"), sem("cs_ready")
        so_T, so_rows, st_out = sem("state_out_T"), sem("state_out_rows"), sem("st_out")
        fs_T, fs_ready = sem("ffn_state_T_mm"), sem("ffn_state_ready")
        tap0_ready, tap1_ready, tap_ready = sem("tap0_ready"), sem("tap1_ready"), sem("tap_ready")
        silu_ready, h_ready, pad_ready, stash_ready = sem("silu_ready"), sem("h_ready"), sem("pad_ready"), sem("stash_ready")
        stash_T, stash_rows_ready, st_ffn = sem("stash_T"), sem("stash_rows_ready"), sem("st_ffn")
        gw_T, gw_copied, gw_ready = sem("gate_w_T_mm"), sem("gate_w_copied"), sem("gate_w_ready")
        bw_zero, bw_ready = sem("block_w_zero"), sem("block_w_ready")
        vsum = sem("vsum")
        vsq_ready, vsq_added = sem("vsq_ready"), sem("vsq_added")
        vn_ready, va_ready, v_T = sem("vn_ready"), sem("va_ready"), sem("v_T")
        vrow_ready, st_v, z_mm, zb_ready = sem("vrow_ready"), [sem("st_v0"), sem("st_v1")], sem("z_mm"), sem("zb_ready")
        uz_ready = sem("uz_ready")
        y_row_done = sem("y_row_done")
        xg_ready, y_T, yrow_ready, y_scaled, st_y = sem("xg_ready"), sem("y_T"), sem("yrow_ready"), sem("y_scaled"), sem("st_y")
        st_state = sem("st_state")

        block = ctx.enter_context(nc.Block())

        def pcol(name, i):
            if isinstance(i, int):
                return par[:, PC[name] + i:PC[name] + i + 1]
            return par[:, bass.ds(i + PC[name], 1)]

        @block.sync
        def _(sp):
            def load(slot, u, src, nk):
                if not isinstance(u, int) or u >= 2:
                    sp.wait_ge(lo_ready, u - 1)
                sp.dma_start(w_raw[slot][:, 0:nk * P].rearrange("p (k n) -> p k n", k=nk), src)\
                    .then_inc(raw_ready[slot], 16)

            def col(w, t):
                v = wblocks(w)
                return v[:, :, t * P:(t + 1) * P] if isinstance(t, int) else v[:, :, bass.ds(t * P, P)]

            def load_rows(u0, n, w, t0=0):
                with sp.Fori(0, n // 2) as i:
                    for j in range(2):
                        load(j, i * 2 + (u0 + j), col(w, i * 2 + (t0 + j)), w.shape[0] // P)

            for q in range(KD // 2):
                cols = slice(2 * q * P, 2 * (q + 1) * P)
                sp.dma_start(x_rows[:, 0:CH, cols], xp_rows[:, :, cols]).then_inc(ld_x[q], 16)
                if q < 2:
                    load(q, U_IN0 + q, col(w_in_ab[0], IN0[q]), KD)
            at = 2 * KD
            for _, ap, n in rows0[1:]:
                sp.dma_start(par_rows[at:at + n, 0, :], flat(ap)).then_inc(ld_p0, 16)
                at += n
            sp.dma_start(pool_rows[0:NS * PB, :], state_pool.rearrange("l s r d -> (l s r) d")).then_inc(ld_par, 16)
            sp.dma_start(par_rows[0:TAPS * KH, 1, :], conv_w.rearrange("l k (t p) -> (l k t) p", p=P)).then_inc(ld_par, 16)
            cw = ffn_conv_w.rearrange("l k (t p) -> (l k t) p", p=P)
            for b in range(3):
                sp.dma_start(par_rows[0:FBLK, 2 + b, :], cw[b * FBLK:(b + 1) * FBLK, :]).then_inc(ld_par, 16)
            sp.dma_start(par_rows[0:FBLK, 5, :], flat(ffn_conv_b)).then_inc(ld_par, 16)
            for b in range(2):
                sp.dma_start(conv_rows[0:4 * CB, b, :],
                             state_conv[0, 4 * b:4 * b + 4].rearrange("s r d -> (s r) d")).then_inc(ld_cs, 16)
            for u in range(2, N_IN0):
                load(u % 2, U_IN0 + u, col(w_in_ab[0], IN0[u]), KD)
                if u == 3:
                    sp.dma_start(poolw[:, :, :], pool_w[0].rearrange("g i o -> i g o")).then_inc(ld_pw, 16)
                    sp.dma_start(pool_sample[0, :, 0:PB - DS, :], state_pool[0, :, DS:PB, :]).then_inc(st_state, 16)
                    sp.dma_start(conv_sample[0, :, 0:CB - DS, :], state_conv[0, :, DS:CB, :]).then_inc(st_state, 16)
            load_rows(U_OUT0, KD, w_out_ab[0, 0:DH])
            load_rows(U_OUT0 + KD, 4, w_out_ab[0, DH:D])
            sp.wait_ge(conv_whole, KH)
            sp.wait_ge(so_T, 2)
            sp.dma_start(state_rows, state_ffn.rearrange("l s r (t p) -> (l s r t) p", p=P)
                         .rearrange("(b q) p -> q b p", q=P)).then_inc(ld_fs, 16)
            load_rows(U_OUT0 + KD + 4, 4, w_out_ab[0, DH:D], 4)
            for layer in range(2):
                if layer == 1:
                    load_rows(U_IN1, KD, w_in_c[0], KD)
                    load_rows(U_IN1 + KD, KD, w_in_c[0])
                    load_rows(U_OUT1, KD, w_out_c[0])
                for (t0, n), ub in zip(GROUPS, U_GROUP):
                    u0 = U_FFN[layer] + ub
                    with sp.Fori(0, n) as i:
                        for j in range(2):
                            load(j, i * 2 + (u0 + j), col(w_up[layer], i + (t0 + j * KF)), KD)
                    load_rows(u0 + 2 * n, KD, w_down[layer, t0 * P:(t0 + n) * P])
            for n, r in enumerate((0, 2, CH)):
                sp.wait_ge(y_row_done, n + 1)
                if r < CH:
                    sp.dma_start(yp_rows[:, r, :], y_rows[:, r, :]).then_inc(st_y, 16)
                else:
                    sp.dma_start(ys_rows, y_rows[P - SM:P, CH, :]).then_inc(st_y, 16)
            sp.wait_ge(st_state, 16 * 2)
            sp.wait_ge(st_out, 16 * 4)
            sp.wait_ge(st_ffn, 16 * 6)
            sp.wait_ge(st_v[0], 16 * KD)
            sp.wait_ge(st_v[1], 16 * KD)
            sp.wait_ge(st_y, 16 * RT)

        @block.tensor
        def _(pe):
            def products(q, k, r_at, nk, rh, rl, first, final):
                for n, (w, r) in enumerate(((w_hi, rh), (w_hi, rl), (w_lo, rh))):
                    for half in range(2):
                        last = nc.tensor.matmul(PS[:, 2 * (q % 2) + half, 0:HALF], w[q][:, k * P:(k + 1) * P],
                                                r[:, r_at, half * HALF:(half + 1) * HALF],
                                                start=(first and n == 0), stop=(final and n == 2))
                return last

            def weights(u):
                pe.wait_ge(lo_ready, u + 1)
                if not isinstance(u, int) or u >= 2:
                    pe.wait_ge(acc_free, u - 1)

            def unit(q, u, nk, rh, rl, ready=None, base=0, middle=None, r0=0, order=None):
                weights(u)
                order = order or range(nk)
                for at, k in enumerate(order):
                    if ready is not None:
                        pe.wait_ge(ready, base + at + 1)
                    last = products(q, k, r0 + k, nk, rh, rl, at == 0, at == nk - 1)
                    if middle is not None and at == nk // 2:
                        middle()
                last.then_inc(unit_done, 1)

            def two_units(u, nk, rh, rl, ready, base):
                for q in range(2):
                    weights(u + q)
                    for k in range(nk - 1):
                        if q == 0:
                            pe.wait_ge(ready, base + k + 1)
                        products((u + q) % 4, k, k, nk, rh, rl, k == 0, False)
                pe.wait_ge(ready, base + nk)
                for q in range(2):
                    products((u + q) % 4, nk - 1, nk - 1, nk, rh, rl, False, True).then_inc(unit_done, 1)

            def row_sums(src, first=True, final=True):
                for r in range(RT):
                    lo = r * P if r < CH else T - P
                    last = nc.tensor.matmul(PS[:, S0, r:r + 1], src[:, lo:lo + P], ones[:, 0:1],
                                            start=(first and r == 0), stop=(final and r == RT - 1),
                                            skip_group_check=True)
                return last

            def spread(r):
                pe.wait_ge(diag_ready, r + 1)
                nc.tensor.matmul(PS[:, M0, 0:PR], ones[:, :], diag[:, 0:CH, :], start=True, stop=True)
                nc.tensor.matmul(PS[:, M1, 0:SM], ones[:, :], diag[:, CH, P - SM:P], start=True, stop=True)\
                    .then_inc(bc_mm, 1)

            def norm_sums(n, r):
                pe.wait_ge(sq_added, (KD - 1) * (n + 1))
                row_sums(sqacc).then_inc(var_mm, 1)

            def turn_x(k):
                b = S0 + 2 * (k % 2)
                pe.wait_ge(ld_x[k // 2], 16)
                if k >= 2:
                    pe.wait_ge(x_ready, k - 1)
                    pe.wait_ge(xs_ready, k - 1)
                for r in range(CH):
                    nc.tensor.transpose(PS[:, b, r * P:(r + 1) * P], x_rows[:, r, k * P:(k + 1) * P], ident[:, :])
                nc.tensor.transpose(PS[:, b + 1, 0:SM], x_rows[0:SM, CH, k * P:(k + 1) * P], ident[0:SM, 0:SM])\
                    .then_inc(xT, 1)

            def first_products(k):
                for q in range(2):
                    if k == 0:
                        weights(q)
                    pe.wait_ge(xl_ready, k + 1)
                    last = products(q, k, k, KD, xh, xl, k == 0, k == KD - 1)
                    if k == KD - 1:
                        last.then_inc(unit_done, 1)

            pe.wait_ge(ident_ready, 1)
            pe.wait_ge(ld_mix, 16)
            nc.tensor.transpose(PS[:, 0, 0:2 * KD], par_rows[0:2 * KD, 0, :], ident[0:2 * KD, 0:2 * KD]).then_inc(p0_T, 1)
            pe.wait_ge(ld_xs, 16)
            for k in range(KD):
                turn_x(k)
                if k == 1:
                    pe.wait_ge(p0_ready, 1)
                if k >= 4:
                    first_products(k - 4)
            first_products(KD - 4)
            first_products(KD - 3)
            pe.wait_ge(x_ready, KD)
            pe.wait_ge(xs_ready, KD)
            norm_sums(0, 0)
            first_products(KD - 2)
            pe.wait_ge(ld_p0, 16 * (len(rows0) - 1))
            nc.tensor.transpose(PS[:, M1, P:P + NP0], par_rows[0:NP0, 0, :], ident[0:NP0, 0:NP0])
            pe.wait_ge(ld_par, 16 * 6)
            for c in range(KH):
                last = nc.tensor.transpose(PS[:, S1, c * NS * PB:(c + 1) * NS * PB],
                                           pool_rows[0:NS * PB, c * P:(c + 1) * P], ident[0:NS * PB, 0:NS * PB])
            last.then_inc(setup_T, 1)
            first_products(KD - 1)
            spread(0)
            at = 0
            for b, n in ((1, TAPS * KH), (2, FBLK), (3, FBLK), (4, FBLK), (5, FBLK)):
                last = nc.tensor.transpose(PS[:, S0, at:at + n], par_rows[0:n, b, :], ident[0:n, 0:n])
                at += n
            last.then_inc(setup_T, 1)
            pe.wait_ge(ld_cs, 32)
            pe.wait_ge(rstd_ready, 1)
            pe.wait_ge(p0_ready, 2)
            for b in range(2):
                for c in range(KH):
                    last = nc.tensor.transpose(PS[:, M0 + b, c * 4 * CB:(c + 1) * 4 * CB],
                                               conv_rows[0:4 * CB, b, c * P:(c + 1) * P],
                                               ident[0:4 * CB, 0:4 * CB])
                last.then_inc(setup_T, 1)

            def conv_taps(c):
                pe.wait_ge(glu_ready, 2 * c + 2)
                if c:
                    pe.wait_ge(conv_whole, c)
                for n in range(PE_TAPS):
                    k = TAPS - PE_TAPS + n
                    pe.wait_ge(tap_w_ready, PE_TAPS * c + n + 1)
                    nc.tensor.matmul(PS[:, S0, 0:PR], tap_w[:, n, :], glu[:, c, k:k + PR],
                                     start=(n == 0), stop=(n == PE_TAPS - 1))
                    last = nc.tensor.matmul(PS[:, S1, 0:SM], tap_w[:, n, :],
                                            smp(glu[:, c, CB + PR:GL], CB + DS)[:, :, k:k + DS],
                                            start=(n == 0), stop=(n == PE_TAPS - 1))
                last.then_inc(conv_mm, 1)

            def pool_map(n):
                pe.wait_ge(d_ready, n + 1)
                if n == 0:
                    pe.wait_ge(ld_pw, 16)
                    pe.wait_ge(setup_ready, 4)
                else:
                    pe.wait_ge(ya_read, n)
                for half in range(2):
                    last = nc.tensor.matmul(PS[:, M0 + half, 0:HALF], poolw[:, POOL_ORDER[n], :],
                                            d_t[n][:, half * HALF:(half + 1) * HALF], start=True, stop=True)
                last.then_inc(pool_mm, 1)

            def conv_mean(c):
                for half in range(2):
                    last = nc.tensor.matmul(PS[:, M0 + half, 0:HALF], ones[:, :],
                                            conv_o[:, c, half * HALF:(half + 1) * HALF],
                                            start=(c == 0), stop=(c == KH - 1))
                return last

            def in_units(*us):
                for u in us:
                    unit(u % 4, U_IN0 + u, KD, xh, xl)

            in_units(2, 3)
            conv_taps(0)
            in_units(4, 5)
            in_units(6)
            pool_map(0)
            conv_taps(1)
            in_units(7, 8)
            pool_map(1)
            in_units(9, 10)
            conv_taps(2)
            pool_map(2)
            in_units(11)
            conv_taps(3)
            pool_map(3)
            pe.wait_ge(ya_read, KH)
            for c in range(KH - 1):
                pe.wait_ge(conv_whole, c + 1)
                conv_mean(c)

            def ya_unit(m, middle=None):
                unit(m % 4, U_OUT0 + m, KH, hh, hl, ya_ready if m == 0 else None, 0, middle, order=POOL_ORDER)

            ya_unit(0)
            ya_unit(1)
            pe.wait_ge(conv_whole, KH)
            conv_mean(KH - 1).then_inc(mean_mm, 1)
            ya_unit(2)
            ya_unit(3)
            pe.wait_ge(csq_added, KH - 1)
            row_sums(d_t[0]).then_inc(var_mm, 1)
            ya_unit(4, lambda: spread(1))
            ya_unit(5)
            pe.wait_ge(rstd_ready, 2)
            for g in range(KH):
                nc.tensor.transpose(PS[0:PB, M0, g * P:(g + 1) * P], xa[:, g, PR:PR + PB], ident[:, :])
            pe.wait_ge(new_packed, KH)
            for g in range(KH):
                last = nc.tensor.transpose(PS[0:SM, M1, g * P:(g + 1) * P], new_x[:, g, :], ident[:, :])
            last.then_inc(so_T, 1)
            ya_unit(6)
            ya_unit(7)

            def yb_unit(m):
                unit(m % 4, U_OUT0 + KD + m, KH, hh, hl, h_lo_ready if m == 0 else None, 0, r0=KH)

            yb_unit(0)
            pe.wait_ge(so_rows, 2)
            for c in range(KH):
                nc.tensor.transpose(PS[0:CB, M0, c * P:(c + 1) * P], glu[:, c, PR:PR + CB], ident[:, :])
            pe.wait_ge(new_packed, KH + 1)
            for c in range(KH):
                last = nc.tensor.transpose(PS[0:SM, M1, c * P:(c + 1) * P], new_glu[:, c, :], ident[:, :])
            last.then_inc(so_T, 1)
            for m in range(1, 6):
                yb_unit(m)
            nb = 2 * NS * FB * 2 * KF // P
            pe.wait_ge(so_rows, 4)
            pe.wait_ge(ld_fs, 16)
            for b in range(nb):
                bank, c = (M0, M1, S1)[b // 4], b % 4
                last = nc.tensor.transpose(PS[:, bank, c * P:(c + 1) * P], state_rows[:, b, :], ident[:, :])
            last.then_inc(fs_T, 1)
            yb_unit(6)
            yb_unit(7)

            def plain_units(u0, nk, rh, rl, n):
                with pe.Fori(0, n // 4) as i:
                    for q in range(4):
                        unit(q, i * 4 + (u0 + q), nk, rh, rl)

            def ffn(layer):
                n = 2 * layer + 1
                r = (2, 5)[layer]
                for g, ((t0, nt), ub) in enumerate(zip(GROUPS, U_GROUP)):
                    u0 = U_FFN[layer] + ub
                    last_group = g == len(GROUPS) - 1
                    if g == 0:
                        unit(0, u0, KD, xh, xl, xl_ready, KD * n)
                        norm_sums(n, r)

                        def middle():
                            if layer == 0:
                                pe.wait_ge(fs_ready, 3)
                            else:
                                pe.wait_ge(vrow_ready, 2 * KD)
                            spread(r)
                        unit(1, u0 + 1, KD, xh, xl, middle=middle)
                        unit(2, u0 + 2, KD, xh, xl)
                        unit(3, u0 + 3, KD, xh, xl)
                        plain_units(u0 + 4, KD, xh, xl, 2 * nt - 4)
                    else:
                        plain_units(u0, KD, xh, xl, 2 * nt)
                    ud = u0 + 2 * nt
                    two_units(ud, nt, hh, hl, h_lo_ready, H_FFN[layer] + t0)
                    if last_group:
                        pe.wait_ge(stash_ready, 2 * 2 * KF * (layer + 1))
                        flat_stash = stash.rearrange("p a b -> p (a b)")
                        at = 0
                        for b in range(7):
                            n_ = FB * 2 * KF if b == 0 else min(P, (FB + NS * FB) * 2 * KF - at)
                            last = nc.tensor.transpose(PS[0:n_, (M0, M1)[b // 4], (b % 4) * P:(b % 4 + 1) * P],
                                                       flat_stash[:, at:at + n_], ident[:, :])
                            at += n_
                        last.then_inc(stash_T, 1)
                    if not last_group or layer == 0:
                        unit(2, ud + 2, nt, hh, hl)
                        unit(3, ud + 3, nt, hh, hl)
                        for q in range(4):
                            unit(q, ud + 4 + q, nt, hh, hl)

            def out_rows(j, m):
                pe.wait_ge(xg_ready, m + 1)
                if isinstance(m, int) and m == 0:
                    pe.wait_ge(stash_rows_ready, 4)
                else:
                    pe.wait_ge(yrow_ready, m * 2)
                for r in range(CH):
                    nc.tensor.transpose(PS[:, M0, r * P:(r + 1) * P], xg[:, j, r * P:(r + 1) * P], ident[:, :])
                nc.tensor.transpose(PS[:, M1, 0:P], xg[:, j, T - P:T], ident[:, :]).then_inc(y_T, 1)

            ffn(0)

            unit(0, U_IN1, KD, xh, xl, xl_ready, KD * 2)
            norm_sums(2, 3)

            def middle1():
                pe.wait_ge(stash_rows_ready, 2)
                spread(3)
            unit(1, U_IN1 + 1, KD, xh, xl, middle=middle1)
            pe.wait_ge(ld_gw, 16)
            pe.wait_ge(rstd_ready, 4)
            for h in range(KD):
                last = nc.tensor.transpose(PS[:, M0 + h // 4, (h % 4) * P:(h % 4 + 1) * P], gate_w_rows[:, h, :],
                                           ident[:, :])
            last.then_inc(gw_T, 1)
            unit(2, U_IN1 + 2, KD, xh, xl)
            unit(3, U_IN1 + 3, KD, xh, xl)
            plain_units(U_IN1 + 4, KD, xh, xl, KD - 4)

            def v_turn(m):
                pe.wait_ge(va_ready, m + 1)
                if m == 0:
                    pe.wait_ge(rstd_ready, 5)
                else:
                    pe.wait_ge(vrow_ready, 2 * m)
                for r in range(CH):
                    nc.tensor.transpose(PS[:, M0, r * P:(r + 1) * P], V[:, m, r * P:(r + 1) * P], ident[:, :])
                nc.tensor.transpose(PS[0:SM, M1, 0:P], V[:, m, PR:T], ident[:, :]).then_inc(v_T, 1)

            def gate(m):
                pe.wait_ge(vrow_ready, 2 * m + 2)
                if m == 0:
                    pe.wait_ge(gw_ready, 1)
                    pe.wait_ge(bw_ready, 16 * NS)
                    pe.wait_ge(std_ready, 5)
                else:
                    pe.wait_ge(zb_ready, 2 * m)
                for c in range(CH):
                    nc.tensor.matmul(PS[:, S0, c * P:(c + 1) * P], v_rows[m % 2][:, c, :], gate_w_T[:, m, :],
                                     start=True, stop=True)
                nc.tensor.matmul(PS[:, S1, 0:SM], v_rows[m % 2][0:SM, CH, :], block_w[:, m, :],
                                 start=True, stop=True).then_inc(z_mm, 1)

            def v_mean():
                pe.wait_ge(vsum, KD - 1)
                for half in range(2):
                    last = nc.tensor.matmul(PS[:, S0 + half, 0:HALF], ones[:, :],
                                            sq[:, 0, half * HALF:(half + 1) * HALF], start=True, stop=True)
                last.then_inc(mean_mm, 1)

            def v_var():
                pe.wait_ge(vsq_added, KD - 1)
                pe.wait_ge(cent_ready, KH + KD)
                row_sums(sqacc).then_inc(var_mm, 1)

            def turn_and_gate(m):
                if m < KD:
                    v_turn(m)
                if m > 0:
                    gate(m - 1)

            uu = U_IN1 + KD
            unit(0, uu, KD, xh, xl, middle=v_mean)
            unit(1, uu + 1, KD, xh, xl)
            unit(2, uu + 2, KD, xh, xl, middle=v_var)
            spread(4)
            for m in range(3, KD):
                unit(m % 4, uu + m, KD, xh, xl, middle=lambda: turn_and_gate(2 * (m - 3)))
                if m < KD - 1:
                    turn_and_gate(2 * (m - 3) + 1)

            two_units(U_OUT1, KD, hh, hl, h_lo_ready, H_MIX[1])
            unit(2, U_OUT1 + 2, KD, hh, hl)
            unit(3, U_OUT1 + 3, KD, hh, hl)
            plain_units(U_OUT1 + 4, KD, hh, hl, KD - 4)

            ffn(1)
            ud = N_UNITS - KD
            nt = GROUPS[-1][1]
            for m in range(2, KD):
                unit(m % 4, ud + m, nt, hh, hl, middle=lambda: out_rows(m % 2, m - 2))
            out_rows(0, KD - 2)
            pe.wait_ge(sq_added, (KD - 1) * 4 + KD - 2)
            row_sums(sqacc, final=False)
            pe.wait_ge(sq_ready, KD * 5)
            row_sums(sq[:, 1, :], first=False).then_inc(var_mm, 1)
            out_rows(1, KD - 1)

        @block.scalar
        def _(act):
            act.dma_start(par_rows[0:2 * KD, 0, :], flat(mix_norm)).then_inc(ld_mix, 16)
            act.dma_start(x_rows[0:SM, CH, :], xs_rows).then_inc(ld_xs, 16)

            def split(slot, u, pair, nk):
                act.wait_ge(raw_ready[slot % 2], (pair + 1) * 16)
                if not isinstance(u, int) or u >= 4:
                    act.wait_ge(unit_done, u - 3)
                nc.scalar.activation(w_hi[slot][:, 0:nk * P], w_raw[slot % 2][:, 0:nk * P], ACT.Copy).then_inc(hi_ready, 1)

            def split_n(u):
                if u < N_UNITS:
                    split(u % 4, u, u // 2, tiles_of(u))

            def norm_in(n, m, r, gname, gi):
                gain_hi(n, m, gname, gi)
                square(n, m, r)

            def gain_hi(n, m, gname, gi):
                act.wait_ge(*((x_ready, m + 1) if n == 0 else (acc_free, X_FINAL[n] + m + 1)))
                nc.scalar.activation(xh[:, m, :], X[:, m, :], ACT.Identity, bias=0.0,
                                     scale=pcol(gname, gi)).then_inc(xh_ready, 1)

            def square(n, m, r):
                if m == 0:
                    if r:
                        act.wait_ge(var_mm, r)
                        act.wait_ge(bc_mm, r)
                elif m >= 3:
                    act.wait_ge(sq_added, (KD - 1) * n + m - 2)
                dst = sqacc[:, :] if m == 0 else sq[:, m % 2, :]
                nc.scalar.activation(dst, X[:, m, :], ACT.Square).then_inc(sq_ready, 1)

            def root(r, width):
                act.wait_ge(var_mm, r + 1)
                nc.scalar.activation(std[:, :], PS[:, S0, 0:RT], ACT.Sqrt, bias=eps[:, 0:1],
                                     scale=1.0 / width).then_inc(std_ready, 1)

            def take_rstd(r, dst):
                act.wait_ge(bc_mm, r + 1)
                nc.scalar.activation(dst[:, 0:PR], PS[:, M0, 0:PR], ACT.Copy)
                nc.scalar.activation(dst[:, PR:T], PS[:, M1, 0:SM], ACT.Copy).then_inc(rstd_ready, 1)

            def table_for(n, func):
                nc.scalar.activation(table[:, n:n + 1], eps[:, 0:1], func)

            act.wait_ge(const_ready, 2)
            table_for(0, ACT.Sqrt)
            act.wait_ge(p0_T, 1)
            nc.scalar.activation(par[:, 0:2 * KD], PS[:, 0, 0:2 * KD], ACT.Copy).then_inc(p0_ready, 1)
            act.wait_ge(p0_ready, 1)
            for m in range(KD):
                act.wait_ge(xT, m + 1)
                nc.scalar.activation(X[:, m, PR:T], PS[:, S0 + 2 * (m % 2) + 1, 0:SM], ACT.Copy).then_inc(xs_ready, 1)
                act.wait_ge(xs_ready, m + 1)
                gain_hi(0, m, "mix_norm", m)
                if m < 2:
                    split_n(m)
                square(0, m, 0)
            split_n(2)
            root(0, D)
            take_rstd(0, rstd)
            nc.scalar.activation(par[:, 2 * KD:NP0], PS[:, M1, P + 2 * KD:P + NP0], ACT.Copy).then_inc(p0_ready, 1)
            split_n(3)
            act.wait_ge(setup_T, 2)
            nc.scalar.activation(par[:, NP0:NPAR], PS[:, S0, 0:NPAR - NP0], ACT.Copy).then_inc(setup_ready, 1)
            for c in range(KH):
                last = nc.scalar.activation(
                    smp(xa[:, c, PB + PR:XL], PB + DS)[:, :, 0:PB],
                    smp(PS[:, S1, c * NS * PB:(c + 1) * NS * PB], PB), ACT.Copy)
            last.then_inc(setup_ready, 1)
            for b in range(2):
                act.wait_ge(setup_T, 3 + b)
                for c in range(KH):
                    last = nc.scalar.activation(
                        smp(glu[:, c, CB + PR:GL], CB + DS)[:, 4 * b:4 * b + 4, 0:CB],
                        smp(PS[:, M0 + b, c * 4 * CB:(c + 1) * 4 * CB], CB), ACT.Copy)
                last.then_inc(setup_ready, 1)

            def diagonals(c):
                if c:
                    act.wait_ge(conv_mm, c)
                else:
                    act.wait_ge(setup_ready, 1)
                for n in range(PE_TAPS):
                    nc.scalar.activation(tap_w[:, n, :], ident[:, :], ACT.Copy,
                                         scale=pcol("conv_w", (TAPS - PE_TAPS + n) * KH + c)).then_inc(tap_w_ready, 1)

            def sigmoid(p):
                act.wait_ge(acc_free, PAIR_UNIT[p] + 2)
                gate_t = ag[:, 2 * (p % 2) + 1, :]
                nc.scalar.activation(gate_t, gate_t, ACT.Sigmoid).then_inc(sig_ready, 1)

            def products(c):
                act.wait_ge(glu_ready, 2 * c + 2)
                act.wait_ge(setup_ready, 4)
                for k in range(G_TAPS):
                    n = c * (G_TAPS - 1) + k - 1
                    dst = g_conv[c] if k == 0 else g_prod[n % 2]
                    if k and n >= 2:
                        act.wait_ge(pool_tap, n - 1)
                    for o, win in ((dst[:, 0:PR], glu[:, c, k:k + PR]),
                                   (smp(dst[:, PR:T]), smp(glu[:, c, CB + PR:GL], CB + DS)[:, :, k:k + DS])):
                        last = nc.scalar.activation(o, win, ACT.Identity, bias=pcol("conv_b", c) if k == 0 else 0.0,
                                                    scale=pcol("conv_w", k * KH + c))
                    last.then_inc(tap_product, 1)

            def window_x(n):
                g = POOL_ORDER[n]
                act.wait_ge(acc_free, U_IN0 + POOL_UNIT[n] + 1)
                new = smp(xa[:, g, PB + PR:XL], PB + DS)[:, :, PB:]
                nc.scalar.activation(d_t[n][:, 0:PR], xa[:, g, PB:PB + PR], ACT.Copy, scale=-float(WINDOWS[g]))
                nc.scalar.activation(smp(d_t[n][:, PR:T]), new, ACT.Copy, scale=-float(WINDOWS[g])).then_inc(wx_ready, 1)
                nc.scalar.activation(smp(new_x[:, g, :]), new, ACT.Copy).then_inc(new_packed, 1)

            def pool_hi(n):
                g = POOL_ORDER[n]
                act.wait_ge(pool_mm, n + 1)
                if n == 0:
                    act.wait_ge(pool_scale_ready, 1)
                nc.scalar.activation(halves(d_t[n]), PS[:, M0:M1 + 1, 0:HALF], ACT.Identity, bias=0.0,
                                     scale=pcol("pool_scale", g)).then_inc(ya_read, 1)
                act.wait_ge(ya_read, n + 1)
                nc.scalar.activation(hh[:, g, :], d_t[n], ACT.Copy).then_inc(ya_hi, 1)

            diagonals(0)
            act.wait_ge(p0_ready, 2)
            for g in range(KH):
                last = nc.scalar.activation(pcol("pool_scale", g), pcol("pool_scale", g), ACT.Copy, scale=1.0 / WINDOWS[g])
            last.then_inc(pool_scale_ready, 1)
            for u in range(1, N_IN0):
                split_n(u + 3)
                if u == 1:
                    sigmoid(0)
                if u == 3:
                    window_x(0)
                    products(0)
                if u == 4:
                    diagonals(1)
                    sigmoid(1)
                if u == 5:
                    products(1)
                if u == 6:
                    window_x(1)
                if u == 7:
                    pool_hi(0)
                    diagonals(2)
                    sigmoid(2)
                if u == 8:
                    products(2)
                if u == 9:
                    window_x(2)
                    pool_hi(1)
                if u == 10:
                    sigmoid(3)
            products(3)
            diagonals(3)
            window_x(3)
            table_for(1, ACT.Sqrt)
            pool_hi(2)
            split_n(U_OUT0 + 3)
            pool_hi(3)
            for c in range(KH):
                last = nc.scalar.activation(smp(new_glu[:, c, :]), smp(glu[:, c, CB + PR:GL], CB + DS)[:, :, CB:],
                                            ACT.Copy)
            last.then_inc(new_packed, 1)

            def state_rows_out(first, bank, n, dst_rows, dst):
                nc.scalar.activation(dst_rows[0:n, :], PS[0:n, bank, :], ACT.Copy).then_inc(so_rows, 1)
                act.wait_ge(so_rows, first)
                act.dma_start(dst, dst_rows[0:n, :]).then_inc(st_out, 16)

            def conv_square(c):
                act.wait_ge(cent_ready, c + 1)
                if c == 0:
                    act.wait_ge(ya_ready, KH)
                nc.scalar.activation(d_t[c], conv_o[:, c, :], ACT.Square).then_inc(csq_ready, 1)

            def conv_silu(c):
                act.wait_ge(cn_ready, c + 1)
                nc.scalar.activation(conv_o[:, c, :], conv_o[:, c, :], ACT.Silu, bias=pcol("conv_norm_b", c),
                                     scale=pcol("conv_norm_g", c)).then_inc(cs_ready, 1)
                act.wait_ge(cs_ready, c + 1)
                nc.scalar.activation(hh[:, KH + c, :], conv_o[:, c, :], ACT.Copy).then_inc(hh_ready, 1)

            for m in range(1, KD):
                split_n(U_OUT0 + m + 3)
                if m == 2:
                    for c in range(KH):
                        conv_square(c)
                if m == 4:
                    root(1, DH)
                    table_for(2, ACT.Silu)
                    take_rstd(1, rstd)
                    conv_silu(0)
                    conv_silu(1)
                if m == 5:
                    conv_silu(2)
                    conv_silu(3)
                    table_for(3, ACT.Sqrt)
                if m == 6:
                    act.wait_ge(so_T, 1)
                    state_rows_out(1, M0, PB, out_rows0[2], pool_prompt[0, 0])
                    state_rows_out(2, M1, SM, out_rows0[3], pool_sample[0, :, PB - DS:PB, :])
            for m in range(KD):
                split_n(U_OUT0 + KD + m + 3)
                if m == 0:
                    act.wait_ge(so_T, 2)
                    state_rows_out(3, M0, CB, out_rows0[0], conv_prompt[0, 0])
                    state_rows_out(4, M1, SM, out_rows0[1], conv_sample[0, :, CB - DS:CB, :])
                if m == 6:
                    act.wait_ge(fs_T, 1)
                    st = state_T[:, :, :, :].rearrange("p l a b -> p (l a b)")
                    for b, (bank, n) in enumerate(((M0, 4 * P), (M1, 4 * P), (S1, 3 * P))):
                        nc.scalar.activation(st[:, b * 4 * P:b * 4 * P + n], PS[:, bank, 0:n], ACT.Copy)\
                            .then_inc(fs_ready, 1)
                norm_in(1, m, 2, "ffn_norm", m)

            def ffn(layer):
                n = 2 * layer + 1
                r = (2, 5)[layer]
                for g, ((t0, nt), ub) in enumerate(zip(GROUPS, U_GROUP)):
                    u0 = U_FFN[layer] + ub
                    c0 = layer * KF + t0

                    def product_hi(i):
                        act.wait_ge(h_ready, i + (c0 + 1))
                        dst = hh[:, i, :] if isinstance(i, int) else \
                            hh[:, bass.ds(i, 1), :].rearrange("p a t -> p (a t)")
                        nc.scalar.activation(dst[:, 0:PR], cv[:, 2, 0:PR], ACT.Copy)
                        nc.scalar.activation(smp(dst[:, PR:T]), smp(cv[:, 2, PR:PR + NS * (FB + DS)], FB + DS)[:, :, FB:],
                                             ACT.Copy).then_inc(hh_ready, 1)

                    def step(i, ahead, before=None, start=False):
                        for j in range(2):
                            ahead(j)
                            if start and j == 0:
                                root(r, D)
                                take_rstd(r, rstd)
                            if j == 0 and before is not None:
                                product_hi(before)
                            act.wait_ge(acc_free, i * 2 + (u0 + j + 1))
                            act.wait_ge(pad_ready, (i + c0) * 2 + (j + 1))
                            ti = i + (t0 + j * KF)
                            nc.scalar.activation(cv[:, j, :], up[:, j, 0:CL], ACT.Identity,
                                                 bias=pcol("ffn_conv_b", ti + layer * 2 * KF),
                                                 scale=pcol("ffn_conv_w", ti + layer * FK * 2 * KF)).then_inc(tap0_ready, 1)
                            if j == 0:
                                act.wait_ge(tap_ready, (i + c0) * 2 + 1)
                                nc.scalar.activation(cv[:, 0, :], cv[:, 0, :], ACT.Silu).then_inc(silu_ready, 1)

                    for e in range(2):
                        step(e, lambda j: split_n(u0 + 2 * e + j + 3), e - 1 if e else None, start=(g == 0 and e == 0))
                    more = nt // 2 - 1 if nt == KD else nt // 2 - 2
                    with act.Fori(0, more) as b:
                        for e in range(2):
                            step(b * 2 + (2 + e), lambda j: split((2 * e + j + 3) % 4, b * 4 + (u0 + 4 + 2 * e + j + 3),
                                                                  b * 2 + (u0 + 4 + 2 * e + j + 3) // 2, KD),
                                 b * 2 + (1 + e))
                    for i in range(2 * more + 2, nt):
                        step(i, lambda j: split_n(u0 + 2 * i + j + 3), i - 1)
                    product_hi(nt - 1)
                    if g == len(GROUPS) - 1:
                        table_for(4 + layer, ACT.Sqrt)
                    ud = u0 + 2 * nt
                    for m in range(KD):
                        split_n(ud + m + 3)
                        if g < len(GROUPS) - 1:
                            continue
                        if m == 0:
                            stash_rows_out(layer)
                        if layer == 0:
                            if m == 4:
                                act.wait_ge(st_ffn, 48)
                                act.wait_ge(h_lo_ready, H_FFN[0] + KF)
                                act.dma_start(gate_w_rows, sgu_w[0].rearrange("h i j -> i h j")).then_inc(ld_gw, 16)
                                act.dma_start(gate_b.rearrange("p h i -> p (h i)"),
                                              sgu_bias.rearrange("l h i -> l (h i)").to_broadcast([P, KD * P]))\
                                    .then_inc(ld_gb, 16)
                            norm_in(2, m, r + 1, "mix_norm", KD + m)
                        else:
                            if m >= 2:
                                take_y(m - 2)
                            act.wait_ge(acc_free, X_FINAL[4] + m + 1)
                            square(4, m, r + 1)
                            nc.scalar.activation(xg[:, m % 2, :], X[:, m, :], ACT.Identity, bias=0.0,
                                                 scale=pcol("final_norm", m)).then_inc(xg_ready, 1)
                if layer == 1:
                    take_y(KD - 2)

            def stash_rows_out(layer):
                act.wait_ge(stash_T, layer + 1)
                sr = stash_rows.rearrange("p a b -> p (a b)")
                np_, ns_ = FB * 2 * KF, NS * FB * 2 * KF
                last_n = ns_ % P
                nc.scalar.activation(sr[0:np_, 0:P], PS[0:np_, M0, 0:P], ACT.Copy)
                nc.scalar.activation(sr[:, P:4 * P], PS[:, M0, P:4 * P], ACT.Copy).then_inc(stash_rows_ready, 1)
                nc.scalar.activation(sr[:, 4 * P:6 * P], PS[:, M1, 0:2 * P], ACT.Copy)
                nc.scalar.activation(sr[0:last_n, 6 * P:7 * P], PS[0:last_n, M1, 2 * P:3 * P], ACT.Copy)\
                    .then_inc(stash_rows_ready, 1)
                act.wait_ge(stash_rows_ready, 2 * layer + 2)
                fp = ffn_prompt[layer].rearrange("b r (t p) -> (b r t) p", p=P)
                fs = ffn_sample[layer].rearrange("s r (t p) -> (s r t) p", p=P)
                act.dma_start(fp, stash_rows[0:np_, 0, :]).then_inc(st_ffn, 16)
                nf = ns_ // P
                act.dma_start(fs[0:nf * P, :].rearrange("(b q) p -> q b p", q=P),
                              stash_rows[:, 1:1 + nf, :]).then_inc(st_ffn, 16)
                act.dma_start(fs[nf * P:ns_, :], stash_rows[0:last_n, 1 + nf, :]).then_inc(st_ffn, 16)

            def take_y(m):
                act.wait_ge(y_T, m + 1)
                nc.scalar.activation(y_rows[:, 0:CH, m * P:(m + 1) * P],
                                     PS[:, M0, :].rearrange("p (r c) -> p r c", r=CH), ACT.Copy).then_inc(yrow_ready, 1)
                nc.scalar.activation(y_rows[P - SM:P, CH, m * P:(m + 1) * P], PS[P - SM:P, M1, 0:P], ACT.Copy)\
                    .then_inc(yrow_ready, 1)

            ffn(0)

            def v_square(m):
                act.wait_ge(cent_ready, KH + m + 1)
                if m == 0:
                    act.wait_ge(bc_mm, 4)
                    act.wait_ge(var_mm, 4)
                elif m >= 3:
                    act.wait_ge(vsq_added, m - 2)
                dst = sqacc[:, :] if m == 0 else sq[:, m % 2, :]
                nc.scalar.activation(dst, V[:, m, :], ACT.Square).then_inc(vsq_ready, 1)

            split_n(U_IN1 + 3)
            root(3, D)
            take_rstd(3, rstd)
            split_n(U_IN1 + 4)
            act.wait_ge(gw_T, 1)
            act.wait_ge(ld_gb, 16)
            nc.scalar.activation(gate_w_T[:, 0:4, :], PS[:, M0, :].rearrange("p (h i) -> p h i", h=4), ACT.Copy)
            nc.scalar.activation(gate_w_T[:, 4:8, :], PS[:, M1, :].rearrange("p (h i) -> p h i", h=4), ACT.Copy)\
                .then_inc(gw_copied, 1)
            for m in range(2, KD):
                split_n(U_IN1 + m + 3)
                if m == 5:
                    act.wait_ge(gw_ready, 1)
                    act.wait_ge(bw_zero, 1)
                    for s in range(NS):
                        act.dma_start(block_w[s * DS:(s + 1) * DS, :, s * DS:(s + 1) * DS],
                                      gate_w_T[0:DS, :, 0:DS]).then_inc(bw_ready, 16)

            def v_affine(m):
                act.wait_ge(vn_ready, m + 1)
                nc.scalar.activation(V[:, m, :], V[:, m, :], ACT.Identity, bias=pcol("sgu_norm_b", m),
                                     scale=pcol("sgu_norm_g", m)).then_inc(va_ready, 1)

            def v_take(m):
                act.wait_ge(v_T, m + 1)
                if m >= 2:
                    act.wait_ge(st_v[m % 2], 32 * (m // 2))
                    act.wait_ge(z_mm, m - 1)
                nc.scalar.activation(v_rows[m % 2][:, 0:CH, :], PS[:, M0, :].rearrange("p (r c) -> p r c", r=CH), ACT.Copy)\
                    .then_inc(vrow_ready, 1)
                nc.scalar.activation(v_rows[m % 2][0:SM, CH, :], PS[0:SM, M1, 0:P], ACT.Copy).then_inc(vrow_ready, 1)
                act.wait_ge(vrow_ready, 2 * m + 2)
                act.dma_start(sgu_v_prompt[0, 0, :, m * P:(m + 1) * P], v_rows[m % 2][:, CH - 1, :]).then_inc(st_v[m % 2], 16)
                act.dma_start(sgu_v_sample[0, :, :, m * P:(m + 1) * P].rearrange("s t p -> (s t) p"),
                              v_rows[m % 2][0:SM, CH, :]).then_inc(st_v[m % 2], 16)

            def uz_hi(m):
                act.wait_ge(uz_ready, m + 1)
                nc.scalar.activation(hh[:, m, :], U[:, m, :], ACT.Copy).then_inc(hh_ready, 1)

            uu = U_IN1 + KD
            split_n(uu + 3)
            for m in range(4):
                v_square(m)
            split_n(uu + 4)
            for m in range(4, KD):
                v_square(m)
            split_n(uu + 5)
            root(4, D)
            take_rstd(4, rstd_v)
            split_n(uu + 6)
            for m in range(3):
                v_affine(m)
            v_take(0)
            for m in range(3, KD):
                v_affine(m)
            for m in range(1, KD):
                if m % 2:
                    split_n(uu + 7 + m // 2)
                if m >= 2:
                    uz_hi(m - 2)
                v_take(m)
            uz_hi(KD - 2)
            uz_hi(KD - 1)
            for m in range(KD):
                split_n(U_OUT1 + m + 3)
                norm_in(3, m, 5, "ffn_norm", KD + m)

            ffn(1)
            root(6, D)
            take_y(KD - 1)
            act.wait_ge(rinv_ready, 7)
            act.wait_ge(yrow_ready, 2 * KD)
            for r in (1, 3):
                nc.scalar.activation(y_rows[:, r, :], y_rows[:, r, :], ACT.Copy, scale=rinv[:, r:r + 1])\
                    .then_inc(y_scaled, 1)
                act.wait_ge(y_scaled, (r + 1) // 2)
                act.dma_start(yp_rows[:, r, :], y_rows[:, r, :]).then_inc(st_y, 16)

        @block.gpsimd
        def _(pool):
            nc.gpsimd.memset(ones[:, :], 1.0).then_inc(const_ready, 1)
            pool.wait_ge(const_ready, 1)
            nc.gpsimd.affine_select(out=ident[:, :], in_=ones[:, :], compare_op=ALU.is_equal, fill=0.0, base=0,
                                    pattern=[[-1, P]], channel_multiplier=1).then_inc(ident_ready, 1)
            nc.gpsimd.memset(eps[:, :], EPS).then_inc(const_ready, 1)
            at = 0
            for w in WINDOWS:
                for j in range(w - 1):
                    nc.gpsimd.memset(corr[:, at:at + 1], w / (j + 1)).then_inc(corr_ready, 1)
                    at += 1

            def split(slot, u, nk):
                pool.wait_ge(hi_ready, u + 1)
                nc.gpsimd.tensor_tensor(w_lo[slot][:, 0:nk * P], w_raw[slot % 2][:, 0:nk * P],
                                        w_hi[slot][:, 0:nk * P].bitcast(F32), ALU.subtract).then_inc(lo_ready, 1)

            def split_n(u):
                if u < N_UNITS:
                    split(u % 4, u, tiles_of(u))

            def add_square(m):
                pool.wait_ge(sq_ready, m + 1)
                if m > 1:
                    pool.wait_ge(sq_added, m - 1)
                nc.gpsimd.tensor_tensor(sqacc[:, :], sqacc[:, :], sq[:, m % 2, :], ALU.add).then_inc(sq_added, 1)

            split_n(0)
            split_n(1)
            for m in range(1, KD):
                add_square(m)
            split_n(2)
            nc.gpsimd.memset(xa[:, :, 0:PB], 0.0).then_inc(pads_zero, 1)
            nc.gpsimd.memset(glu[:, :, 0:CB], 0.0).then_inc(pads_zero, 1)

            steps = [0]

            def windows(n):
                g = POOL_ORDER[n]
                pool.wait_ge(acc_free, U_IN0 + POOL_UNIT[n] + 1)
                if n == 0:
                    pool.wait_ge(corr_ready, sum(WINDOWS) - len(WINDOWS))
                    pool.wait_ge(setup_ready, 4)
                    pool.wait_ge(bc_mm, 1)
                else:
                    pool.wait_ge(d_ready, n)
                src, lo, width = xa[:, g, :], 0, 1
                for level in range(g + 1):
                    dst = pool_tmp[level % 2]
                    lo += width
                    nc.gpsimd.tensor_tensor(dst[:, lo:XL], src[:, lo:XL], src[:, lo - width:XL - width], ALU.add)\
                        .then_inc(win_step, 1)
                    steps[0] += 1
                    pool.wait_ge(win_step, steps[0])
                    src, width = dst, 2 * width
                w = WINDOWS[g]
                c0 = sum(WINDOWS[:g]) - g
                nc.gpsimd.tensor_tensor(src[:, PB:PB + w - 1], src[:, PB:PB + w - 1], corr[:, c0:c0 + w - 1], ALU.mult)\
                    .then_inc(win_step, 1)
                steps[0] += 1
                pool.wait_ge(win_step, steps[0])
                pool.wait_ge(wx_ready, n + 1)
                nc.gpsimd.tensor_tensor(d_t[n][:, 0:PR], src[:, PB:PB + PR], d_t[n][:, 0:PR], ALU.add)
                nc.gpsimd.tensor_tensor(smp(d_t[n][:, PR:T]), smp(src[:, PB + PR:XL], PB + DS)[:, :, PB:],
                                        smp(d_t[n][:, PR:T]), ALU.add).then_inc(d_ready, 1)

            def pool_lo(n):
                g = POOL_ORDER[n]
                pool.wait_ge(ya_hi, n + 1)
                nc.gpsimd.tensor_tensor(hl[:, g, :], d_t[n], hh[:, g, :].bitcast(F32), ALU.subtract)\
                    .then_inc(ya_ready, 1)

            def conv(c):
                for k in range(1, G_TAPS):
                    n = c * (G_TAPS - 1) + k - 1
                    pool.wait_ge(tap_product, G_TAPS * c + k + 1)
                    if n:
                        pool.wait_ge(pool_tap, n)
                    nc.gpsimd.tensor_tensor(g_conv[c], g_conv[c], g_prod[n % 2], ALU.add)\
                        .then_inc(pool_tap, 1)

            for u in range(N_IN0):
                split_n(u + 3)
                if u == 3:
                    conv(0)
                    windows(0)
                if u == 5:
                    conv(1)
                if u == 6:
                    windows(1)
                if u == 8:
                    conv(2)
                if u == 9:
                    windows(2)
            conv(3)
            windows(3)
            for n in range(3):
                pool_lo(n)
            split_n(U_OUT0 + 3)
            pool_lo(3)
            for m in range(1, 2 * KD):
                split_n(U_OUT0 + m + 3)
            pool.wait_ge(st_out, 16 * 4)
            pool.wait_ge(xl_ready, 2 * KD)
            nc.gpsimd.memset(up[:, :, 0:FB], 0.0).then_inc(pads_zero, 1)

            def ffn(layer):
                for g, ((t0, nt), ub) in enumerate(zip(GROUPS, U_GROUP)):
                    u0 = U_FFN[layer] + ub
                    c0 = layer * KF + t0
                    so = state_T[:, layer, :, :]

                    def pads(j, i):
                        ti = i + (t0 + j * KF)
                        src = so[:, :, ti:ti + 1] if isinstance(ti, int) else so[:, :, bass.ds(ti, 1)]
                        nc.gpsimd.tensor_copy(smp(up[:, j, FB + PR:UL], FB + DS)[:, :, 0:FB],
                                              src.rearrange("p (s r) o -> p s (r o)", r=FB)).then_inc(pad_ready, 1)

                    def step(i, ahead, start=False):
                        for j in range(2):
                            if start and layer == 0 and j == 0:
                                pool.wait_ge(fs_ready, 3)
                            if not (layer == 0 and start):
                                pool.wait_ge(tap_ready, (i + c0) * 2 + (j - 1))
                            pads(j, i)
                            ahead(j)
                            pool.wait_ge(acc_free, i * 2 + (u0 + j + 1))
                            ti = i + (t0 + j * KF)
                            dst = stash[:, :, ti:ti + 1] if isinstance(ti, int) else stash[:, :, bass.ds(ti, 1)]
                            nc.gpsimd.tensor_copy(dst[:, 0:FB, :].rearrange("p r o -> p (r o)"), up[:, j, PR:PR + FB])\
                                .then_inc(stash_ready, 1)
                            nc.gpsimd.tensor_copy(
                                dst[:, FB:, :].rearrange("p (s r) o -> p s (r o)", r=FB),
                                smp(up[:, j, FB + PR:UL], FB + DS)[:, :, DS:DS + FB]).then_inc(stash_ready, 1)

                    first = 0
                    if g == 0:
                        for e in range(2):
                            step(e, lambda j: split_n(u0 + 2 * e + j + 3), start=(e == 0))
                        first = 1
                    end = nt // 2 if nt == KD else nt // 2 - 1
                    with pool.Fori(first, end) as b:
                        for e in range(2):
                            step(b * 2 + e, lambda j: split((2 * e + j + 3) % 4, b * 4 + (u0 + 2 * e + j + 3), KD))
                    for i in range(2 * end, nt):
                        step(i, lambda j: split_n(u0 + 2 * i + j + 3))
                    ud = u0 + 2 * nt
                    for m in range(KD):
                        split_n(ud + m + 3)

            ffn(0)
            nc.gpsimd.memset(block_w, 0.0).then_inc(bw_zero, 1)
            for m in range(KD):
                split_n(U_IN1 + m + 3)
                if m == 2:
                    pool.wait_ge(gw_copied, 1)
                    nc.gpsimd.affine_select(out=gate_w_T, in_=gate_w_T, compare_op=ALU.is_ge, fill=0.0, base=0,
                                            pattern=[[0, KD], [1, P]], channel_multiplier=-1).then_inc(gw_ready, 1)
                if m == 1:
                    pool.wait_ge(acc_free, U_IN1 + 2)
                    pool.wait_ge(bc_mm, 4)
                    nc.gpsimd.tensor_tensor(sq[:, 0, :], V[:, 0, :], V[:, 1, :], ALU.add).then_inc(vsum, 1)
                elif m > 1:
                    pool.wait_ge(acc_free, U_IN1 + m + 1)
                    pool.wait_ge(vsum, m - 1)
                    nc.gpsimd.tensor_tensor(sq[:, 0, :], sq[:, 0, :], V[:, m, :], ALU.add).then_inc(vsum, 1)

            uu = U_IN1 + KD
            for m in range(2 * KD):
                split_n(uu + m + 3)
            pool.wait_ge(xl_ready, 4 * KD)
            pool.wait_ge(st_v[0], 16 * KD)
            pool.wait_ge(st_v[1], 16 * KD)
            nc.gpsimd.memset(up[:, :, 0:FB], 0.0).then_inc(pads_zero, 1)
            ffn(1)

        @block.vector
        def _(dve):
            def x_lo(n, m, gname, gi):
                dve.wait_ge(xh_ready, KD * n + m + 1)
                nc.vector.scalar_tensor_tensor(out=xl[:, m, :], in0=X[:, m, :], scalar=pcol(gname, gi),
                                               in1=xh[:, m, :].bitcast(F32), op0=ALU.mult, op1=ALU.subtract)\
                    .then_inc(xl_ready, 1)

            def add_square(n, m):
                dve.wait_ge(sq_ready, KD * n + m + 1)
                if m > 1:
                    dve.wait_ge(sq_added, (KD - 1) * n + m - 1)
                nc.vector.tensor_tensor(sqacc[:, :], sqacc[:, :], sq[:, m % 2, :], ALU.add).then_inc(sq_added, 1)

            def residual(u, m):
                dve.wait_ge(unit_done, u + 1)
                nc.vector.tensor_tensor(halves(X[:, m, :]), acc(u % 2), halves(X[:, m, :]), ALU.add)\
                    .then_inc(acc_free, 1)

            def factors(r):
                dve.wait_ge(std_ready, r + 1)
                nc.vector.reciprocal(rinv[:, :], std[:, :]).then_inc(rinv_ready, 1)
                dve.wait_ge(rinv_ready, r + 1)
                if r < 6:
                    for t in range(RT):
                        last = nc.vector.tensor_scalar(diag[:, t, :], ident[:, :], rinv[:, t:t + 1], None, ALU.mult)
                    last.then_inc(diag_ready, 1)

            def scaled(u, dst):
                dve.wait_ge(unit_done, u + 1)
                nc.vector.tensor_tensor(halves(dst), acc(u % 2), halves(rstd[:, :]), ALU.mult).then_inc(acc_free, 1)

            def scaled_padded(slot, u, dst, pad):
                dve.wait_ge(unit_done, u + 1)
                nc.vector.tensor_tensor(dst[:, pad:pad + HALF], PS[:, 2 * slot, 0:HALF], rstd[:, 0:HALF], ALU.mult)
                nc.vector.tensor_tensor(dst[:, pad + HALF:pad + PR], PS[:, 2 * slot + 1, 0:PR - HALF],
                                        rstd[:, HALF:PR], ALU.mult)
                n = NS * (pad + DS)
                nc.vector.tensor_tensor(smp(dst[:, pad + PR:pad + PR + n], pad + DS)[:, :, pad:],
                                        smp(PS[:, 2 * slot + 1, PR - HALF:HALF]), smp(rstd[:, PR:T]), ALU.mult)\
                    .then_inc(acc_free, 1)

            for k in range(KD):
                dve.wait_ge(xT, k + 1)
                nc.vector.tensor_copy(X[:, k, 0:PR], PS[:, S0 + 2 * (k % 2), :]).then_inc(x_ready, 1)
                if k >= 1:
                    x_lo(0, k - 1, "mix_norm", k - 1)
            x_lo(0, KD - 1, "mix_norm", KD - 1)
            factors(0)
            dve.wait_ge(rstd_ready, 1)

            def evacuate(u):
                if u in POOL_UNIT:
                    scaled_padded(u % 2, U_IN0 + u, xa[:, IN0[u], :], PB)
                    return
                gate = u not in PAIR_UNIT
                p = PAIR_UNIT.index(u - gate)
                if p >= 2:
                    dve.wait_ge(glu_ready, 2 * p - 2)
                scaled(U_IN0 + u, ag[:, 2 * (p % 2) + gate, :])

            def make_glu(c):
                if c == 0:
                    dve.wait_ge(pads_zero, 2)
                    dve.wait_ge(setup_ready, 4)
                a_t, g_t = ag[:, 2 * (c % 2), :], ag[:, 2 * (c % 2) + 1, :]
                dve.wait_ge(sig_ready, c + 1)
                nc.vector.tensor_tensor(glu[:, c, CB:CB + PR], a_t[:, 0:PR], g_t[:, 0:PR], ALU.mult)\
                    .then_inc(glu_ready, 1)
                nc.vector.tensor_tensor(smp(glu[:, c, CB + PR:GL], CB + DS)[:, :, CB:], smp(a_t[:, PR:T]),
                                        smp(g_t[:, PR:T]), ALU.mult).then_inc(glu_ready, 1)

            steps_made = [0]

            def conv(c, first, end):
                dve.wait_ge(glu_ready, 2 * c + 2)
                if c and first == 0:
                    dve.wait_ge(conv_whole, min(c, 2))
                for k in range(G_TAPS + first, G_TAPS + end):
                    w = pcol("conv_w", k * KH + c)
                    sides = ((conv_o[:, c, 0:PR], glu[:, c, k:k + PR]),
                             (smp(conv_o[:, c, PR:T]), smp(glu[:, c, CB + PR:GL], CB + DS)[:, :, k:k + DS]))
                    for o, win in sides:
                        if k == G_TAPS:
                            ins = nc.vector.tensor_scalar(o, win, w, None, ALU.mult)
                        else:
                            dve.wait_ge(conv_step, steps_made[0] - 1)
                            ins = nc.vector.scalar_tensor_tensor(out=o, in0=win, scalar=w, in1=o,
                                                                 op0=ALU.mult, op1=ALU.add)
                        ins.then_inc(conv_step, 1)
                        steps_made[0] += 1

            def combine(c):
                dve.wait_ge(conv_mm, c + 1)
                dve.wait_ge(conv_step, 2 * V_TAPS * (c + 1))
                nc.vector.tensor_tensor(conv_o[:, c, 0:PR], PS[:, S0, 0:PR], conv_o[:, c, 0:PR], ALU.add)\
                    .then_inc(pe_added, 1)
                nc.vector.tensor_tensor(conv_o[:, c, PR:T], PS[:, S1, 0:SM], conv_o[:, c, PR:T], ALU.add)\
                    .then_inc(pe_added, 1)
                dve.wait_ge(pool_tap, (G_TAPS - 1) * (c + 1))
                dve.wait_ge(pe_added, 2 * c + 2)
                nc.vector.tensor_tensor(conv_o[:, c, :], conv_o[:, c, :], g_conv[c], ALU.add)\
                    .then_inc(conv_whole, 1)

            V3 = V_TAPS // 3
            evacuate(0)
            evacuate(1)
            make_glu(0)
            conv(0, 0, V3)
            evacuate(2)
            conv(0, V3, 2 * V3)
            evacuate(3)
            conv(0, 2 * V3, V_TAPS)
            evacuate(4)
            combine(0)
            make_glu(1)
            conv(1, 0, V3)
            evacuate(5)
            conv(1, V3, 2 * V3)
            evacuate(6)
            conv(1, 2 * V3, V_TAPS)
            evacuate(7)
            combine(1)
            make_glu(2)
            conv(2, 0, V3)
            evacuate(8)
            conv(2, V3, 2 * V3)
            evacuate(9)
            conv(2, 2 * V3, V_TAPS)
            evacuate(10)
            make_glu(3)
            conv(3, 0, V3)
            combine(2)
            evacuate(11)
            conv(3, V3, V_TAPS)
            residual(U_OUT0, 0)
            combine(3)

            residual(U_OUT0 + 1, 1)
            dve.wait_ge(mean_mm, 1)
            for c in range(KH):
                nc.vector.scalar_tensor_tensor(out=halves(conv_o[:, c, :]), in0=PS[:, M0:M1 + 1, 0:HALF],
                                               scalar=-1.0 / DH, in1=halves(conv_o[:, c, :]), op0=ALU.mult,
                                               op1=ALU.add).then_inc(cent_ready, 1)
            residual(U_OUT0 + 2, 2)
            for c in (0, 2):
                dve.wait_ge(csq_ready, c + 2)
                nc.vector.tensor_tensor(d_t[c], d_t[c], d_t[c + 1], ALU.add).then_inc(csq_added, 1)
            dve.wait_ge(csq_added, 2)
            nc.vector.tensor_tensor(d_t[0], d_t[0], d_t[2], ALU.add).then_inc(csq_added, 1)
            residual(U_OUT0 + 3, 3)
            factors(1)
            dve.wait_ge(rstd_ready, 2)

            def conv_norm(c):
                nc.vector.tensor_tensor(conv_o[:, c, :], conv_o[:, c, :], rstd[:, :], ALU.mult).then_inc(cn_ready, 1)

            def conv_lo(c):
                dve.wait_ge(hh_ready, c + 1)
                nc.vector.tensor_tensor(hl[:, KH + c, :], conv_o[:, c, :], hh[:, KH + c, :].bitcast(F32), ALU.subtract)\
                    .then_inc(h_lo_ready, 1)

            conv_norm(0)
            conv_norm(1)
            residual(U_OUT0 + 4, 4)
            conv_norm(2)
            conv_norm(3)
            conv_lo(0)
            residual(U_OUT0 + 5, 5)
            conv_lo(1)
            residual(U_OUT0 + 6, 6)
            conv_lo(2)
            conv_lo(3)
            residual(U_OUT0 + 7, 7)
            for m in range(KD):
                dve.wait_ge(acc_free, U_OUT0 + m + 1)
                residual(U_OUT0 + KD + m, m)
                x_lo(1, m, "ffn_norm", m)
                if m:
                    add_square(1, m)

            def ffn(layer):
                n = 2 * layer + 1
                r = (2, 5)[layer]
                for g, ((t0, nt), ub) in enumerate(zip(GROUPS, U_GROUP)):
                    u0 = U_FFN[layer] + ub
                    c0 = layer * KF + t0

                    def product_lo(i):
                        dve.wait_ge(hh_ready, i + (H_FFN[layer] + t0 + 1))
                        if isinstance(i, int):
                            hi_, lo_ = hh[:, i, :], hl[:, i, :]
                        else:
                            hi_ = hh[:, bass.ds(i, 1), :].rearrange("p a t -> p (a t)")
                            lo_ = hl[:, bass.ds(i, 1), :].rearrange("p a t -> p (a t)")
                        nc.vector.tensor_tensor(lo_[:, 0:PR], cv[:, 2, 0:PR], hi_[:, 0:PR].bitcast(F32), ALU.subtract)
                        nc.vector.tensor_tensor(smp(lo_[:, PR:T]), smp(cv[:, 2, PR:PR + NS * (FB + DS)], FB + DS)[:, :, FB:],
                                                smp(hi_[:, PR:T].bitcast(F32)), ALU.subtract).then_inc(h_lo_ready, 1)

                    def step(i, before=None):
                        for j in range(2):
                            u = i * 2 + (u0 + j)
                            if layer or g or not isinstance(i, int) or i > 0:
                                dve.wait_ge(stash_ready, (i + c0) * 4 + (2 * j - 2))
                            scaled_padded(j, u, up[:, j, :], FB)
                            if j == 0 and before is not None:
                                product_lo(before)
                            dve.wait_ge(tap0_ready, (i + c0) * 2 + (j + 1))
                            ti = i + (t0 + j * KF)
                            for k in range(1, FK):
                                if k > 1:
                                    dve.wait_ge(tap1_ready, (i + c0) * 2 + (j + 1))
                                nc.vector.scalar_tensor_tensor(
                                    out=cv[:, j, :], in0=up[:, j, k:k + CL],
                                    scalar=pcol("ffn_conv_w", ti + (layer * FK + k) * 2 * KF), in1=cv[:, j, :],
                                    op0=ALU.mult, op1=ALU.add).then_inc(tap1_ready if k == 1 else tap_ready, 1)
                        dve.wait_ge(silu_ready, i + c0 + 1)
                        dve.wait_ge(tap_ready, (i + c0) * 2 + 2)
                        nc.vector.tensor_tensor(cv[:, 2, :], cv[:, 0, :], cv[:, 1, :], ALU.mult).then_inc(h_ready, 1)

                    if g == 0:
                        factors(r)
                        dve.wait_ge(rstd_ready, r + 1)
                    step(0)
                    with dve.Fori(0, nt - 1) as i:
                        step(i + 1, i)
                    product_lo(nt - 1)
                    ud = u0 + 2 * nt
                    for m in range(KD):
                        residual(ud + m, m)
                        if g == len(GROUPS) - 1:
                            if layer == 0:
                                x_lo(2, m, "mix_norm", KD + m)
                            if 0 < m < KD - layer:
                                add_square(2 * layer + 2, m)

            ffn(0)

            dve.wait_ge(st_ffn, 48)
            factors(3)
            dve.wait_ge(rstd_ready, 4)
            for m in range(KD):
                scaled(U_IN1 + m, V[:, m, :])
            uu = U_IN1 + KD

            def u_take(m):
                if m == 0:
                    dve.wait_ge(gw_T, 1)
                scaled(uu + m, U[:, m, :])

            def v_norm(m):
                nc.vector.tensor_tensor(V[:, m, :], V[:, m, :], rstd_v[:, :], ALU.mult).then_inc(vn_ready, 1)

            def z_bias(m):
                dve.wait_ge(z_mm, m + 1)
                nc.vector.tensor_tensor(V[:, m, 0:PR].rearrange("p (c i) -> p c i", c=CH),
                                        PS[:, S0, :].rearrange("p (c i) -> p c i", c=CH),
                                        gate_b[:, m:m + 1, :].to_broadcast([P, CH, P]), ALU.add).then_inc(zb_ready, 1)
                nc.vector.tensor_tensor(smp(V[:, m, PR:T]), smp(PS[:, S1, 0:SM]),
                                        gate_b[:, m:m + 1, 0:DS].to_broadcast([P, NS, DS]), ALU.add).then_inc(zb_ready, 1)

            def uz(m):
                dve.wait_ge(zb_ready, 2 * m + 2)
                dve.wait_ge(acc_free, uu + m + 1)
                nc.vector.tensor_tensor(U[:, m, :], U[:, m, :], V[:, m, :], ALU.mult).then_inc(uz_ready, 1)

            def uz_lo(m):
                dve.wait_ge(uz_ready, m + 1)
                dve.wait_ge(hh_ready, H_MIX[1] + m + 1)
                nc.vector.tensor_tensor(hl[:, m, :], U[:, m, :], hh[:, m, :].bitcast(F32), ALU.subtract)\
                    .then_inc(h_lo_ready, 1)

            def v_center(m):
                nc.vector.scalar_tensor_tensor(out=halves(V[:, m, :]), in0=PS[:, S0:S1 + 1, 0:HALF],
                                               scalar=-1.0 / D, in1=halves(V[:, m, :]), op0=ALU.mult,
                                               op1=ALU.add).then_inc(cent_ready, 1)

            def add_v_square(m):
                dve.wait_ge(vsq_ready, m + 1)
                if m > 1:
                    dve.wait_ge(vsq_added, m - 1)
                nc.vector.tensor_tensor(sqacc[:, :], sqacc[:, :], sq[:, m % 2, :], ALU.add).then_inc(vsq_added, 1)

            dve.wait_ge(mean_mm, 2)
            for m in range(3):
                v_center(m)
            for m in range(3, KD):
                v_center(m)
                add_v_square(m - 2)
                if m == 4:
                    u_take(0)
            u_take(1)
            for m in range(KD - 2, KD):
                add_v_square(m)
            factors(4)
            u_take(2)
            dve.wait_ge(rstd_ready, 5)
            for m in range(KD):
                v_norm(m)
            u_take(3)
            dve.wait_ge(ld_gb, 16)
            for m in range(KD):
                if m in (2, 4, 6):
                    u_take(3 + m // 2)
                z_bias(m)
                if m:
                    uz_lo(m - 1)
                if m == KD - 1:
                    u_take(KD - 1)
                uz(m)
            uz_lo(KD - 1)
            for m in range(KD):
                residual(U_OUT1 + m, m)
                x_lo(3, m, "ffn_norm", KD + m)
                if m:
                    add_square(3, m)

            ffn(1)
            factors(6)
            dve.wait_ge(yrow_ready, 2 * KD)
            for n, r in enumerate((0, 2, CH)):
                if r < CH:
                    rows = y_rows[:, r, :]
                    nc.vector.tensor_scalar(rows, rows, rinv[:, r:r + 1], None, ALU.mult).then_inc(y_row_done, 1)
                else:
                    rows = y_rows[P - SM:P, CH, :]
                    nc.vector.tensor_scalar(rows, rows, rinv[P - SM:P, CH:CH + 1], None, ALU.mult).then_inc(y_row_done, 1)


_INS = ["x_prompt", "x_sample", "state_pool", "state_conv", "state_ffn", "mix_norm", "w_in_ab", "pool_w",
        "pool_scale", "conv_w", "conv_b", "conv_norm_g", "conv_norm_b", "w_out_ab", "w_in_c", "sgu_norm_g",
        "sgu_norm_b", "sgu_w", "sgu_bias", "w_out_c", "ffn_norm", "w_up", "ffn_conv_w", "ffn_conv_b", "w_down",
        "final_norm"]

def kernel(**inputs):
    import numpy as np
    import concourse.bacc as bacc
    from concourse.bass_utils import run_bass_kernel_spmd

    nc = bacc.Bacc("TRN2", target_bir_lowering=False, num_devices=1)
    arrays, args = {}, {}
    for name in _INS:
        a = np.ascontiguousarray(inputs[name])
        arrays[f"in_{name}"] = a
        args[name] = nc.dram_tensor(f"in_{name}", a.shape, mybir.dt.from_np(a.dtype), kind="ExternalInput").ap()
    xp, xs = arrays["in_x_prompt"].shape, arrays["in_x_sample"].shape
    sp, sc, sf = (arrays[f"in_state_{n}"].shape for n in ("pool", "conv", "ffn"))
    outs = {
        "y_prompt": xp, "y_sample": xs,
        "pool_prompt": (sp[0], xp[0], *sp[2:]), "pool_sample": sp,
        "conv_prompt": (sc[0], xp[0], *sc[2:]), "conv_sample": sc,
        "sgu_v_prompt": (1, xp[0], P, xp[2]), "sgu_v_sample": (1, *xs),
        "ffn_prompt": (sf[0], xp[0], *sf[2:]), "ffn_sample": sf,
    }
    for name, shape in outs.items():
        args[name] = nc.dram_tensor(f"out_{name}", shape, F32, kind="ExternalOutput").ap()
    hybrid_trunk(nc, **args)
    r = run_bass_kernel_spmd(nc, [arrays], core_ids=[0])
    return tuple(r.results[0][f"out_{name}"] for name in outs)
```
